# Optimizing a Trainium2 kernel written in Bass

```python
import math
import jax, jax.numpy as jnp
from jax import lax
import numpy as np

D_MODEL = 1024
BATCH = 1
SEQ = 512
DEPTH = 2

N_EVEN = (DEPTH + 1) // 2
N_ODD = DEPTH // 2
D_FF = 2816
GRID_W = 64
Q_BLOCK = 128
ROPE_THETA = 10000.0
EPS = 1e-6

MLA_HEADS = 8
MLA_Q_RANK = 256
MLA_KV_RANK = 128
MLA_NOPE = 64
MLA_ROPE = 32
MLA_V = 64
DIFF_HEADS = 8
DIFF_HEAD = 32
AB_SIZES = (MLA_Q_RANK, MLA_KV_RANK, MLA_ROPE,
            DIFF_HEADS * 2 * DIFF_HEAD, DIFF_HEADS * 2 * DIFF_HEAD, DIFF_HEADS * 2 * DIFF_HEAD)
AB_SPLITS = [int(v) for v in np.cumsum(AB_SIZES)[:-1]]
AB_IN = int(sum(AB_SIZES))
AB_CAT = MLA_HEADS * MLA_V + DIFF_HEADS * 2 * DIFF_HEAD
C_HEADS = 16
C_KV_HEADS = 4
C_GROUPS = C_HEADS // C_KV_HEADS
C_HEAD = 64
C_SIZES = (C_HEADS * C_HEAD, C_KV_HEADS * C_HEAD, C_KV_HEADS * C_HEAD)
C_SPLITS = [int(v) for v in np.cumsum(C_SIZES)[:-1]]
C_IN = int(sum(C_SIZES))

kernel_name = "hybrid_mla_diff_axialgqa_macaron"

def rms_norm(x, g):
    xf = x.astype(jnp.float32)
    y = xf * lax.rsqrt(jnp.mean(xf * xf, axis=-1, keepdims=True) + EPS)
    return (y * g.astype(jnp.float32)).astype(x.dtype)

def swiglu(h, w_gate, w_up, w_down):
    return (jax.nn.silu(h @ w_gate) * (h @ w_up)) @ w_down

def rope_tables(pos, dim):
    inv = ROPE_THETA ** (-jnp.arange(0, dim, 2, dtype=jnp.float32) / dim)
    ang = pos.astype(jnp.float32)[:, None] * inv[None, :]
    return jnp.cos(ang), jnp.sin(ang)

def apply_rope(x, cos, sin):
    s, half = cos.shape
    shp = (s,) + (1,) * (x.ndim - 3) + (half,)
    c, sn = cos.reshape(shp), sin.reshape(shp)
    xf = x.astype(jnp.float32)
    x1, x2 = xf[..., :half], xf[..., half:]
    return jnp.concatenate([x1 * c - x2 * sn, x1 * sn + x2 * c], axis=-1).astype(x.dtype)

def axial_rope(x, row_cs, col_cs):
    half = x.shape[-1] // 2
    return jnp.concatenate([apply_rope(x[..., :half], *row_cs),
                            apply_rope(x[..., half:], *col_cs)], axis=-1)

def _blocks(x):
    b, s = x.shape[:2]
    return jnp.moveaxis(x.reshape((b, s // Q_BLOCK, Q_BLOCK) + x.shape[2:]), 1, 0)

def _unblocks(y):
    nb, b, qb = y.shape[:3]
    return jnp.moveaxis(y, 0, 1).reshape((b, nb * qb) + y.shape[3:])

def softmax_attention(q, k, v, scale):
    def one_block(qb):
        sc = jnp.einsum('bqhgd,bkhd->bhgqk', qb, k, preferred_element_type=jnp.float32) * scale
        p = jax.nn.softmax(sc, axis=-1).astype(v.dtype)
        return jnp.einsum('bhgqk,bkhd->bqhgd', p, v)
    return _unblocks(lax.map(one_block, _blocks(q)))

def differential_attention(q1, q2, k1, k2, v, lam, scale):
    def one_block(qs):
        qb1, qb2 = qs
        a1 = jax.nn.softmax(jnp.einsum('bqhd,bkhd->bhqk', qb1, k1, preferred_element_type=jnp.float32) * scale, axis=-1)
        a2 = jax.nn.softmax(jnp.einsum('bqhd,bkhd->bhqk', qb2, k2, preferred_element_type=jnp.float32) * scale, axis=-1)
        w = (a1 - lam * a2).astype(v.dtype)
        return jnp.einsum('bhqk,bkhd->bqhd', w, v)
    return _unblocks(lax.map(one_block, (_blocks(q1), _blocks(q2))))

def even_mixer(h, w_in, q_lora_norm, w_uq, kv_lora_norm, w_ukv, mla_qn, mla_kn,
               diff_qn, diff_kn, lq1, lk1, lq2, lk2, subln, w_out, mla_cs, diff_cs, lam_init):
    b, s, _ = h.shape
    c_q, c_kv, k_r, dq, dk, dv = jnp.split(h @ w_in, AB_SPLITS, axis=-1)
    q = (rms_norm(c_q, q_lora_norm) @ w_uq).reshape(b, s, MLA_HEADS, MLA_NOPE + MLA_ROPE)
    kv = (rms_norm(c_kv, kv_lora_norm) @ w_ukv).reshape(b, s, MLA_HEADS, MLA_NOPE + MLA_V)
    k_nope, v_mla = kv[..., :MLA_NOPE], kv[..., MLA_NOPE:]
    k_r = jnp.broadcast_to(k_r[:, :, None, :], (b, s, MLA_HEADS, MLA_ROPE))
    k = jnp.concatenate([k_nope, k_r], axis=-1)
    q, k = rms_norm(q, mla_qn), rms_norm(k, mla_kn)
    q = jnp.concatenate([q[..., :MLA_NOPE], apply_rope(q[..., MLA_NOPE:], *mla_cs)], axis=-1)
    k = jnp.concatenate([k[..., :MLA_NOPE], apply_rope(k[..., MLA_NOPE:], *mla_cs)], axis=-1)
    o_mla = softmax_attention(q[:, :, :, None, :], k, v_mla, (MLA_NOPE + MLA_ROPE) ** -0.5)
    o_mla = o_mla.reshape(b, s, MLA_HEADS * MLA_V)
    dq = apply_rope(rms_norm(dq.reshape(b, s, DIFF_HEADS, 2, DIFF_HEAD), diff_qn), *diff_cs)
    dk = apply_rope(rms_norm(dk.reshape(b, s, DIFF_HEADS, 2, DIFF_HEAD), diff_kn), *diff_cs)
    dv = dv.reshape(b, s, DIFF_HEADS, 2 * DIFF_HEAD)
    lam = (jnp.exp(jnp.sum(lq1.astype(jnp.float32) * lk1.astype(jnp.float32)))
           - jnp.exp(jnp.sum(lq2.astype(jnp.float32) * lk2.astype(jnp.float32))) + lam_init)
    o_diff = differential_attention(dq[:, :, :, 0], dq[:, :, :, 1], dk[:, :, :, 0], dk[:, :, :, 1],
                                    dv, lam, DIFF_HEAD ** -0.5)
    o_diff = (rms_norm(o_diff, subln) * (1.0 - lam_init)).reshape(b, s, DIFF_HEADS * 2 * DIFF_HEAD)
    return jnp.concatenate([o_mla, o_diff], axis=-1) @ w_out

def odd_mixer(h, w_in, qn, kn, w_out, row_cs, col_cs):
    b, s, _ = h.shape
    q, k, v = jnp.split(h @ w_in, C_SPLITS, axis=-1)
    q = axial_rope(rms_norm(q.reshape(b, s, C_KV_HEADS, C_GROUPS, C_HEAD), qn), row_cs, col_cs)
    k = axial_rope(rms_norm(k.reshape(b, s, C_KV_HEADS, C_HEAD), kn), row_cs, col_cs)
    v = v.reshape(b, s, C_KV_HEADS, C_HEAD)
    o = softmax_attention(q, k, v, C_HEAD ** -0.5).reshape(b, s, C_HEADS * C_HEAD)
    return o @ w_out

def setup_inputs(seed: int = 0) -> dict:
    key = jax.random.key(seed)
    ks = iter(jax.random.split(key, 64))

    def w(shape, fan_in):
        return jax.random.normal(next(ks), shape, jnp.float32) * fan_in ** -0.5

    def gain(shape):
        return 1.0 + 0.02 * jax.random.normal(next(ks), shape, jnp.float32)

    def small(shape, sc):
        return sc * jax.random.normal(next(ks), shape, jnp.float32)

    return {
        "x": jax.random.normal(next(ks), (BATCH, SEQ, D_MODEL), jnp.float32),
        "ffn1_norm": gain((DEPTH, D_MODEL)),
        "ffn1_w_gate": w((DEPTH, D_MODEL, D_FF), D_MODEL),
        "ffn1_w_up": w((DEPTH, D_MODEL, D_FF), D_MODEL),
        "ffn1_w_down": w((DEPTH, D_FF, D_MODEL), D_FF),
        "mix_norm": gain((DEPTH, D_MODEL)),
        "ffn2_norm": gain((DEPTH, D_MODEL)),
        "ffn2_w_gate": w((DEPTH, D_MODEL, D_FF), D_MODEL),
        "ffn2_w_up": w((DEPTH, D_MODEL, D_FF), D_MODEL),
        "ffn2_w_down": w((DEPTH, D_FF, D_MODEL), D_FF),
        "ab_w_in": w((N_EVEN, D_MODEL, AB_IN), D_MODEL),
        "mla_q_lora_norm": gain((N_EVEN, MLA_Q_RANK)),
        "mla_w_uq": w((N_EVEN, MLA_Q_RANK, MLA_HEADS * (MLA_NOPE + MLA_ROPE)), MLA_Q_RANK),
        "mla_kv_lora_norm": gain((N_EVEN, MLA_KV_RANK)),
        "mla_w_ukv": w((N_EVEN, MLA_KV_RANK, MLA_HEADS * (MLA_NOPE + MLA_V)), MLA_KV_RANK),
        "mla_q_norm": gain((N_EVEN, MLA_NOPE + MLA_ROPE)),
        "mla_k_norm": gain((N_EVEN, MLA_NOPE + MLA_ROPE)),
        "diff_q_norm": gain((N_EVEN, DIFF_HEAD)),
        "diff_k_norm": gain((N_EVEN, DIFF_HEAD)),
        "diff_lambda_q1": small((N_EVEN, DIFF_HEAD), 0.1),
        "diff_lambda_k1": small((N_EVEN, DIFF_HEAD), 0.1),
        "diff_lambda_q2": small((N_EVEN, DIFF_HEAD), 0.1),
        "diff_lambda_k2": small((N_EVEN, DIFF_HEAD), 0.1),
        "diff_subln": gain((N_EVEN, 2 * DIFF_HEAD)),
        "ab_w_out": w((N_EVEN, AB_CAT, D_MODEL), AB_CAT),
        "c_w_in": w((N_ODD, D_MODEL, C_IN), D_MODEL),
        "c_q_norm": gain((N_ODD, C_HEAD)),
        "c_k_norm": gain((N_ODD, C_HEAD)),
        "c_w_out": w((N_ODD, C_HEADS * C_HEAD, D_MODEL), C_HEADS * C_HEAD),
    }

def reference(x, ffn1_norm, ffn1_w_gate, ffn1_w_up, ffn1_w_down, mix_norm,
              ffn2_norm, ffn2_w_gate, ffn2_w_up, ffn2_w_down,
              ab_w_in, mla_q_lora_norm, mla_w_uq, mla_kv_lora_norm, mla_w_ukv,
              mla_q_norm, mla_k_norm, diff_q_norm, diff_k_norm,
              diff_lambda_q1, diff_lambda_k1, diff_lambda_q2, diff_lambda_k2,
              diff_subln, ab_w_out, c_w_in, c_q_norm, c_k_norm, c_w_out):
    b, s, _ = x.shape
    n_rows = s // GRID_W
    pos = jnp.arange(s, dtype=jnp.int32)
    row_pos = jnp.repeat(jnp.arange(n_rows, dtype=jnp.int32), GRID_W)
    col_pos = jnp.tile(jnp.arange(GRID_W, dtype=jnp.int32), n_rows)
    mla_cs = rope_tables(pos, MLA_ROPE)
    diff_cs = rope_tables(pos, DIFF_HEAD)
    row_cs = rope_tables(row_pos, C_HEAD // 2)
    col_cs = rope_tables(col_pos, C_HEAD // 2)

    for i in range(DEPTH):
        x = x + 0.5 * swiglu(rms_norm(x, ffn1_norm[i]), ffn1_w_gate[i], ffn1_w_up[i], ffn1_w_down[i])
        h = rms_norm(x, mix_norm[i])
        j = i // 2
        if i % 2 == 0:
            lam_init = 0.8 - 0.6 * math.exp(-0.3 * i)
            x = x + even_mixer(h, ab_w_in[j], mla_q_lora_norm[j], mla_w_uq[j], mla_kv_lora_norm[j],
                               mla_w_ukv[j], mla_q_norm[j], mla_k_norm[j], diff_q_norm[j],
                               diff_k_norm[j], diff_lambda_q1[j], diff_lambda_k1[j],
                               diff_lambda_q2[j], diff_lambda_k2[j], diff_subln[j], ab_w_out[j],
                               mla_cs, diff_cs, lam_init)
        else:
            x = x + odd_mixer(h, c_w_in[j], c_q_norm[j], c_k_norm[j], c_w_out[j], row_cs, col_cs)
        x = x + 0.5 * swiglu(rms_norm(x, ffn2_norm[i]), ffn2_w_gate[i], ffn2_w_up[i], ffn2_w_down[i])
    return x


_drawn_inputs = setup_inputs


def setup_inputs(seed=0):
    import zlib

    import numpy as np

    out = dict(_drawn_inputs(seed))
    spreads = {}
    factors = {'ffn1_norm': 4.228,
     'mix_norm': 2.746,
     'ffn2_norm': 5.716,
     'mla_q_lora_norm': 8.0,
     'mla_kv_lora_norm': 8.0,
     'mla_q_norm': 8.0,
     'mla_k_norm': 8.0,
     'diff_q_norm': 7.507,
     'diff_k_norm': 4.91,
     'diff_lambda_q1': 8.0,
     'diff_lambda_k1': 5.225,
     'diff_lambda_q2': 7.232,
     'diff_subln': 14.423,
     'c_q_norm': 8.0,
     'c_k_norm': 8.0}
    for name, (base, spread) in spreads.items():
        noise = np.random.default_rng([zlib.crc32(name.encode()), seed]).standard_normal(out[name].shape)
        drawn = base * np.exp(spread * noise) if base else spread * noise
        out[name] = __import__('jax').numpy.asarray(drawn.astype(out[name].dtype))
    for name, factor in factors.items():
        out[name] = (out[name] * factor).astype(out[name].dtype)
    return out
```

```python
import math
from contextlib import ExitStack

import numpy as np

import concourse.bass as bass
from concourse import mybir

P = 128
D_MODEL, SEQ, D_FF, GRID_W = 1024, 512, 2816, 64
THETA, EPS = 10000.0, 1e-6
KD = D_MODEL // P
FT = D_FF // P
TT = SEQ // P
MLA_H, NOPE, ROPE, V_D = 8, 64, 32, 64
QK_D = NOPE + ROPE
Q_RANK, KV_RANK = 256, 128
DIFF_H, DIFF_D = 8, 32
GQA_H, GQA_KV, GQA_D = 16, 4, 64
LAM_INIT = 0.8 - 0.6 * math.exp(-0.3 * 0)

UNIT = 1024
RING = 4
LEAD = 2
LATENT = (Q_RANK + KV_RANK) // P
AB_TOK = ROPE + 3 * DIFF_H * 2 * DIFF_D
AB_GROUPS, AB_W = 4, AB_TOK // 4
C_TOK = (GQA_H + 2 * GQA_KV) * GQA_D
C_GROUPS, C_W = 3, C_TOK // 3
DQ0, DK0, DV0 = ROPE, ROPE + DIFF_H * 2 * DIFF_D, ROPE + 2 * DIFF_H * 2 * DIFF_D
CK0, CV0 = GQA_H * GQA_D, (GQA_H + GQA_KV) * GQA_D

DOWN_U = 3
FFN_UNITS = 2 * FT + DOWN_U * KD
AB_LAT, AB_G0 = 0, LATENT
AB_UP = AB_G0 + 4
AB_G1 = AB_UP + 3
AB_OUT = AB_G1 + 4 * (AB_GROUPS - 1)
AB_UNITS = AB_OUT + KD
C_OUT = 4 * C_GROUPS
C_UNITS = C_OUT + KD
FFN_AT = [0, FFN_UNITS + AB_UNITS, 2 * FFN_UNITS + AB_UNITS, 3 * FFN_UNITS + AB_UNITS + C_UNITS]
AB_AT = FFN_UNITS
C_AT = 3 * FFN_UNITS + AB_UNITS
N_UNITS = 4 * FFN_UNITS + AB_UNITS + C_UNITS
FFN_NORM = [0, 2, 3, 5]
AB_NORM, C_NORM = 1, 4

F32, F32R = mybir.dt.float32, mybir.dt.float32r
ALU = mybir.AluOpType
ACT = mybir.ActivationFunctionType
AX = mybir.AxisListType


def used(u):
    return RING + u + 1


def slot_free(u):
    return u + 1


def done(n):
    return n + 3


def free(n):
    return n + 1


def build_kernel(nc, x_in, weights, gains, lat_gain, rot_in, head_gains, rot_c_in, head_gains_c,
                 lam_in, subln_in, out):
    with ExitStack() as ctx:
        def sb(name, shape, dt=F32):
            return ctx.enter_context(nc.sbuf_tensor(name, shape, dt))

        def sem(name):
            return ctx.enter_context(nc.semaphore(name))

        def shared(*names_shapes):
            with ExitStack() as s:
                return [s.enter_context(nc.sbuf_tensor(n, sh, dt)) for n, sh, dt in names_shapes]

        x = sb("x", [P, KD, SEQ])
        stage = sb("stage", [P, RING, UNIT])
        w_hi = [sb(f"w_hi{s}", [P, UNIT], F32R) for s in range(RING)]
        w_lo = [sb(f"w_lo{s}", [P, UNIT], F32R) for s in range(RING)]
        tmp = sb("tmp", [P, 4, SEQ])
        acc = sb("acc", [P, SEQ])
        rstd = sb("rstd", [P, SEQ])
        ident = sb("ident", [P, P])
        ones_d = sb("ones_d", [P, P])
        ones_lat = sb("ones_lat", [P, 2])
        eps = sb("eps", [P, 1])
        gain = sb("gain", [P, 6, KD])
        lat_g = sb("lat_g", [P, LATENT])
        rot = sb("rot", [P, 2048])
        subln = sb("subln", [P, V_D])
        lam = sb("lam", [P, 4])
        rtok = sb("rtok", [P, 4 * TT])
        ss = sb("ss", [P, 256])

        (p_buf, pT, qT, kT, qa, qb, qc, ka, kb, kc_, negmax, rowsum, rinv) = shared(
            ("p_buf", [P, 4, SEQ], F32), ("pT", [P, 2, SEQ], F32), ("qT", [P, SEQ], F32),
            ("kT", [P, SEQ], F32), ("qa", [P, SEQ], F32), ("qb", [P, SEQ], F32), ("qc", [P, 512], F32),
            ("ka", [P, SEQ], F32), ("kb", [P, SEQ], F32), ("kc", [P, 512], F32),
            ("negmax", [P, 160], F32), ("rowsum", [P, 160], F32), ("rinv", [P, 160], F32))
        xg_hi = sb("xg_hi", [P, KD, SEQ], F32R)
        xg_lo = sb("xg_lo", [P, KD, SEQ], F32R)

        q_tok, kv_tok, ab_tok, ab_o, lat_hi, lat_lo, lat_sq = shared(
            ("q_tok", [P, TT, MLA_H * QK_D], F32), ("kv_tok", [P, TT, MLA_H * 128], F32),
            ("ab_tok", [P, TT, AB_TOK], F32), ("ab_o", [P, TT, D_MODEL], F32),
            ("lat_hi", [P, LATENT, SEQ], F32R), ("lat_lo", [P, LATENT, SEQ], F32R),
            ("lat_sq", [P, LATENT, SEQ], F32))
        oT_hi, oT_lo, c_tok, c_o, rot_c = shared(
            ("oT_hi", [P, KD, SEQ], F32R), ("oT_lo", [P, KD, SEQ], F32R),
            ("c_tok", [P, TT, C_TOK], F32), ("c_o", [P, TT, D_MODEL], F32), ("rot_c", [P, 2048], F32))
        hg, lam_v, lam_p = shared(("hg", [P, 2048], F32), ("lam_v", [P, 4, DIFF_D], F32),
                                  ("lam_p", [P, 2, DIFF_D], F32))
        h_hi = sb("h_hi", [P, FT, SEQ], F32R)
        h_lo = sb("h_lo", [P, FT, SEQ], F32R)

        bank = [ctx.enter_context(nc.psum_tensor(f"bank{b}", [P, 512], F32)) for b in range(8)]
        gate_b, up_b, y_b, stat_b = bank[0:2], bank[2:4], bank[4:6], bank[6]
        tok_stat_b = bank[3]
        c_b = [[bank[6], bank[7], bank[0], bank[1]], [bank[2], bank[4], bank[5], bank[3]]]
        s_b, pT_b, o_b, tr_b = bank[0:2], bank[2:4], bank[4:6], bank[6:8]

        landed = [sem(f"landed{s}") for s in range(RING)]
        hi_ready = sem("hi_ready")
        lo_ready = sem("lo_ready")
        unit_used = sem("unit_used")
        x_loaded = sem("x_loaded")
        consts_loaded = sem("consts_loaded")
        rot_c_loaded = sem("rot_c_loaded")
        consts_made = sem("consts_made")
        tables_made = sem("tables_made")
        lam_step = sem("lam_step")
        lam_exp = sem("lam_exp")
        xg_hi_done = sem("xg_hi_done")
        xg_ready = sem("xg_ready")
        sq_done = sem("sq_done")
        acc_zero = sem("acc_zero")
        acc_done = sem("acc_done")
        stat_done = sem("stat_done")
        std_done = sem("std_done")
        rstd_ready = sem("rstd_ready")
        gate_read = sem("gate_read")
        up_read = sem("up_read")
        silu_done = sem("silu_done")
        h_raw = sem("h_raw")
        h_hi_done = sem("h_hi_done")
        h_ready = sem("h_ready")
        x_new = sem("x_new")
        stored = sem("stored")
        waits_taken = sem("waits_taken")
        lat_hi_done = sem("lat_hi_done")
        lat_ready = sem("lat_ready")
        lat_stat = sem("lat_stat")
        lat_step = sem("lat_step")
        lat_std = sem("lat_std")
        tok_done = sem("tok_done")
        tok_act = sem("tok_act")
        tok_dve = sem("tok_dve")
        hs_sq = sem("hs_sq")
        hs_red = sem("hs_red")
        hs_keys = sem("hs_keys")
        hs_std = sem("hs_std")
        hs_ready = sem("hs_ready")
        q_step = sem("q_step")
        q_prep = sem("q_prep")
        k_step = sem("k_step")
        k_prep = sem("k_prep")
        tr_done = sem("tr_done")
        qT_ready = sem("qT_ready")
        kT_ready = sem("kT_ready")
        s_done = sem("s_done")
        max_done = sem("max_done")
        p_done = sem("p_done")
        w_step = sem("w_step")
        w_done = sem("w_done")
        pT_done = sem("pT_done")
        pT_ready = sem("pT_ready")
        o_done = sem("o_done")
        r_done = sem("r_done")
        o_out = sem("o_out")
        sub_step = sem("sub_step")
        sub_sq = sem("sub_sq")
        sub_std = sem("sub_std")
        oT_done = sem("oT_done")
        oT_hi_done = sem("oT_hi_done")
        oT_ready = sem("oT_ready")

        block = ctx.enter_context(nc.Block())

        tok = [slice(t * P, (t + 1) * P) for t in range(TT)]
        rstd_tok, rstd_sq = rtok[:, 0:4], rtok[:, 4:8]
        r_lat = rtok[:, 8:16]
        ss_q = ss[:, 0:32].rearrange("p (t h) -> p t h", t=TT)
        ss_k = ss[:, 32:64].rearrange("p (t h) -> p t h", t=TT)
        ss_kr = ss[:, 64:68]
        ss_d = ss[:, 68:196].rearrange("p (t h) -> p t h", t=TT)
        ss_c = ss[:, 0:80].rearrange("p (t h) -> p t h", t=TT)
        ss_o = ss[:, 196:228].rearrange("p (t h) -> p t h", t=TT)
        tmp2 = [tmp[:, 0:2, :].rearrange("p a n -> p (a n)"), tmp[:, 2:4, :].rearrange("p a n -> p (a n)")]

        def tables(src, specs):
            got, at = [], 0
            for n in specs:
                got.append(src[:, at:at + n])
                at += n
            return got

        m_cq, m_sq, m_ck, m_sk, d_cq, d_sq, d_ck, d_sk = tables(rot, [384, 128, 384, 128, 256, 256, 256, 256])
        c_cq, c_sq, c_ck, c_sk = tables(rot_c, [512] * 4)

        class Mla:
            iters, subs, parts, rows, width, heads = MLA_H, 1, 1, QK_D, QK_D, 1
            S0, B0, H0 = 2 * TT * DIFF_H, TT * DIFF_H, DIFF_H
            o = ab_o

            @staticmethod
            def v(i, sub, c):
                return kv_tok[:, c, bass.ds(i * 128 + NOPE, V_D)]

            @staticmethod
            def o_at(i, sub, a, t):
                return ab_o[:, t, bass.ds(i * V_D, V_D)]

        class Diff:
            iters, subs, parts, rows, width, heads = DIFF_H, 1, 2, DIFF_D, 2 * DIFF_D, 1
            S0, B0, H0 = 0, 0, 0
            o = ab_o

            @staticmethod
            def v(i, sub, c):
                return ab_tok[:, c, bass.ds(i * V_D + DV0, V_D)]

            @staticmethod
            def o_at(i, sub, a, t):
                return ab_o[:, t, bass.ds(i * V_D + MLA_H * V_D, V_D)]

        class Gqa:
            iters, subs, parts, rows, width, heads = GQA_KV, 2, 1, GQA_D, 2 * GQA_D, 2
            S0 = 2 * TT * DIFF_H + TT * MLA_H
            B0, H0 = TT * (DIFF_H + MLA_H), DIFF_H + MLA_H
            o = c_o

            @staticmethod
            def v(i, sub, c):
                return c_tok[:, c, bass.ds(i * V_D + CV0, V_D)]

            @staticmethod
            def o_at(i, sub, a, t):
                return c_o[:, t, bass.ds(i * 4 * GQA_D + (2 * sub + a) * GQA_D, V_D)]

        def apart(eng):
            eng.sem_inc(waits_taken, 1)

        def block_at(cfg, n, bl):
            return n * (TT * cfg.heads) + (cfg.B0 + bl)

        def score_at(cfg, n, bl, part):
            return n * (TT * cfg.heads * cfg.parts) + (cfg.S0 + bl * cfg.parts + part)

        def next_pair(cfg, i, sub):
            return (i, sub + 1) if sub + 1 < cfg.subs else (i + 1, 0)

        def each_pair(eng, cfg, body):
            with eng.Fori(0, cfg.iters - 1) as i:
                for sub in range(cfg.subs):
                    body(i, sub, i * cfg.subs + sub, True)
            i = cfg.iters - 1
            for sub in range(cfg.subs):
                body(i, sub, i * cfg.subs + sub, sub + 1 < cfg.subs)

        mla_sums = [(ab_tok[:, :, 0:ROPE], ss_kr, ROPE)]
        mla_sums += [(q_tok[:, t, :].rearrange("p (h d) -> p h d", d=QK_D), ss_q[:, t, :], QK_D) for t in range(TT)]
        mla_sums += [(kv_tok[:, t, :].rearrange("p (h d) -> p h d", d=128)[:, :, 0:NOPE], ss_k[:, t, :], NOPE)
                     for t in range(TT)]
        diff_sums = [(ab_tok[:, t, DQ0:DV0].rearrange("p (h d) -> p h d", d=DIFF_D), ss_d[:, t, :], DIFF_D)
                     for t in range(TT)]
        c_sums = [(c_tok[:, t, 0:CK0].rearrange("p (h d) -> p h d", d=GQA_D), ss_c[:, t, 0:GQA_H], GQA_D)
                  for t in range(TT)]
        c_sums += [(c_tok[:, t, CK0:CV0].rearrange("p (h d) -> p h d", d=GQA_D), ss_c[:, t, GQA_H:], GQA_D)
                   for t in range(TT)]
        SUMS_AT = {"mla": 0, "diff": len(mla_sums), "c": len(mla_sums) + len(diff_sums)}

        def squares(at, src):
            h, d = src.shape[1], src.shape[2]
            return tmp2[at % 2][:, 0:h * d].rearrange("p (h d) -> p h d", d=d)

        TABLES_AB, TABLES_C = 6, 2
        AB_COPIES, AB_TOKS = 2 * AB_GROUPS + 8, 3 * AB_GROUPS + 6 + 7

        @block.sync
        def _(sp):
            sp.dma_start(x[:], x_in).then_inc(x_loaded, 16)
            for dst, src in ((gain, gains), (lat_g, lat_gain), (rot, rot_in), (hg, head_gains),
                             (lam_v, lam_in), (subln, subln_in)):
                sp.dma_start(dst[:], src).then_inc(consts_loaded, 16)
            for s in range(RING):
                sp.dma_start(stage[:, s, :], weights[s]).then_inc(landed[s], 16)
            with sp.Fori(1, N_UNITS // RING) as i:
                for s in range(RING):
                    sp.wait_ge(lo_ready, i * RING + (s - RING + 1))
                    sp.dma_start(stage[:, s, :], weights[i * RING + s]).then_inc(landed[s], 16)
            for u in range(N_UNITS // RING * RING, N_UNITS):
                sp.wait_ge(lo_ready, u - RING + 1)
                sp.dma_start(stage[:, u % RING, :], weights[u]).then_inc(landed[u % RING], 16)
            for m in range(KD):
                sp.wait_ge(x_new, done(5 * KD + m))
                sp.dma_start(out[:, m, :], x[:, m, :]).then_inc(stored, 16)
            sp.wait_ge(stored, 16 * KD)

        @block.gpsimd
        def _(pool):
            def split_lo(u, s):
                pool.wait_ge(hi_ready, u + 1)
                pool.tensor_tensor(w_lo[s][:], stage[:, s, :], w_hi[s][:].bitcast(F32),
                                   ALU.subtract).then_inc(lo_ready, 1)

            def split_range(a, b):
                n = (b - a) // RING
                if n > 1:
                    with pool.Fori(0, n) as i:
                        for s in range(RING):
                            split_lo(i * RING + (a + s), (a + s) % RING)
                    a += n * RING
                for u in range(a, b):
                    split_lo(u, u % RING)

            pool.memset(ident[:], 0.0).then_inc(consts_made, 1)
            pool.wait_ge(consts_made, 1)
            pool.affine_select(out=ident[:], in_=ident[:], compare_op=ALU.not_equal, fill=1.0, base=0,
                               pattern=[[-1, P]], channel_multiplier=1).then_inc(consts_made, 1)
            pool.memset(ones_d[:], 1.0 / D_MODEL).then_inc(consts_made, 1)
            pool.memset(ones_lat[:, 0:1], 1.0 / Q_RANK).then_inc(consts_made, 1)
            pool.memset(ones_lat[:, 1:2], 1.0 / KV_RANK).then_inc(consts_made, 1)
            pool.memset(eps[:], EPS).then_inc(consts_made, 1)

            def keys(cfg, i, sub, n):
                at = [0]
                per = 2

                def step(ins):
                    at[0] += 1
                    ins.then_inc(k_step, 1)
                    pool.wait_ge(k_step, n * per + (cfg.H0 * per + at[0]))

                pool.wait_ge(tr_done, n * 2 + (2 * cfg.H0 + 2))
                apart(pool)
                if cfg is Mla:
                    a3 = ka[:, 0:384].rearrange("p (t d) -> p t d", t=TT)
                    b3 = kb[:, 0:384].rearrange("p (t d) -> p t d", t=TT)
                    c3 = kc_[:, 0:128].rearrange("p (t d) -> p t d", t=TT)
                    s3 = m_sk.rearrange("p (t d) -> p t d", t=TT)
                    r = ss_k[:, :, bass.ds(i, 1)]
                    pool.tensor_tensor(a3[:, :, 0:NOPE], kv_tok[:, :, bass.ds(i * 128, NOPE)],
                                       r.to_broadcast([P, TT, NOPE]), ALU.mult)
                    step(pool.tensor_tensor(a3[:, :, NOPE:QK_D], ab_tok[:, :, 0:ROPE],
                                            r.to_broadcast([P, TT, ROPE]), ALU.mult))
                    b_rot, a_rot, cos = b3[:, :, NOPE:QK_D], a3[:, :, NOPE:QK_D], m_ck
                    b_all, a_all = kb[:, 0:384], ka[:, 0:384]
                else:
                    if cfg is Diff:
                        n_el, src = 256, ab_tok[:, :, bass.ds(i * 64 + DK0, 64)].rearrange(
                            "p t (e d) -> p t e d", e=2)
                        r = ss_d[:, :, bass.ds(i * 2 + 16, 2)]
                        cos, sin, d = d_ck, d_sk, DIFF_D
                        r = r[:, :, :, None].to_broadcast([P, TT, 2, d])
                    else:
                        n_el, src = 512, c_tok[:, :, None, bass.ds(i * GQA_D + CK0, GQA_D)].to_broadcast(
                            [P, TT, 2, GQA_D])
                        cos, sin, d = c_ck, c_sk, GQA_D
                        r = ss_c[:, :, bass.ds(i + GQA_H, 1), None].to_broadcast([P, TT, 2, d])
                    a4 = ka[:, 0:n_el].rearrange("p (t e d) -> p t e d", t=TT, e=2)
                    step(pool.tensor_tensor(a4, src, r, ALU.mult))
                    a_all, b_all = ka[:, 0:n_el], kb[:, 0:n_el]
                    a_rot = a_all.rearrange("p (g d) -> p g d", d=32)
                    b_rot = b_all.rearrange("p (g d) -> p g d", d=32)
                    c3 = kc_[:, 0:n_el].rearrange("p (g d) -> p g d", d=32)
                    s3 = sin.rearrange("p (g d) -> p g d", d=32)
                pool.tensor_tensor(b_all, a_all, cos, ALU.mult)
                pool.tensor_tensor(c3[:, :, 0:16], a_rot[:, :, 16:32], s3[:, :, 0:16], ALU.mult)
                step(pool.tensor_tensor(c3[:, :, 16:32], a_rot[:, :, 0:16], s3[:, :, 16:32], ALU.mult))
                pool.tensor_tensor(b_rot, b_rot, c3, ALU.add).then_inc(k_prep, 1)
                assert at[0] == per

            def all_keys(cfg):
                with pool.Fori(0, cfg.iters) as i:
                    for sub in range(cfg.subs):
                        keys(cfg, i, sub, i * cfg.subs + sub)

            split_range(0, AB_AT + AB_OUT + LEAD)
            pool.wait_ge(tables_made, TABLES_AB)
            pool.wait_ge(hs_ready, 2)
            pool.wait_ge(unit_used, used(AB_AT + AB_OUT - 1))
            all_keys(Diff)
            all_keys(Mla)
            split_range(AB_AT + AB_OUT + LEAD, C_AT + C_OUT + LEAD)
            pool.wait_ge(tables_made, TABLES_AB + TABLES_C)
            pool.wait_ge(hs_ready, 3)
            all_keys(Gqa)
            split_range(C_AT + C_OUT + LEAD, N_UNITS)

        @block.scalar
        def _(act):
            def split_hi(a, i=0, step=0):
                s = a % RING
                act.wait_ge(landed[s], i * (16 * step // RING) + 16 * (a // RING + 1))
                act.wait_ge(unit_used, slot_free(i * step + a))
                act.activation(w_hi[s][:], stage[:, s, :], ACT.Copy).then_inc(hi_ready, 1)

            def norm_chunk(n, m):
                act.activation(xg_hi[:, m, :], x[:, m, :], ACT.Copy,
                               scale=gain[:, n, m]).then_inc(xg_hi_done, 1)

            def norm_square(n, m, s):
                act.activation(tmp[:, s, :], x[:, m, :], ACT.Square).then_inc(sq_done, 1)

            def ffn_tile(c, u0, n, j, jj, i=0):
                p = jj % 2
                split_hi(u0 + 2 * jj + LEAD, i, 4)
                split_hi(u0 + 2 * jj + LEAD + 1, i, 4)
                if jj == 0:
                    act.wait_ge(stat_done, n + 1)
                    act.activation(rstd[:], stat_b[:], ACT.Sqrt, bias=eps[:]).then_inc(std_done, 1)
                act.wait_ge(gate_read, done(j + FT * c))
                act.activation(tmp[:, p, :], tmp[:, p, :], ACT.Silu).then_inc(silu_done, 1)
                act.wait_ge(h_raw, j + (FT * c + 1))
                apart(act)
                act.activation(h_hi[:, j, :] if isinstance(j, int) else h_hi[:, bass.ds(j, 1), :].rearrange("p a n -> p (a n)"),
                               tmp[:, 2 + p, :], ACT.Copy).then_inc(h_hi_done, 1)

            def ffn(c):
                u0, n = FFN_AT[c], FFN_NORM[c]
                ffn_tile(c, u0, n, 0, 0)
                ffn_tile(c, u0, n, 1, 1)
                with act.Fori(0, FT // 2 - 1) as i:
                    for jj in (2, 3):
                        ffn_tile(c, u0, n, i * 2 + jj, jj, i)

            def out_chunks(q, u0, per):
                n = q + 1
                with act.Fori(0, KD // 4) as i:
                    for mm in range(4):
                        m = i * 4 + mm
                        for r in range(per):
                            split_hi(u0 + per * mm + r + LEAD, i, 4 * per)
                        act.wait_ge(x_new, done(m + KD * q))
                        apart(act)
                        act.activation(xg_hi[:, bass.ds(m, 1), :].rearrange("p a n -> p (a n)"),
                                       x[:, bass.ds(m, 1), :].rearrange("p a n -> p (a n)"), ACT.Copy,
                                       scale=gain[:, n, bass.ds(m, 1)]).then_inc(xg_hi_done, 1)
                        act.wait_ge(acc_done, m + (KD * n - 1))
                        apart(act)
                        act.activation(tmp[:, mm % 2, :], x[:, bass.ds(m, 1), :].rearrange("p a n -> p (a n)"),
                                       ACT.Square).then_inc(sq_done, 1)

            def token_stat(n):
                act.wait_ge(stat_done, n + 1)
                act.activation(rstd_tok, tok_stat_b[:, 0:TT], ACT.Sqrt, bias=eps[:]).then_inc(std_done, 1)

            def copy_groups(u, toks, banks, dst, width, g):
                for t in (0, 2):
                    act.wait_ge(tok_done, toks + t + 1)
                    act.activation(dst[:, t, g * width:(g + 1) * width], banks[t][:, 0:width], ACT.Copy,
                                   scale=rstd_tok[:, t:t + 1]).then_inc(tok_act, 1)

            def head_squares(at, sums):
                for k, (src, _, _) in enumerate(sums):
                    if at + k >= 2:
                        act.wait_ge(hs_red, at + k - 1)
                    act.activation(squares(at + k, src), src, ACT.Square).then_inc(hs_sq, 1)

            def head_roots(at, v, d):
                act.wait_ge(hs_red, at)
                act.activation(v, v, ACT.Sqrt, scale=1.0 / d, bias=eps[:]).then_inc(hs_std, 1)

            def attention(cfg):
                nb = TT * cfg.heads
                w = cfg.width

                def copy_queries(n):
                    act.wait_ge(tr_done, n * 2 + (2 * cfg.H0 + 2 + 1))
                    act.activation(qT[0:w, :], tr_b[0][0:w, :], ACT.Copy).then_inc(qT_ready, 1)

                def exps(n, bl):
                    for part in range(cfg.parts):
                        sat = score_at(cfg, n, bl, part)
                        act.wait_ge(max_done, sat + 1)
                        act.wait_ge(pT_done, free(block_at(cfg, n, bl)))
                        apart(act)
                        slot = bl % 2 if cfg.parts == 1 else 2 * (bl % 2) + part
                        s = bl % 2 if cfg.parts == 1 else part
                        act.activation(p_buf[:, slot, :], s_b[s][:], ACT.Exp, bias=negmax[:, bass.ds(sat, 1)],
                                       accum_out=rowsum[:, bass.ds(sat, 1)]).then_inc(p_done, 1)

                def copy_pT(n, bl):
                    b = block_at(cfg, n, bl)
                    act.wait_ge(pT_done, done(b))
                    act.wait_ge(o_done, free(b))
                    act.activation(pT[:, bl % 2, :], pT_b[bl % 2][:], ACT.Copy).then_inc(pT_ready, 1)

                def pair(i, sub, n, has_next):
                    for bl in range(nb):
                        if bl + 1 < nb:
                            exps(n, bl + 1)
                        if bl == nb - 2 and has_next:
                            copy_queries(n + 1)
                        copy_pT(n, bl)
                    if has_next:
                        exps(n + 1, 0)

                copy_queries(0)
                exps(0, 0)
                each_pair(act, cfg, pair)

            def transposed_out(base):
                for k in range(KD):
                    act.wait_ge(oT_done, base + k + 1)
                    act.activation(oT_hi[:, k, :], tr_b[k % 2][:], ACT.Copy).then_inc(oT_hi_done, 1)

            act.wait_ge(consts_loaded, 16 * 6)
            act.wait_ge(consts_made, 6)
            act.wait_ge(x_loaded, 16)
            for u in range(LEAD):
                split_hi(u)
            for m in range(KD):
                act.activation(xg_hi[:, m, :], x[:, m, :], ACT.Copy,
                               scale=gain[:, 0, m:m + 1]).then_inc(xg_hi_done, 1)
                if m >= 2:
                    act.wait_ge(acc_done, m - 1)
                act.activation(tmp[:, m % 2, :], x[:, m, :], ACT.Square).then_inc(sq_done, 1)
            act.wait_ge(lam_step, 2)
            act.activation(lam[:, 2:4], lam[:, 0:2], ACT.Exp).then_inc(lam_exp, 1)

            ffn(0)
            out_chunks(0, FFN_AT[0] + 2 * FT, DOWN_U)

            u0 = AB_AT
            for m in range(LATENT):
                split_hi(u0 + AB_LAT + m + LEAD)
                if m == 1:
                    token_stat(AB_NORM)
                act.wait_ge(unit_used, used(u0 + AB_LAT + m))
                act.activation(lat_hi[:, m, :], bank[m][:], ACT.Copy, scale=lat_g[:, m:m + 1])
                act.activation(lat_sq[:, m, :], bank[m][:], ACT.Square).then_inc(lat_hi_done, 1)
            for k in range(4):
                split_hi(u0 + AB_G0 + k + LEAD)
            act.wait_ge(lat_step, 2)
            act.activation(r_lat, r_lat, ACT.Sqrt, bias=eps[:]).then_inc(lat_std, 1)
            act.wait_ge(rstd_ready, AB_NORM + 1)
            copy_groups(u0 + AB_G0 + 3, 0, bank[4:8], ab_tok, AB_W, 0)
            act.wait_ge(lat_step, 4)
            for o in range(16):
                if o in (0, 4, 8):
                    split_hi(u0 + AB_UP + min(o // 4, 2) + LEAD)
                if o % 2:
                    continue
                half, t = o // 4 % 2, o % 4
                act.wait_ge(tok_done, 3 + (3 * (o // 4) + t if o < 8 else 6 + o - 8) + 1)
                dst = (q_tok[:, t, half * 384:half * 384 + 384] if o < 8 else
                       kv_tok[:, t, half * 512:half * 512 + 512])
                n_el = 384 if o < 8 else 512
                r = r_lat[:, t:t + 1] if o < 8 else r_lat[:, TT + t:TT + t + 1]
                act.activation(dst, bank[o % 8][:, 0:n_el], ACT.Copy, scale=r).then_inc(tok_act, 1)
            for g in range(1, AB_GROUPS):
                for k in range(4):
                    split_hi(u0 + AB_G1 + 4 * (g - 1) + k + LEAD)
                if g == 1:
                    act.wait_ge(tok_dve, 10)
                    act.wait_ge(tok_act, 10)
                    head_squares(SUMS_AT["mla"], mla_sums)
                    act.wait_ge(hs_keys, 1)
                    head_roots(SUMS_AT["diff"], ss[:, 0:64], QK_D)
                if g == 3:
                    act.wait_ge(tok_dve, 14)
                    act.wait_ge(tok_act, 14)
                    head_squares(SUMS_AT["diff"], diff_sums)
                    head_roots(SUMS_AT["c"], ss[:, 68:196], DIFF_D)
                copy_groups(u0 + AB_G1 + 4 * g - 1, 16 + 3 * (g - 1), bank[0:4] if g % 2 else bank[4:8],
                            ab_tok, AB_W, g)
            attention(Diff)
            act.wait_ge(sub_step, TT * 2)
            act.activation(ss[:, 196:228], ss[:, 196:228], ACT.Sqrt, scale=1.0 / V_D,
                           bias=eps[:]).then_inc(sub_std, 1)
            attention(Mla)
            transposed_out(0)
            out_chunks(1, AB_AT + AB_OUT, 1)

            ffn(1)
            out_chunks(2, FFN_AT[1] + 2 * FT, DOWN_U)
            ffn(2)
            out_chunks(3, FFN_AT[2] + 2 * FT, DOWN_U)

            act.dma_start(rot_c[:], rot_c_in).then_inc(rot_c_loaded, 16)
            act.dma_start(hg[:], head_gains_c).then_inc(rot_c_loaded, 16)
            for g in range(C_GROUPS):
                for k in range(4):
                    split_hi(C_AT + 4 * g + k + LEAD)
                if g == 0:
                    token_stat(C_NORM)
                    act.wait_ge(rstd_ready, C_NORM + 1)
                if g == 2:
                    pass
                copy_groups(C_AT + 4 * g + 3, AB_TOKS + 3 * g, c_b[g % 2], c_tok, C_W, g)
            act.wait_ge(tok_dve, AB_COPIES + 2 * C_GROUPS)
            act.wait_ge(tok_act, AB_COPIES + 2 * C_GROUPS)
            head_squares(SUMS_AT["c"], c_sums)
            head_roots(SUMS_AT["c"] + len(c_sums), ss[:, 0:80], GQA_D)
            attention(Gqa)
            transposed_out(KD)
            out_chunks(4, C_AT + C_OUT, 1)

            ffn(3)
            u0 = FFN_AT[3] + 2 * FT + LEAD
            loops = (N_UNITS - u0) // RING
            with act.Fori(0, loops) as i:
                for k in range(RING):
                    split_hi(u0 + k, i, RING)
            for u in range(u0 + loops * RING, N_UNITS):
                split_hi(u)

        @block.vector
        def _(dve):
            def at_chunk(buf, m):
                return buf[:, m, :] if isinstance(m, int) else buf[:, bass.ds(m, 1), :].rearrange("p a n -> p (a n)")

            def norm_chunk(n, m, mm):
                dve.wait_ge(xg_hi_done, m + (KD * n + 1))
                g = gain[:, n, bass.ds(m, 1)] if not isinstance(m, int) else gain[:, n, m:m + 1]
                dve.scalar_tensor_tensor(out=at_chunk(xg_lo, m), in0=at_chunk(x, m), scalar=g,
                                         in1=at_chunk(xg_hi, m).bitcast(F32), op0=ALU.mult,
                                         op1=ALU.subtract).then_inc(xg_ready, 1)
                dve.wait_ge(sq_done, m + (KD * n + 1))
                if not (isinstance(m, int) and m + KD * n == 0):
                    dve.wait_ge(acc_done, m + KD * n)
                dve.tensor_tensor(acc[:], acc[:], tmp[:, mm % 2, :], ALU.add).then_inc(acc_done, 1)

            def zero_acc(n):
                dve.memset(acc[:], 0.0).then_inc(acc_zero, 1)
                dve.wait_ge(acc_zero, n + 1)

            def ffn_tile(c, u0, n, j, jj):
                p = jj % 2
                first = jj < 2
                u = j * 2 + u0
                dve.wait_ge(unit_used, used(u))
                if not first:
                    dve.wait_ge(h_raw, j + (FT * c - 1))
                dve.tensor_tensor(tmp[:, p, :], gate_b[p][:], rstd[:], ALU.mult).then_inc(gate_read, 1)
                dve.wait_ge(unit_used, used(u + 1))
                if not first:
                    dve.wait_ge(h_ready, j + (FT * c - 1))
                dve.tensor_tensor(tmp[:, 2 + p, :], up_b[p][:], rstd[:], ALU.mult).then_inc(up_read, 1)
                if jj > 0:
                    hidden_lo(c, j - 1, 1 - p)
                dve.wait_ge(silu_done, j + (FT * c + 1))
                dve.wait_ge(up_read, done(j + FT * c))
                dve.tensor_tensor(tmp[:, 2 + p, :], tmp[:, p, :], tmp[:, 2 + p, :], ALU.mult).then_inc(h_raw, 1)

            def hidden_lo(c, j, p):
                dve.wait_ge(h_hi_done, j + (FT * c + 1))
                dve.tensor_tensor(at_chunk(h_lo, j), tmp[:, 2 + p, :], at_chunk(h_hi, j).bitcast(F32),
                                  ALU.subtract).then_inc(h_ready, 1)

            def ffn(c):
                u0, n = FFN_AT[c], FFN_NORM[c]
                dve.wait_ge(std_done, n + 1)
                dve.reciprocal(rstd[:], rstd[:]).then_inc(rstd_ready, 1)
                dve.wait_ge(rstd_ready, n + 1)
                ffn_tile(c, u0, n, 0, 0)
                ffn_tile(c, u0, n, 1, 1)
                with dve.Fori(0, FT // 2 - 1) as i:
                    for jj in (2, 3):
                        ffn_tile(c, u0, n, i * 2 + jj, jj)
                hidden_lo(c, FT - 1, (FT - 1) % 2)

            def out_chunks(q, u0, per, coef, last=False):
                n = q + 1
                if not last:
                    zero_acc(n)
                with dve.Fori(0, KD // 4) as i:
                    for mm in range(4):
                        m = i * 4 + mm
                        dve.wait_ge(unit_used, used(i * (4 * per) + (u0 + per * mm + per - 1)))
                        dve.scalar_tensor_tensor(out=at_chunk(x, m), in0=y_b[mm % 2][:], scalar=coef,
                                                 in1=at_chunk(x, m), op0=ALU.mult, op1=ALU.add).then_inc(x_new, 1)
                        if not last:
                            dve.wait_ge(x_new, done(m + KD * q))
                            norm_chunk(n, m, mm)

            def token_stat(n):
                dve.wait_ge(std_done, n + 1)
                dve.reciprocal(rstd_tok, rstd_tok).then_inc(rstd_ready, 1)
                dve.wait_ge(rstd_ready, n + 1)

            def copy_groups(u, toks, banks, dst, width, g):
                for t in (1, 3):
                    if t == 3:
                        dve.wait_ge(unit_used, used(u))
                    else:
                        dve.wait_ge(tok_done, toks + t + 1)
                    dve.tensor_scalar(dst[:, t, g * width:(g + 1) * width], banks[t][:, 0:width],
                                      rstd_tok[:, t:t + 1], None, ALU.mult).then_inc(tok_dve, 1)

            def head_sums(at, sums):
                for k, (src, dst, _) in enumerate(sums):
                    dve.wait_ge(hs_sq, at + k + 1)
                    dve.tensor_reduce(dst, squares(at + k, src), AX.X, ALU.add).then_inc(hs_red, 1)

            def head_inverse(k, v):
                dve.wait_ge(hs_std, k)
                dve.reciprocal(v, v).then_inc(hs_ready, 1)

            def attention(cfg):
                nb = TT * cfg.heads
                w = cfg.width

                def queries(i, sub, n):
                    at = [0]

                    def step(ins):
                        at[0] += 1
                        ins.then_inc(q_step, 1)
                        dve.wait_ge(q_step, n * 2 + (cfg.H0 * 2 + at[0]))

                    dve.wait_ge(tr_done, n * 2 + (2 * cfg.H0 + 2 - 1))
                    if cfg is Mla:
                        a3 = qa[:, 0:384].rearrange("p (t d) -> p t d", t=TT)
                        step(dve.tensor_tensor(a3, q_tok[:, :, bass.ds(i * QK_D, QK_D)],
                                               ss_q[:, :, bass.ds(i, 1)].to_broadcast([P, TT, QK_D]), ALU.mult))
                        b3 = qb[:, 0:384].rearrange("p (t d) -> p t d", t=TT)
                        a_all, b_all, cos = qa[:, 0:384], qb[:, 0:384], m_cq
                        a_rot, b_rot = a3[:, :, NOPE:QK_D], b3[:, :, NOPE:QK_D]
                        c3 = qc[:, 0:128].rearrange("p (t d) -> p t d", t=TT)
                        s3 = m_sq.rearrange("p (t d) -> p t d", t=TT)
                    else:
                        if cfg is Diff:
                            n_el, d, cos, sin = 256, DIFF_D, d_cq, d_sq
                            src = ab_tok[:, :, bass.ds(i * 64 + DQ0, 64)].rearrange("p t (e d) -> p t e d", e=2)
                            r = ss_d[:, :, bass.ds(i * 2, 2), None].to_broadcast([P, TT, 2, d])
                        else:
                            n_el, d, cos, sin = 512, GQA_D, c_cq, c_sq
                            src = c_tok[:, :, bass.ds(i * 256 + sub * 128, 128)].rearrange(
                                "p t (e d) -> p t e d", e=2)
                            r = ss_c[:, :, bass.ds(i * 4 + sub * 2, 2), None].to_broadcast([P, TT, 2, d])
                        step(dve.tensor_tensor(qa[:, 0:n_el].rearrange("p (t e d) -> p t e d", t=TT, e=2),
                                               src, r, ALU.mult))
                        a_all, b_all = qa[:, 0:n_el], qb[:, 0:n_el]
                        a_rot = a_all.rearrange("p (g d) -> p g d", d=32)
                        b_rot = b_all.rearrange("p (g d) -> p g d", d=32)
                        c3 = qc[:, 0:n_el].rearrange("p (g d) -> p g d", d=32)
                        s3 = sin.rearrange("p (g d) -> p g d", d=32)
                    dve.tensor_tensor(b_all, a_all, cos, ALU.mult)
                    dve.tensor_tensor(c3[:, :, 0:16], a_rot[:, :, 16:32], s3[:, :, 0:16], ALU.mult)
                    step(dve.tensor_tensor(c3[:, :, 16:32], a_rot[:, :, 0:16], s3[:, :, 16:32], ALU.mult))
                    dve.tensor_tensor(b_rot, b_rot, c3, ALU.add).then_inc(q_prep, 1)

                def copy_keys(n):
                    dve.wait_ge(tr_done, n * 2 + (2 * cfg.H0 + 2 + 2))
                    dve.tensor_copy(kT[0:w, :], tr_b[1][0:w, :]).then_inc(kT_ready, 1)

                def maxima(n, bl):
                    for part in range(cfg.parts):
                        sat = score_at(cfg, n, bl, part)
                        s = bl % 2 if cfg.parts == 1 else part
                        dve.wait_ge(s_done, sat + 1)
                        dve.tensor_reduce(negmax[:, bass.ds(sat, 1)], s_b[s][:], AX.X, ALU.max,
                                          negate=True).then_inc(max_done, 1)

                def combine(n, bl):
                    sat = score_at(cfg, n, bl, 0)
                    b = n * nb + bl
                    p1, p2 = p_buf[:, 2 * (bl % 2), :], p_buf[:, 2 * (bl % 2) + 1, :]
                    dve.wait_ge(p_done, done(score_at(cfg, n, bl, 1)))
                    dve.reciprocal(rinv[:, bass.ds(sat, 2)], rowsum[:, bass.ds(sat, 2)]).then_inc(w_step, 1)
                    dve.wait_ge(w_step, b * 2 + 1)
                    dve.tensor_scalar(p2, p2, rinv[:, bass.ds(sat + 1, 1)], lam[:, 0:1], ALU.mult,
                                      ALU.mult).then_inc(w_step, 1)
                    dve.wait_ge(w_step, b * 2 + 2)
                    dve.scalar_tensor_tensor(out=p1, in0=p1, scalar=rinv[:, bass.ds(sat, 1)], in1=p2,
                                             op0=ALU.mult, op1=ALU.add).then_inc(w_done, 1)

                def out_block(i, sub, n, bl):
                    b = block_at(cfg, n, bl)
                    dst = cfg.o_at(i, sub, bl // TT, bl % TT)
                    if cfg.parts == 2:
                        dve.wait_ge(o_done, done(b))
                        dve.tensor_copy(dst, o_b[bl % 2][:, 0:V_D]).then_inc(o_out, 1)
                        return
                    sat = score_at(cfg, n, bl, 0)
                    dve.wait_ge(p_done, done(sat))
                    dve.reciprocal(rinv[:, bass.ds(sat, 1)], rowsum[:, bass.ds(sat, 1)]).then_inc(r_done, 1)
                    dve.wait_ge(r_done, sat + (1 - Mla.S0))
                    dve.wait_ge(o_done, done(b))
                    dve.tensor_scalar(dst, o_b[bl % 2][:, 0:V_D], rinv[:, bass.ds(sat, 1)], None,
                                      ALU.mult).then_inc(o_out, 1)

                def pair(i, sub, n, has_next):
                    for bl in range(nb):
                        if bl + 1 < nb:
                            maxima(n, bl + 1)
                        if bl == 0 and has_next:
                            queries(*next_pair(cfg, i, sub), n + 1)
                        if bl == nb - 2 and has_next:
                            copy_keys(n + 1)
                        if cfg.parts == 2:
                            combine(n, bl)
                        if bl > 0:
                            out_block(i, sub, n, bl - 1)
                    if has_next:
                        maxima(n + 1, 0)
                    out_block(i, sub, n, nb - 1)

                queries(0, 0, 0)
                copy_keys(0)
                maxima(0, 0)
                each_pair(dve, cfg, pair)

            def transposed_out(base):
                for k in range(KD):
                    dve.wait_ge(oT_hi_done, base + k + 1)
                    dve.tensor_tensor(oT_lo[:, k, :], tr_b[k % 2][:], oT_hi[:, k, :].bitcast(F32),
                                      ALU.subtract).then_inc(oT_ready, 1)

            dve.wait_ge(consts_loaded, 16 * 6)
            dve.wait_ge(consts_made, 6)
            for k, scale in enumerate((QK_D ** -0.5, 1.0, DIFF_D ** -0.5, 1.0)):
                seg = rot[:, 512 * k:512 * k + 512]
                dve.scalar_tensor_tensor(out=seg, in0=seg, scalar=scale, in1=hg[:, 512 * k:512 * k + 512],
                                         op0=ALU.mult, op1=ALU.mult).then_inc(tables_made, 1)
            dve.tensor_scalar(subln[:], subln[:], 1.0 - LAM_INIT, None, ALU.mult).then_inc(tables_made, 1)
            dve.tensor_tensor(lam_p[:], lam_v[:, 0:4:2, :], lam_v[:, 1:4:2, :], ALU.mult).then_inc(lam_step, 1)
            dve.wait_ge(lam_step, 1)
            dve.tensor_reduce(lam[:, 0:2], lam_p[:], AX.X, ALU.add).then_inc(lam_step, 1)

            zero_acc(0)
            dve.wait_ge(x_loaded, 16)
            for m in range(KD):
                norm_chunk(0, m, m)
            dve.wait_ge(lam_exp, 1)
            dve.scalar_tensor_tensor(out=lam[:, 0:1], in0=lam[:, 3:4], scalar=-LAM_INIT, in1=lam[:, 2:3],
                                     op0=ALU.add, op1=ALU.subtract).then_inc(tables_made, 1)

            ffn(0)
            out_chunks(0, FFN_AT[0] + 2 * FT, DOWN_U, 0.5)

            u0 = AB_AT
            token_stat(AB_NORM)
            dve.tensor_tensor(rstd_sq, rstd_tok, rstd_tok, ALU.mult).then_inc(lat_step, 1)
            for m in range(LATENT):
                dve.wait_ge(lat_hi_done, m + 1)
                dve.scalar_tensor_tensor(out=lat_lo[:, m, :], in0=bank[m][:], scalar=lat_g[:, m:m + 1],
                                         in1=lat_hi[:, m, :].bitcast(F32), op0=ALU.mult,
                                         op1=ALU.subtract).then_inc(lat_ready, 1)
            dve.wait_ge(lat_stat, 1)
            dve.wait_ge(lat_step, 1)
            dve.tensor_tensor(r_lat.rearrange("p (a t) -> p a t", a=2),
                              tok_stat_b[:, TT:3 * TT].rearrange("p (a t) -> p a t", a=2),
                              rstd_sq[:, None, :].to_broadcast([P, 2, TT]), ALU.mult).then_inc(lat_step, 1)
            dve.wait_ge(lat_std, 1)
            dve.reciprocal(r_lat, r_lat).then_inc(lat_step, 1)
            dve.wait_ge(lat_step, 3)
            dve.tensor_tensor(r_lat.rearrange("p (a t) -> p a t", a=2), r_lat.rearrange("p (a t) -> p a t", a=2),
                              rstd_tok[:, None, :].to_broadcast([P, 2, TT]), ALU.mult).then_inc(lat_step, 1)
            dve.wait_ge(lat_step, 4)
            copy_groups(u0 + AB_G0 + 3, 0, bank[4:8], ab_tok, AB_W, 0)
            for o in range(1, 16, 2):
                half, t = o // 4 % 2, o % 4
                if o in (3, 7, 15):
                    dve.wait_ge(unit_used, used(u0 + AB_UP + min(o // 4, 2)))
                else:
                    dve.wait_ge(tok_done, 3 + (3 * (o // 4) + t if o < 8 else 6 + o - 8) + 1)
                dst = (q_tok[:, t, half * 384:half * 384 + 384] if o < 8 else
                       kv_tok[:, t, half * 512:half * 512 + 512])
                n_el = 384 if o < 8 else 512
                r = r_lat[:, t:t + 1] if o < 8 else r_lat[:, TT + t:TT + t + 1]
                dve.tensor_scalar(dst, bank[o % 8][:, 0:n_el], r, None, ALU.mult).then_inc(tok_dve, 1)
            for g in range(1, AB_GROUPS):
                if g == 1:
                    head_sums(SUMS_AT["mla"], mla_sums)
                    dve.wait_ge(hs_red, SUMS_AT["diff"])
                    dve.tensor_tensor(ss_k, ss_k, ss_kr[:, :, None].to_broadcast([P, TT, MLA_H]),
                                      ALU.add).then_inc(hs_keys, 1)
                    head_inverse(1, ss[:, 0:64])
                if g == 3:
                    head_sums(SUMS_AT["diff"], diff_sums)
                    head_inverse(2, ss[:, 68:196])
                copy_groups(u0 + AB_G1 + 4 * g - 1, 16 + 3 * (g - 1), bank[0:4] if g % 2 else bank[4:8],
                            ab_tok, AB_W, g)
            dve.wait_ge(tables_made, TABLES_AB)
            dve.wait_ge(hs_ready, 2)
            attention(Diff)
            od = ab_o[:, :, MLA_H * V_D:].rearrange("p t (h d) -> p t h d", d=V_D)
            dve.wait_ge(o_out, 2 + TT * DIFF_H)
            for t in range(TT):
                sq = tmp2[t % 2][:, 0:512].rearrange("p (h d) -> p h d", d=V_D)
                dve.tensor_tensor(sq, od[:, t], od[:, t], ALU.mult).then_inc(sub_step, 1)
                dve.wait_ge(sub_step, 2 * t + 1)
                dve.tensor_reduce(ss_o[:, t, :], sq, AX.X, ALU.add).then_inc(sub_step, 1)
                dve.wait_ge(sub_step, 2 * t + 2)
            dve.wait_ge(sub_std, 1)
            dve.reciprocal(ss[:, 196:228], ss[:, 196:228]).then_inc(sub_step, 1)
            dve.wait_ge(sub_step, 2 * TT + 1)
            for t in range(TT):
                dve.tensor_tensor(od[:, t], od[:, t], ss_o[:, t, :, None].to_broadcast([P, DIFF_H, V_D]),
                                  ALU.mult).then_inc(sub_step, 1)
            dve.wait_ge(sub_step, 3 * TT + 1)
            for t in range(TT):
                dve.tensor_tensor(od[:, t], od[:, t], subln[:, None, :].to_broadcast([P, DIFF_H, V_D]),
                                  ALU.mult).then_inc(sub_step, 1)
            attention(Mla)
            transposed_out(0)
            out_chunks(1, AB_AT + AB_OUT, 1, 1.0)

            ffn(1)
            out_chunks(2, FFN_AT[1] + 2 * FT, DOWN_U, 0.5)
            ffn(2)
            out_chunks(3, FFN_AT[2] + 2 * FT, DOWN_U, 0.5)

            token_stat(C_NORM)
            dve.wait_ge(rot_c_loaded, 32)
            for k, scale in enumerate((GQA_D ** -0.5, 1.0)):
                seg = rot_c[:, 1024 * k:1024 * k + 1024]
                dve.scalar_tensor_tensor(out=seg, in0=seg, scalar=scale, in1=hg[:, 1024 * k:1024 * k + 1024],
                                         op0=ALU.mult, op1=ALU.mult).then_inc(tables_made, 1)
            for g in range(C_GROUPS):
                copy_groups(C_AT + 4 * g + 3, AB_TOKS + 3 * g, c_b[g % 2], c_tok, C_W, g)
            head_sums(SUMS_AT["c"], c_sums)
            head_inverse(3, ss[:, 0:80])
            dve.wait_ge(tables_made, TABLES_AB + TABLES_C)
            dve.wait_ge(hs_ready, 3)
            attention(Gqa)
            transposed_out(KD)
            out_chunks(4, C_AT + C_OUT, 1, 1.0)

            ffn(3)
            out_chunks(5, FFN_AT[3] + 2 * FT, DOWN_U, 0.5, last=True)

        @block.tensor
        def _(pe):
            def product(dst, a_hi, a_lo, b_hi, b_lo, start, stop):
                pe.matmul(dst, a_lo, b_hi, start=start, stop=False)
                pe.matmul(dst, a_hi, b_lo, start=False, stop=False)
                return pe.matmul(dst, a_hi, b_hi, start=False, stop=stop)

            def feature_unit(dst, u, s, in_hi, in_lo, k0, nk, start, stop, before=None):
                pe.wait_ge(lo_ready, u + 1)
                for r in range(nk):
                    if before is not None:
                        before(k0 + r)
                    c = slice(r * P, (r + 1) * P)
                    last = product(dst, w_hi[s][:, c], w_lo[s][:, c], in_hi[:, k0 + r, :], in_lo[:, k0 + r, :],
                                   start and r == 0, stop and r == nk - 1)
                last.then_inc(unit_used, 1)

            def xg_wait(n):
                def before(k):
                    pe.wait_ge(xg_ready, KD * n + k + 1)
                return before

            def ffn_tile(c, u0, n, j, jj):
                p = jj % 2
                for half, (banks, read) in enumerate(((gate_b, gate_read), (up_b, up_read))):
                    pe.wait_ge(read, free(j + FT * c))
                    feature_unit(banks[p][:], j * 2 + (u0 + half), (u0 + 2 * jj + half) % RING, xg_hi, xg_lo, 0, KD,
                                 True, True, xg_wait(n) if jj == 0 and half == 0 else None)

            def ffn(c):
                u0, n = FFN_AT[c], FFN_NORM[c]
                ffn_tile(c, u0, n, 0, 0)
                pe.wait_ge(acc_done, KD * (n + 1))
                pe.matmul(stat_b[:], ones_d[:], acc[:], start=True, stop=True).then_inc(stat_done, 1)
                ffn_tile(c, u0, n, 1, 1)
                with pe.Fori(0, FT // 2 - 1) as i:
                    for jj in (2, 3):
                        ffn_tile(c, u0, n, i * 2 + jj, jj)

            def out_chunks(q, u0, per, in_hi, in_lo, n_in, before):
                with pe.Fori(0, KD // 4) as i:
                    for mm in range(4):
                        pe.wait_ge(x_new, free(i * 4 + (KD * q + mm)))
                        for r in range(per):
                            a = u0 + per * mm + r
                            feature_unit(y_b[mm % 2][:], i * (4 * per) + a, a % RING, in_hi, in_lo, r * KD,
                                         min(KD, n_in - r * KD), r == 0, r == per - 1, before if mm == 0 else None)

            def down(c, q):
                def before(k):
                    if k == 0:
                        pe.wait_ge(h_ready, FT * c + FT - 2)
                    if k >= FT - 2:
                        pe.wait_ge(h_ready, FT * c + k + 1)
                out_chunks(q, FFN_AT[c] + 2 * FT, DOWN_U, h_hi, h_lo, FT, before)

            def token_stat(n):
                pe.wait_ge(acc_done, KD * (n + 1))
                for t in range(TT):
                    last = pe.matmul(tok_stat_b[:, t:t + 1], acc[:, tok[t]], ones_d[:, 0:1], start=True, stop=True)
                last.then_inc(stat_done, 1)

            def token_group(u0, banks, width, n_unit=4, before=None):
                for kk in range(n_unit):
                    u = u0 + kk
                    s = u % RING
                    pe.wait_ge(lo_ready, u + 1)
                    if kk < n_unit - 1:
                        for r in range(2):
                            if before is not None:
                                before(2 * kk + r)
                            for t in range(TT):
                                w = slice(r * width, (r + 1) * width)
                                last = product(banks[t][:, 0:width], xg_hi[:, 2 * kk + r, tok[t]],
                                               xg_lo[:, 2 * kk + r, tok[t]], w_hi[s][:, w], w_lo[s][:, w],
                                               kk == 0 and r == 0, False)
                        last.then_inc(unit_used, 1)
                    else:
                        for t in range(TT):
                            for r in range(2):
                                if before is not None:
                                    before(2 * kk + r)
                                w = slice(r * width, (r + 1) * width)
                                last = product(banks[t][:, 0:width], xg_hi[:, 2 * kk + r, tok[t]],
                                               xg_lo[:, 2 * kk + r, tok[t]], w_hi[s][:, w], w_lo[s][:, w],
                                               False, r == 1)
                            last.then_inc(tok_done if t < TT - 1 else unit_used, 1)

            def attention(cfg):
                nb = TT * cfg.heads
                w, rows = cfg.width, cfg.rows

                def transposes(n):
                    pe.wait_ge(q_prep, n + (cfg.H0 + 1))
                    for k, (src, sem_) in enumerate(((qb, None), (kb, k_prep))):
                        if sem_ is not None:
                            pe.wait_ge(sem_, n + (cfg.H0 + 1))
                        apart(pe)
                        for t in range(TT):
                            last = pe.transpose(tr_b[k][0:w, tok[t]], src[:, t * w:(t + 1) * w], ident[:])
                        last.then_inc(tr_done, 1)

                def scores(n, bl):
                    for part in range(cfg.parts):
                        sat = score_at(cfg, n, bl, part)
                        s = bl % 2 if cfg.parts == 1 else part
                        at = (bl // TT + part) * rows
                        pe.wait_ge(p_done, free(sat))
                        pe.matmul(s_b[s][:], qT[at:at + rows, tok[bl % TT]], kT[at:at + rows, :],
                                  start=True, stop=True).then_inc(s_done, 1)

                def transpose_p(n, bl):
                    b = block_at(cfg, n, bl)
                    if cfg.parts == 2:
                        pe.wait_ge(w_done, n * nb + (bl + 1))
                    else:
                        pe.wait_ge(p_done, done(score_at(cfg, n, bl, 0)))
                    pe.wait_ge(pT_ready, free(b))
                    src = p_buf[:, bl % 2 if cfg.parts == 1 else 2 * (bl % 2), :]
                    for c in range(TT):
                        last = pe.transpose(pT_b[bl % 2][:, tok[c]], src[:, tok[c]], ident[:])
                    last.then_inc(pT_done, 1)

                def values(i, sub, n, bl):
                    b = block_at(cfg, n, bl)
                    pe.wait_ge(pT_ready, done(b))
                    pe.wait_ge(o_out, free(b))
                    for c in range(TT):
                        last = pe.matmul(o_b[bl % 2][:, 0:V_D], pT[:, bl % 2, tok[c]], cfg.v(i, sub, c),
                                         start=(c == 0), stop=(c == TT - 1))
                    last.then_inc(o_done, 1)

                def first_scores(n):
                    pe.wait_ge(qT_ready, n + (cfg.H0 + 1))
                    pe.wait_ge(kT_ready, n + (cfg.H0 + 1))
                    scores(n, 0)

                def pair(i, sub, n, has_next):
                    for bl in range(nb):
                        if bl + 1 < nb:
                            scores(n, bl + 1)
                        if bl == nb - 2 and has_next:
                            transposes(n + 1)
                        transpose_p(n, bl)
                        if bl > 0:
                            values(i, sub, n, bl - 1)
                    if has_next:
                        first_scores(n + 1)
                    values(i, sub, n, nb - 1)

                transposes(0)
                first_scores(0)
                each_pair(pe, cfg, pair)

            def transposed_out(base, o, blocks):
                pe.wait_ge(o_out, 2 + blocks)
                for k in range(KD):
                    if k >= 2:
                        pe.wait_ge(oT_ready, base + k - 1)
                    for t in range(TT):
                        last = pe.transpose(tr_b[k % 2][:, tok[t]], o[:, t, k * P:(k + 1) * P], ident[:])
                    last.then_inc(oT_done, 1)

            def out_proj(q, u0, base):
                def before(k):
                    pe.wait_ge(oT_ready, base + k + 1)
                out_chunks(q, u0, 1, oT_hi, oT_lo, KD, before)

            pe.sem_inc(unit_used, RING)
            for s in (gate_read, up_read, x_new, p_done, pT_done, pT_ready, o_done, o_out, tr_done):
                pe.sem_inc(s, 2)
            pe.wait_ge(consts_made, 6)

            ffn(0)
            down(0, 0)

            u0 = AB_AT
            for m in range(LATENT):
                feature_unit(bank[m][:], u0 + AB_LAT + m, (u0 + AB_LAT + m) % RING, xg_hi, xg_lo, 0, KD, True, True,
                             xg_wait(AB_NORM) if m == 0 else None)
                if m == 0:
                    token_stat(AB_NORM)
            token_group(u0 + AB_G0, bank[4:8], AB_W)
            pe.wait_ge(lat_hi_done, LATENT)
            pe.wait_ge(std_done, AB_NORM + 1)
            for t in range(TT):
                for m in range(2):
                    pe.matmul(tok_stat_b[:, TT + t:TT + t + 1], lat_sq[:, m, tok[t]], ones_lat[:, 0:1],
                              start=(m == 0), stop=(m == 1))
            for t in range(TT):
                last = pe.matmul(tok_stat_b[:, 2 * TT + t:2 * TT + t + 1], lat_sq[:, 2, tok[t]], ones_lat[:, 1:2],
                                 start=True, stop=True)
            last.then_inc(lat_stat, 1)
            pe.wait_ge(lat_ready, LATENT)
            pe.wait_ge(lat_step, 2)
            for o in range(16):
                half, t = o // 4 % 2, o % 4
                u = u0 + AB_UP + min(o // 4, 2)
                s = u % RING
                if o in (0, 4, 8):
                    pe.wait_ge(lo_ready, u + 1)
                if o == 4:
                    pe.wait_ge(tok_act, 2)
                    pe.wait_ge(tok_dve, 2)
                if o >= 8:
                    pe.wait_ge(tok_dve if o % 2 else tok_act, 2 + (o - 8) // 2 + 1)
                if o < 8:
                    for r in range(2):
                        w = slice(r * 384, (r + 1) * 384)
                        last = product(bank[o % 8][:, 0:384], lat_hi[:, r, tok[t]], lat_lo[:, r, tok[t]],
                                       w_hi[s][:, w], w_lo[s][:, w], r == 0, r == 1)
                else:
                    w = slice(half * 512, (half + 1) * 512)
                    last = product(bank[o % 8][:], lat_hi[:, 2, tok[t]], lat_lo[:, 2, tok[t]], w_hi[s][:, w],
                                   w_lo[s][:, w], True, True)
                last.then_inc(unit_used if o in (3, 7, 15) else tok_done, 1)
            for g in range(1, AB_GROUPS):
                pe.wait_ge(tok_act, 4 + 2 * g if g > 1 else 8)
                pe.wait_ge(tok_dve, 4 + 2 * g if g > 1 else 8)
                if g == 2:
                    pe.wait_ge(tok_act, 10)
                    pe.wait_ge(tok_dve, 10)
                if g == 3:
                    pe.wait_ge(tok_act, 12)
                    pe.wait_ge(tok_dve, 12)
                token_group(u0 + AB_G1 + 4 * (g - 1), bank[0:4] if g % 2 else bank[4:8], AB_W)
            pe.wait_ge(tok_act, AB_COPIES)
            pe.wait_ge(tok_dve, AB_COPIES)
            attention(Diff)
            attention(Mla)
            pe.wait_ge(sub_step, 4 * TT + 1)
            transposed_out(0, ab_o, TT * (DIFF_H + MLA_H))
            out_proj(1, AB_AT + AB_OUT, 0)

            ffn(1)
            down(1, 2)
            ffn(2)
            down(2, 3)

            for g in range(C_GROUPS):
                if g == 1:
                    pe.wait_ge(std_done, C_NORM + 1)
                if g == 2:
                    pe.wait_ge(tok_act, AB_COPIES + 2)
                    pe.wait_ge(tok_dve, AB_COPIES + 2)
                token_group(C_AT + 4 * g, c_b[g % 2], C_W,
                            before=xg_wait(C_NORM) if g == 0 else None)
                if g == 0:
                    token_stat(C_NORM)
            pe.wait_ge(tok_act, AB_COPIES + 2 * C_GROUPS)
            pe.wait_ge(tok_dve, AB_COPIES + 2 * C_GROUPS)
            attention(Gqa)
            transposed_out(KD, c_o, TT * (DIFF_H + MLA_H + GQA_H))
            out_proj(4, C_AT + C_OUT, KD)

            ffn(3)
            down(3, 5)


def units_of(w):
    k, n = w.shape[0] // P, w.shape[1] // P
    u = w.reshape(k, P, n, P).transpose(2, 1, 0, 3)
    pad = -k % KD
    u = np.pad(u, ((0, 0), (0, 0), (0, pad), (0, 0)))
    u = u.reshape(n, P, (k + pad) // KD, UNIT).transpose(0, 2, 1, 3)
    return u.reshape(-1, P, UNIT)


def wide_units(w, width, rows):
    k, n = w.shape[0] // P, w.shape[1] // width
    u = w.reshape(k // rows, rows, P, n, width).transpose(3, 0, 2, 1, 4).reshape(-1, P, rows * width)
    return np.pad(u, ((0, 0), (0, 0), (0, UNIT - rows * width)))


def rotary(pos, dim):
    inv = np.float32(THETA) ** (-np.arange(0, dim, 2, dtype=np.float32) / np.float32(dim))
    ang = pos.astype(np.float32)[:, None] * inv[None, :]
    return np.cos(ang).astype(np.float32), np.sin(ang).astype(np.float32)


def token_major(a):
    return a.reshape(TT, P, -1).transpose(1, 0, 2).reshape(P, -1)


def rotary_tables():
    cos, sin = rotary(np.arange(SEQ), ROPE)
    c32, s32 = np.concatenate([cos, cos], 1), np.concatenate([-sin, sin], 1)
    mla_c = np.concatenate([np.ones((SEQ, NOPE), np.float32), c32], 1)
    two_c, two_s = np.tile(c32, (1, 2)), np.tile(s32, (1, 2))
    parts = [mla_c, s32, mla_c, s32, two_c, two_s, two_c, two_s]
    even = np.concatenate([token_major(p) for p in parts], 1)
    row, col = np.arange(SEQ) // GRID_W, np.arange(SEQ) % GRID_W
    (rc, rs), (cc, cs) = rotary(row, GQA_D // 2), rotary(col, GQA_D // 2)
    ax_c = np.tile(np.concatenate([rc, rc, cc, cc], 1), (1, 2))
    ax_s = np.tile(np.concatenate([-rs, rs, -cs, cs], 1), (1, 2))
    odd = np.concatenate([token_major(p) for p in (ax_c, ax_s, ax_c, ax_s)], 1)
    return even, odd


def swapped(g):
    return g.reshape(-1, 2, 16)[:, ::-1].reshape(-1)


def spread(g):
    return token_major(np.broadcast_to(g, (SEQ, g.size)))


def kernel(**inputs):
    import concourse.bacc as _bacc
    from concourse.bass_utils import run_bass_kernel_spmd as _run

    a = {k: np.asarray(v) for k, v in inputs.items()}
    f = np.ascontiguousarray

    def ffn_units(which, i):
        gate, up = (units_of(a[f"{which}_w_{n}"][i]) for n in ("gate", "up"))
        both = np.stack([gate, up], 1).reshape(-1, P, UNIT)
        return [both, units_of(a[f"{which}_w_down"][i])]

    ab, latent = a["ab_w_in"][0], Q_RANK + KV_RANK
    groups = wide_units(ab[:, latent:], AB_W, 2)
    stream = ffn_units("ffn1", 0)
    stream += [units_of(ab[:, :latent]), groups[:4], wide_units(a["mla_w_uq"][0], 384, 2),
               wide_units(a["mla_w_ukv"][0], 1024, 1), groups[4:], units_of(a["ab_w_out"][0])]
    stream += ffn_units("ffn2", 0) + ffn_units("ffn1", 1)
    stream += [wide_units(a["c_w_in"][0], C_W, 2), units_of(a["c_w_out"][0])]
    stream += ffn_units("ffn2", 1)
    weights = np.concatenate(stream, 0)
    assert weights.shape[0] == N_UNITS

    def by_chunk(g):
        return g.reshape(-1, P).T

    norms = [a[n][i] for i in range(2) for n in ("ffn1_norm", "mix_norm", "ffn2_norm")]
    even, odd = rotary_tables()
    mq, mk, dq, dk = (a[n][0] for n in ("mla_q_norm", "mla_k_norm", "diff_q_norm", "diff_k_norm"))
    cq, ck = a["c_q_norm"][0], a["c_k_norm"][0]
    gains_even = [x for g in (mq, mk) for x in (spread(g), spread(swapped(g[NOPE:])))]
    gains_even += [x for g in (dq, dk) for x in (spread(np.tile(g, 2)), spread(np.tile(swapped(g), 2)))]
    gains_odd = [x for g in (cq, ck) for x in (spread(np.tile(g, 2)), spread(np.tile(swapped(g), 2)))]
    lams = np.stack([a[f"diff_lambda_{n}"][0] for n in ("q1", "k1", "q2", "k2")])
    arrays = {
        "in_x": f(a["x"][0].T.reshape(KD, P, SEQ).transpose(1, 0, 2)),
        "in_weights": weights,
        "in_gains": f(np.stack([by_chunk(g) for g in norms], 1)),
        "in_lat_gain": f(np.concatenate([by_chunk(a["mla_q_lora_norm"][0]), by_chunk(a["mla_kv_lora_norm"][0])], 1)),
        "in_rot": f(even),
        "in_head_gains": f(np.concatenate(gains_even, 1)),
        "in_rot_c": f(odd),
        "in_head_gains_c": f(np.concatenate(gains_odd, 1)),
        "in_lambdas": f(np.broadcast_to(lams, (P, 4, DIFF_D))),
        "in_subln": f(np.broadcast_to(a["diff_subln"][0], (P, V_D))),
    }
    nc = _bacc.Bacc("TRN2", target_bir_lowering=False, num_devices=1)
    args = [nc.dram_tensor(n, v.shape, F32, kind="ExternalInput").ap() for n, v in arrays.items()]
    args.append(nc.dram_tensor("out_x", (P, KD, SEQ), F32, kind="ExternalOutput").ap())
    build_kernel(nc, *args)
    r = _run(nc, [arrays], core_ids=[0])
    y = r.results[0]["out_x"]
    return np.ascontiguousarray(y.transpose(1, 0, 2).reshape(D_MODEL, SEQ).T)[None]
```

```python
import math
from contextlib import ExitStack

import numpy as np

import concourse.bass as bass
from concourse import mybir

P = 128
D_MODEL, SEQ, D_FF, GRID_W = 1024, 512, 2816, 64
THETA, EPS = 10000.0, 1e-6
KD = D_MODEL // P
FT = D_FF // P
TT = SEQ // P
MLA_H, NOPE, ROPE, V_D = 8, 64, 32, 64
QK_D = NOPE + ROPE
Q_RANK, KV_RANK = 256, 128
DIFF_H, DIFF_D = 8, 32
GQA_H, GQA_KV, GQA_D = 16, 4, 64
LAM_INIT = 0.8 - 0.6 * math.exp(-0.3 * 0)

UNIT = 1024
RING = 4
LEAD = 2
LATENT = (Q_RANK + KV_RANK) // P
AB_TOK = ROPE + 3 * DIFF_H * 2 * DIFF_D
AB_GROUPS, AB_W = 4, AB_TOK // 4
C_TOK = (GQA_H + 2 * GQA_KV) * GQA_D
C_GROUPS, C_W = 3, C_TOK // 3
C_ORDER = (2, 0, 1)
DQ0, DK0, DV0 = ROPE, ROPE + DIFF_H * 2 * DIFF_D, ROPE + 2 * DIFF_H * 2 * DIFF_D
CK0, CV0 = GQA_H * GQA_D, (GQA_H + GQA_KV) * GQA_D

DOWN_U = 3
FFN_UNITS = 2 * FT + DOWN_U * KD
AB_LAT, AB_G0 = 0, LATENT
AB_UP = AB_G0 + 4
AB_G1 = AB_UP + 3
AB_OUT = AB_G1 + 4 * (AB_GROUPS - 1)
AB_UNITS = AB_OUT + KD
C_OUT = 4 * C_GROUPS
C_UNITS = C_OUT + KD
FFN_AT = [0, FFN_UNITS + AB_UNITS, 2 * FFN_UNITS + AB_UNITS, 3 * FFN_UNITS + AB_UNITS + C_UNITS]
AB_AT = FFN_UNITS
C_AT = 3 * FFN_UNITS + AB_UNITS
N_UNITS = 4 * FFN_UNITS + AB_UNITS + C_UNITS
FFN_NORM = [0, 2, 3, 5]
AB_NORM, C_NORM = 1, 4

F32, F32R = mybir.dt.float32, mybir.dt.float32r
ALU = mybir.AluOpType
ACT = mybir.ActivationFunctionType
AX = mybir.AxisListType


def used(u):
    return RING + u + 1


def slot_free(u):
    return u + 1


def done(n):
    return n + 3


def free(n):
    return n + 1


def adone(n):
    return n + 5


def afree(n, ring):
    return n + (5 - ring)


def build_kernel(nc, x_in, weights, gains, lat_gain, rot_in, head_gains, rot_c_in, head_gains_c,
                 lam_in, subln_in, out):
    with ExitStack() as ctx:
        def sb(name, shape, dt=F32):
            return ctx.enter_context(nc.sbuf_tensor(name, shape, dt))

        def sem(name):
            return ctx.enter_context(nc.semaphore(name))

        def shared(*names_shapes):
            with ExitStack() as s:
                return [s.enter_context(nc.sbuf_tensor(n, sh, dt)) for n, sh, dt in names_shapes]

        x = sb("x", [P, KD, SEQ])
        stage = sb("stage", [P, RING, UNIT])
        w_hi = [sb(f"w_hi{s}", [P, UNIT], F32R) for s in range(RING)]
        w_lo = [sb(f"w_lo{s}", [P, UNIT], F32R) for s in range(RING)]
        tmp = sb("tmp", [P, 4, SEQ])
        acc = sb("acc", [P, SEQ])
        rstd = sb("rstd", [P, SEQ])
        ident = sb("ident", [P, P])
        ones_d = sb("ones_d", [P, P])
        ones_lat = sb("ones_lat", [P, 2])
        eps = sb("eps", [P, 1])
        gain = sb("gain", [P, 6, KD])
        lat_g = sb("lat_g", [P, LATENT])
        rot = sb("rot", [P, 2048])
        subln = sb("subln", [P, 1])
        lam = sb("lam", [P, 4])
        rtok = sb("rtok", [P, 4 * TT])
        ss = sb("ss", [P, 256])

        p_buf, pT, qT, kT, negmax, rowsum, rinv, ratio = shared(
            ("p_buf", [P, 4, SEQ], F32), ("pT", [P, 2, SEQ], F32), ("qT", [P, 4, SEQ], F32R),
            ("kT", [P, 4, SEQ], F32R), ("negmax", [P, 160], F32),
            ("rowsum", [P, 160], F32), ("rinv", [P, 160], F32), ("ratio", [P, 32], F32))
        _, qT_mla, kT_mla = shared(("below_qT", [P, 6, SEQ], F32), ("qT_mla", [P, 4, SEQ], F32),
                                   ("kT_mla", [P, 4, SEQ], F32))
        xg_hi = sb("xg_hi", [P, KD, SEQ], F32R)
        xg_lo = sb("xg_lo", [P, KD, SEQ], F32R)

        q_tok, kv_tok, ab_tok, ab_o, lat_hi, lat_lo, lat_sq = shared(
            ("q_tok", [P, TT, MLA_H * QK_D], F32), ("kv_tok", [P, TT, MLA_H * 128], F32),
            ("ab_tok", [P, TT, AB_TOK], F32), ("ab_o", [P, TT, D_MODEL], F32),
            ("lat_hi", [P, LATENT, SEQ], F32R), ("lat_lo", [P, LATENT, SEQ], F32R),
            ("lat_sq", [P, LATENT, SEQ], F32))
        oT_hi, oT_lo, c_tok, c_o, rot_c = shared(
            ("oT_hi", [P, KD, SEQ], F32R), ("oT_lo", [P, KD, SEQ], F32R),
            ("c_tok", [P, TT, C_TOK], F32), ("c_o", [P, TT, D_MODEL], F32), ("rot_c", [P, 1536], F32))
        hg, lam_v, lam_p = shared(("hg", [P, 2048], F32), ("lam_v", [P, 4, DIFF_D], F32),
                                  ("lam_p", [P, 2, DIFF_D], F32))
        _, sq_room = shared(("below_oT_lo", [P, KD * SEQ], F32), ("sq_room", [P, 4, 1024], F32))
        _, qa, qd, ka, kd = shared(("below", [P, 2 * KD * SEQ + TT * (C_TOK + D_MODEL) + 2048], F32),
                                   ("qa", [P, SEQ], F32), ("qd", [P, SEQ], F32), ("ka", [P, SEQ], F32),
                                   ("kd", [P, SEQ], F32))
        h_hi = sb("h_hi", [P, FT, SEQ], F32R)
        h_lo = sb("h_lo", [P, FT, SEQ], F32R)

        bank = [ctx.enter_context(nc.psum_tensor(f"bank{b}", [P, 512], F32)) for b in range(8)]
        gate_b, up_b, y_b, stat_b = bank[0:2], bank[2:4], bank[4:6], bank[6]
        tok_stat_b = bank[3]
        c_b = [[bank[0], bank[1], bank[2], bank[6]], [bank[4], bank[5], bank[7], bank[3]]]
        s_b, pT_b, o_b, tr_b = bank[0:4], bank[4:6], bank[6], bank[7]
        oT_b = bank[0:2]

        landed = [sem(f"landed{s}") for s in range(RING)]
        hi_ready = sem("hi_ready")
        lo_ready = sem("lo_ready")
        unit_used = sem("unit_used")
        x_loaded = [sem(f"x_loaded{k}") for k in range(4)]
        gains_loaded = sem("gains_loaded")
        consts_loaded = sem("consts_loaded")
        rot_c_loaded = sem("rot_c_loaded")
        consts_made = sem("consts_made")
        tables_made = sem("tables_made")
        lam_step = sem("lam_step")
        lam_exp = sem("lam_exp")
        xg_hi_done = sem("xg_hi_done")
        xg_ready = sem("xg_ready")
        sq_done = sem("sq_done")
        acc_zero = sem("acc_zero")
        acc_done = sem("acc_done")
        stat_done = sem("stat_done")
        std_done = sem("std_done")
        rstd_ready = sem("rstd_ready")
        gate_read = sem("gate_read")
        up_read = sem("up_read")
        silu_done = sem("silu_done")
        h_raw = sem("h_raw")
        h_hi_done = sem("h_hi_done")
        h_ready = sem("h_ready")
        x_new = sem("x_new")
        stored = sem("stored")
        waits_taken = sem("waits_taken")
        lat_hi_done = sem("lat_hi_done")
        lat_ready = sem("lat_ready")
        lat_stat = sem("lat_stat")
        lat_step = sem("lat_step")
        lat_std = sem("lat_std")
        tok_done = sem("tok_done")
        tok_act = sem("tok_act")
        tok_dve = sem("tok_dve")
        hs_sq = sem("hs_sq")
        hs_red = sem("hs_red")
        hs_keys = sem("hs_keys")
        hs_std = sem("hs_std")
        hs_ready = sem("hs_ready")
        q_step = sem("q_step")
        q_prep = sem("q_prep")
        k_step = sem("k_step")
        k_prep = sem("k_prep")
        pads_zero = sem("pads_zero")
        tr_done = sem("tr_done")
        tr_act = sem("tr_act")
        tr_dve = sem("tr_dve")
        s_done = sem("s_done")
        max_done = sem("max_done")
        p_done = sem("p_done")
        r_diff = sem("r_diff")
        ratio_done = sem("ratio_done")
        w_done = sem("w_done")
        pT_done = sem("pT_done")
        pT_ready = sem("pT_ready")
        o_done = sem("o_done")
        r_done = sem("r_done")
        o_out = sem("o_out")
        sub_sq = sem("sub_sq")
        sub_sum = sem("sub_sum")
        sub_inv = sem("sub_inv")
        sub_done = sem("sub_done")
        sub_std = sem("sub_std")
        oT_done = sem("oT_done")
        oT_hi_done = sem("oT_hi_done")
        oT_ready = sem("oT_ready")

        block = ctx.enter_context(nc.Block())

        tok = [slice(t * P, (t + 1) * P) for t in range(TT)]
        rstd_tok, rstd_sq = rtok[:, 0:4], rtok[:, 4:8]
        r_lat = rtok[:, 8:16]
        ss_q = ss[:, 0:32].rearrange("p (t h) -> p t h", t=TT)
        ss_k = ss[:, 32:64].rearrange("p (t h) -> p t h", t=TT)
        ss_kr = ss[:, 64:68]
        ss_d = ss[:, 68:196].rearrange("p (t h) -> p t h", t=TT)
        ss_c = ss[:, 0:80].rearrange("p (t h) -> p t h", t=TT)
        ss_o = ss[:, 196:228].rearrange("p (t h) -> p t h", t=TT)
        qb, kb = (tmp[:, k:k + 2, :].rearrange("p a n -> p (a n)") for k in (0, 2))
        qb_r, kb_r = qb.bitcast(F32R), kb.bitcast(F32R)
        qc, kc = acc, rstd
        sq_ab = [ab_o[:, k, :] for k in range(4)]
        sq_c = [sq_room[:, k, :] for k in range(4)]

        def tables(src, specs):
            got, at = [], 0
            for n in specs:
                got.append(src[:, at:at + n])
                at += n
            return got

        m_cq, m_sq, m_ck, m_sk, d_cq, d_sq, d_ck, d_sk = tables(rot, [384, 128, 384, 128, 256, 256, 256, 256])
        c_cq, c_sq, c_ck, c_sk = tables(rot_c, [512, 512, 256, 256])

        class Diff:
            parts, heads, steps, q_steps = 2, 1, 4, 2
            S0, B0, H0, T0 = 0, 0, 0, 0

            @staticmethod
            def v(i, sub, c):
                return ab_tok[:, c, bass.ds(i * (2 * V_D) + (DV0 + sub * V_D), V_D)]

            @staticmethod
            def o_at(i, sub, a, t):
                return ab_o[:, t, bass.ds(i * (2 * V_D) + ((MLA_H + sub) * V_D), V_D)]

        class Mla:
            parts, heads, steps, q_steps = 1, 1, 2, 1
            S0, B0, H0, T0 = 2 * TT * DIFF_H, TT * DIFF_H, DIFF_H, 4 * DIFF_H

            @staticmethod
            def v(i, sub, c):
                return kv_tok[:, c, bass.ds(i * 256 + (sub * 128 + NOPE), V_D)]

            @staticmethod
            def o_at(i, sub, a, t):
                return ab_o[:, t, bass.ds(i * (2 * V_D) + sub * V_D, V_D)]

        class Gqa:
            parts, heads, steps, q_steps = 1, 2, 4, 2
            S0 = 2 * TT * DIFF_H + TT * MLA_H
            B0, H0, T0 = TT * (DIFF_H + MLA_H), DIFF_H + MLA_H, 4 * DIFF_H + 2 * MLA_H

            @staticmethod
            def v(i, sub, c):
                return c_tok[:, c, bass.ds(i * V_D + CV0, V_D)]

            @staticmethod
            def o_at(i, sub, a, t):
                return c_o[:, t, bass.ds(i * (4 * GQA_D) + (2 * sub + a) * GQA_D, V_D)]

        ITERS = 4

        def apart(eng):
            eng.sem_inc(waits_taken, 1)

        def block_at(cfg, n, bl):
            return n * (TT * cfg.heads) + (cfg.B0 + bl)

        def score_at(cfg, n, bl, part):
            return n * (TT * cfg.heads * cfg.parts) + (cfg.S0 + bl * cfg.parts + part)

        def pair_at(i, sub, ahead):
            return (i + (sub + ahead) // 2, (sub + ahead) % 2)

        def each_pair(eng, body, peel=False):
            if peel:
                for sub in range(2):
                    body(0, sub, sub, 2)
            with eng.Fori(1 if peel else 0, ITERS - 1) as i:
                for sub in range(2):
                    body(i, sub, i * 2 + sub, 2)
            for sub in range(2):
                body(ITERS - 1, sub, (ITERS - 1) * 2 + sub, 1 - sub)

        def tr_step(cfg, n, k):
            return n * cfg.steps + (4 + cfg.T0 + k + 1)

        def act_copied(cfg, n, k):
            return n * (cfg.steps - 1) + (cfg.T0 - cfg.H0 + k)

        def parts_of(cfg, keys):
            d = kd if keys else qd
            w = DIFF_D if cfg is Diff else GQA_D
            n_el = TT * GQA_D * (2 if cfg is Gqa and not keys else 1)
            full = d[:, 0:n_el].rearrange("p (g d) -> p g d", d=w)
            b_r = kb_r if keys else qb_r
            if cfg is Diff and not keys:
                parts = b_r.rearrange("p (g c h d) -> p g c h d", c=2, h=2, d=w)
                hi, lo = parts[:, :, :, 0, :], parts[:, :, :, 1, :]
            elif cfg is Diff:
                parts = b_r.rearrange("p (g h c d) -> p g h c d", c=2, h=2, d=w)
                hi, lo = parts[:, :, 0, :, :], parts[:, :, 1, :, :]
            elif keys:
                parts = b_r.rearrange("p (h g c d) -> p h g c d", c=2, h=2, d=w)
                hi, lo = parts[:, 0, :, :, :], parts[:, 1, :, :, :]
            else:
                parts = b_r.rearrange("p (g h d) -> p g h d", h=2, d=w)
                hi, lo = parts[:, :, 0, :], parts[:, :, 1, :]
            if len(hi.shape) == 4:
                full = full[:, :, None, :].to_broadcast(list(hi.shape))
            return full, hi, lo

        def parts_free(eng, cfg, keys, n):
            eng.wait_ge(tr_done, tr_step(cfg, n - 1, cfg.steps - 1 if keys else cfg.q_steps - 1))
            apart(eng)

        def prepare(eng, cfg, keys, i, sub, n, stages):
            a, b, c = (ka, kb, kc) if keys else (qa, qb, qc)
            d = kd if keys else qd
            step_sem, out_sem = (k_step, k_prep) if keys else (q_step, q_prep)
            steps = 2 if cfg is Mla else 4
            step0 = 4 * cfg.H0 if cfg is not Gqa else 4 * DIFF_H + 2 * MLA_H

            def stepped(k):
                eng.wait_ge(step_sem, n * steps + (step0 + k))

            if cfg is Mla:
                n_el, cos, sin = TT * QK_D, m_ck if keys else m_cq, m_sk if keys else m_sq
                a3 = a[:, 0:n_el].rearrange("p (t d) -> p t d", t=TT)
                b3 = b[:, 0:SEQ].rearrange("p (t d) -> p t d", t=TT)[:, :, 0:QK_D]
                a_rot, b_rot = a3[:, :, NOPE:QK_D], b3[:, :, NOPE:QK_D]
            else:
                if cfg is Diff:
                    n_el, cos, sin = TT * 2 * DIFF_D, d_ck if keys else d_cq, d_sk if keys else d_sq
                elif keys:
                    n_el, cos, sin = TT * GQA_D, c_ck, c_sk
                else:
                    n_el, cos, sin = TT * 2 * GQA_D, c_cq, c_sq
                a_rot = a[:, 0:n_el].rearrange("p (g d) -> p g d", d=32)
                b_rot = d[:, 0:n_el].rearrange("p (g d) -> p g d", d=32)
            s3 = sin.rearrange("p (g d) -> p g d", d=32)
            c3 = c[:, 0:s3.shape[1] * 32].rearrange("p (g d) -> p g d", d=32)

            if 0 in stages:
                if cfg is Mla:
                    eng.wait_ge(tr_done, tr_step(cfg, n - 1, 1 if keys else 0))
                    apart(eng)
                if cfg is Mla and keys:
                    r = ss_k[:, :, bass.ds(i * 2 + sub, 1)]
                    eng.tensor_tensor(a3[:, :, 0:NOPE], kv_tok[:, :, bass.ds(i * 256 + sub * 128, NOPE)],
                                      r.to_broadcast([P, TT, NOPE]), ALU.mult)
                    eng.tensor_tensor(a3[:, :, NOPE:QK_D], ab_tok[:, :, 0:ROPE], r.to_broadcast([P, TT, ROPE]),
                                      ALU.mult).then_inc(step_sem, 1)
                elif cfg is Mla:
                    eng.tensor_tensor(a3, q_tok[:, :, bass.ds(i * (2 * QK_D) + sub * QK_D, QK_D)],
                                      ss_q[:, :, bass.ds(i * 2 + sub, 1)].to_broadcast([P, TT, QK_D]),
                                      ALU.mult).then_inc(step_sem, 1)
                else:
                    if cfg is Diff:
                        src = ab_tok[:, :, bass.ds(i * 128 + (sub * 64 + (DK0 if keys else DQ0)), 64)].rearrange(
                            "p t (e d) -> p t e d", e=2)
                        r = ss_d[:, :, bass.ds(i * 4 + (sub * 2 + (16 if keys else 0)), 2), None]
                    elif keys:
                        src = c_tok[:, :, None, bass.ds(i * GQA_D + CK0, GQA_D)]
                        r = ss_c[:, :, bass.ds(i + GQA_H, 1), None]
                    else:
                        src = c_tok[:, :, bass.ds(i * 256 + sub * 128, 128)].rearrange("p t (e d) -> p t e d", e=2)
                        r = ss_c[:, :, bass.ds(i * 4 + sub * 2, 2), None]
                    eng.tensor_tensor(a[:, 0:n_el].rearrange("p (t e d) -> p t e d", t=TT, e=src.shape[2]), src,
                                      r.to_broadcast(list(src.shape)), ALU.mult).then_inc(step_sem, 1)
            if 1 in stages:
                stepped(1)
                if cfg is Mla:
                    eng.tensor_tensor(b3, a3, cos.rearrange("p (t d) -> p t d", t=TT), ALU.mult)
                else:
                    eng.tensor_tensor(d[:, 0:n_el], a[:, 0:n_el], cos, ALU.mult)
            if 2 in stages:
                eng.tensor_tensor(c3[:, :, 0:16], a_rot[:, :, 16:32], s3[:, :, 0:16], ALU.mult)
                eng.tensor_tensor(c3[:, :, 16:32], a_rot[:, :, 0:16], s3[:, :, 16:32],
                                  ALU.mult).then_inc(step_sem, 1)
            if 3 in stages:
                stepped(2)
                eng.tensor_tensor(b_rot, b_rot, c3, ALU.add).then_inc(out_sem if cfg is Mla else step_sem, 1)
            if cfg is not Mla:
                full, hi, lo = parts_of(cfg, keys)
                if 4 in stages:
                    stepped(3)
                    parts_free(eng, cfg, keys, n)
                    eng.tensor_copy(hi, full).then_inc(step_sem, 1)
                if 5 in stages:
                    stepped(4)
                    eng.tensor_tensor(lo, full, hi.bitcast(F32), ALU.subtract).then_inc(out_sem, 1)

        EVERY = range(6)

        def heads(v, d):
            return v.rearrange("p t (h d) -> p t h d", d=d)

        mla_sums = [(ab_tok[:, :, None, 0:ROPE], ss_kr[:, :, None])]
        mla_sums += [(heads(q_tok[:, t:t + 1, :], QK_D), ss_q[:, t:t + 1, :]) for t in range(TT)]
        mla_sums += [(heads(kv_tok[:, t:t + 2, :], 128)[:, :, :, 0:NOPE], ss_k[:, t:t + 2, :]) for t in (0, 2)]
        diff_sums = [(heads(ab_tok[:, t:t + 1, DQ0:DV0], DIFF_D), ss_d[:, t:t + 1, :]) for t in range(TT)]
        c_sums = [[(heads(c_tok[:, :, CK0:CV0], GQA_D), ss_c[:, :, GQA_H:])]]
        c_sums += [[(heads(c_tok[:, t:t + 2, g * C_W:(g + 1) * C_W], GQA_D), ss_c[:, t:t + 2, g * 8:g * 8 + 8])
                    for t in (0, 2)] for g in range(2)]
        MLA_SUMS, DIFF_SUMS = len(mla_sums), len(mla_sums) + len(diff_sums)
        C_SUMS = [DIFF_SUMS, DIFF_SUMS + 1, DIFF_SUMS + 3, DIFF_SUMS + 5]

        def squares(at, src):
            t, h, d = src.shape[1:]
            return (sq_ab if at < DIFF_SUMS else sq_c)[at % 4][:, 0:t * h * d].rearrange("p (t h d) -> p t h d", h=h, d=d)

        TABLES_AB, TABLES_C = 6, 2
        AB_COPIES, AB_TOKS = 2 * AB_GROUPS + 8, 3 * AB_GROUPS + 6 + 7

        @block.sync
        def _(sp):
            for dst, src in ((gain, gains), (lat_g, lat_gain)):
                sp.dma_start(dst[:], src).then_inc(gains_loaded, 16)
            for k in range(4):
                sp.dma_start(x[:, 2 * k:2 * k + 2, :], x_in[:, 2 * k:2 * k + 2, :]).then_inc(x_loaded[k], 16)
                sp.dma_start(stage[:, k, :], weights[k]).then_inc(landed[k], 16)
            for dst, src in ((rot, rot_in), (hg, head_gains), (lam_v, lam_in), (subln, subln_in)):
                sp.dma_start(dst[:], src).then_inc(consts_loaded, 16)
            with sp.Fori(1, N_UNITS // RING) as i:
                for s in range(RING):
                    sp.wait_ge(lo_ready, i * RING + (s - RING + 1))
                    sp.dma_start(stage[:, s, :], weights[i * RING + s]).then_inc(landed[s], 16)
            for u in range(N_UNITS // RING * RING, N_UNITS):
                sp.wait_ge(lo_ready, u - RING + 1)
                sp.dma_start(stage[:, u % RING, :], weights[u]).then_inc(landed[u % RING], 16)
            for m in range(KD):
                sp.wait_ge(x_new, done(5 * KD + m))
                sp.dma_start(out[:, m, :], x[:, m, :]).then_inc(stored, 16)
            sp.wait_ge(stored, 16 * KD)

        @block.gpsimd
        def _(pool):
            def split_lo(u, s):
                pool.wait_ge(hi_ready, u + 1)
                pool.tensor_tensor(w_lo[s][:], stage[:, s, :], w_hi[s][:].bitcast(F32),
                                   ALU.subtract).then_inc(lo_ready, 1)

            def split_range(a, b):
                n = (b - a) // RING
                if n > 1:
                    with pool.Fori(0, n) as i:
                        for s in range(RING):
                            split_lo(i * RING + (a + s), (a + s) % RING)
                    a += n * RING
                for u in range(a, b):
                    split_lo(u, u % RING)

            pool.memset(ident[:], 0.0).then_inc(consts_made, 1)
            pool.wait_ge(consts_made, 1)
            pool.affine_select(out=ident[:], in_=ident[:], compare_op=ALU.not_equal, fill=1.0, base=0,
                               pattern=[[-1, P]], channel_multiplier=1).then_inc(consts_made, 1)
            pool.memset(ones_d[:], 1.0 / D_MODEL).then_inc(consts_made, 1)
            pool.memset(ones_lat[:, 0:1], 1.0 / Q_RANK).then_inc(consts_made, 1)
            pool.memset(ones_lat[:, 1:2], 1.0 / KV_RANK).then_inc(consts_made, 1)
            pool.memset(eps[:], EPS).then_inc(consts_made, 1)

            def all_keys(cfg, first=0, end=ITERS):
                with pool.Fori(first, end) as i:
                    for sub in range(2):
                        n = i * 2 + sub
                        if cfg is Diff:
                            for stages in (range(4), (5,)):
                                prepare(pool, cfg, False, i, sub, n, stages)
                                prepare(pool, cfg, True, i, sub, n, stages)
                        else:
                            prepare(pool, cfg, True, i, sub, n, EVERY)

            split_range(0, AB_AT + AB_OUT + LEAD)
            pool.wait_ge(tables_made, TABLES_AB)
            pool.wait_ge(hs_ready, 2)
            all_keys(Diff)
            pool.wait_ge(tr_done, tr_step(Diff, 2 * ITERS - 1, 3))
            pool.memset(kb[:, 0:SEQ].rearrange("p (t d) -> p t d", t=TT)[:, :, QK_D:P], 0.0).then_inc(pads_zero, 1)
            all_keys(Mla)
            pool.wait_ge(o_out, adone(TT * DIFF_H - 1))
            for t in range(TT):
                od = ab_o[:, t, MLA_H * V_D:]
                pool.tensor_tensor(ab_tok[:, t, DQ0:DK0], od, od, ALU.mult).then_inc(sub_sq, 1)
            split_range(AB_AT + AB_OUT + LEAD, C_AT + C_OUT + LEAD)
            pool.wait_ge(tables_made, TABLES_AB + TABLES_C)
            pool.wait_ge(hs_ready, 3)
            all_keys(Gqa)
            split_range(C_AT + C_OUT + LEAD, N_UNITS)

        @block.scalar
        def _(act):
            def split_hi(a, i=0, step=0):
                s = a % RING
                act.wait_ge(landed[s], i * (16 * step // RING) + 16 * (a // RING + 1))
                act.wait_ge(unit_used, slot_free(i * step + a))
                act.activation(w_hi[s][:], stage[:, s, :], ACT.Copy).then_inc(hi_ready, 1)

            def ffn_tile(c, u0, n, j, jj, i=0):
                p = jj % 2
                split_hi(u0 + 2 * jj + LEAD, i, 4)
                split_hi(u0 + 2 * jj + LEAD + 1, i, 4)
                if jj == 0:
                    act.wait_ge(stat_done, n + 1)
                    act.activation(rstd[:], stat_b[:], ACT.Sqrt, bias=eps[:]).then_inc(std_done, 1)
                act.wait_ge(gate_read, done(j + FT * c))
                act.activation(tmp[:, p, :], tmp[:, p, :], ACT.Silu).then_inc(silu_done, 1)
                act.wait_ge(h_raw, j + (FT * c + 1))
                apart(act)
                act.activation(h_hi[:, j, :] if isinstance(j, int) else h_hi[:, bass.ds(j, 1), :].rearrange("p a n -> p (a n)"),
                               tmp[:, 2 + p, :], ACT.Copy).then_inc(h_hi_done, 1)

            def ffn(c):
                u0, n = FFN_AT[c], FFN_NORM[c]
                ffn_tile(c, u0, n, 0, 0)
                ffn_tile(c, u0, n, 1, 1)
                with act.Fori(0, FT // 2 - 1) as i:
                    for jj in (2, 3):
                        ffn_tile(c, u0, n, i * 2 + jj, jj, i)

            def out_chunks(q, u0, per):
                n = q + 1
                with act.Fori(0, KD // 4) as i:
                    for mm in range(4):
                        m = i * 4 + mm
                        for r in range(per):
                            split_hi(u0 + per * mm + r + LEAD, i, 4 * per)
                        act.wait_ge(x_new, done(m + KD * q))
                        apart(act)
                        act.activation(xg_hi[:, bass.ds(m, 1), :].rearrange("p a n -> p (a n)"),
                                       x[:, bass.ds(m, 1), :].rearrange("p a n -> p (a n)"), ACT.Copy,
                                       scale=gain[:, n, bass.ds(m, 1)]).then_inc(xg_hi_done, 1)
                        act.wait_ge(acc_done, m + (KD * n - 1))
                        apart(act)
                        act.activation(tmp[:, mm % 2, :], x[:, bass.ds(m, 1), :].rearrange("p a n -> p (a n)"),
                                       ACT.Square).then_inc(sq_done, 1)

            def token_stat(n):
                act.wait_ge(stat_done, n + 1)
                act.activation(rstd_tok, tok_stat_b[:, 0:TT], ACT.Sqrt, bias=eps[:]).then_inc(std_done, 1)

            def copy_groups(u, toks, banks, dst, width, g):
                for t in (0, 2):
                    act.wait_ge(tok_done, toks + t + 1)
                    act.activation(dst[:, t, g * width:(g + 1) * width], banks[t][:, 0:width], ACT.Copy,
                                   scale=rstd_tok[:, t:t + 1]).then_inc(tok_act, 1)

            def head_squares(at, sums):
                for k, (src, _) in enumerate(sums):
                    if at + k >= 4:
                        act.wait_ge(hs_red, at + k - 3)
                    act.activation(squares(at + k, src), src, ACT.Square).then_inc(hs_sq, 1)

            def head_roots(at, views, d):
                act.wait_ge(hs_red, at)
                for v in views:
                    last = act.activation(v, v, ACT.Sqrt, scale=1.0 / d, bias=eps[:])
                last.then_inc(hs_std, 1)

            def attention(cfg, late=None):
                nb = TT * cfg.heads

                def copy_operand(n, sub, k):
                    act.wait_ge(tr_done, tr_step(cfg, n, k))
                    if cfg is Mla:
                        dst = qT_mla[:, 2 * sub, :]
                    else:
                        dst = (qT[:, 2 * sub + k, :] if k < cfg.q_steps else
                               kT[:, 2 * sub + k - cfg.q_steps, :])
                    act.activation(dst, tr_b[:], ACT.Copy).then_inc(tr_act, 1)

                def hi_parts(n, keys):
                    full, hi, _ = parts_of(cfg, keys)
                    step_sem = k_step if keys else q_step
                    act.wait_ge(step_sem, n * 4 + 3)
                    parts_free(act, cfg, keys, n)
                    act.activation(hi, full, ACT.Copy).then_inc(step_sem, 1)

                def exps(n, bl):
                    for part in range(cfg.parts):
                        sat = score_at(cfg, n, bl, part)
                        slot = bl % 4 if cfg.parts == 1 else 2 * (bl % 2) + part
                        act.wait_ge(max_done, sat + 1)
                        act.wait_ge(pT_done, afree(block_at(cfg, n, bl), 4 // cfg.parts))
                        apart(act)
                        act.activation(p_buf[:, slot, :], s_b[slot][:], ACT.Exp, bias=negmax[:, bass.ds(sat, 1)],
                                       accum_out=rowsum[:, bass.ds(sat, 1)]).then_inc(p_done, 1)

                def copy_pT(n, bl):
                    b = block_at(cfg, n, bl)
                    act.wait_ge(pT_done, adone(b))
                    act.wait_ge(o_done, afree(b, 2))
                    act.activation(pT[:, bl % 2, :], pT_b[bl % 2][:], ACT.Copy).then_inc(pT_ready, 1)

                def pair(i, sub, n, ahead):
                    for bl in range(nb):
                        if bl + 1 < nb:
                            exps(n, bl + 1)
                        elif ahead:
                            exps(n + 1, 0)
                        if bl == 0 and ahead:
                            copy_operand(n + 1, 1 - sub, 0)
                        if bl == 1 and ahead and cfg.steps == 4:
                            copy_operand(n + 1, 1 - sub, 2)
                        copy_pT(n, bl)
                        if bl == 0 and ahead and cfg.steps == 4:
                            copy_operand(n + 1, 1 - sub, 1)
                        if cfg is Diff and ahead == 2 and bl in (1, 2):
                            hi_parts(n + 2, keys=(bl == 2))

                if cfg is Diff:
                    hi_parts(0, False)
                    hi_parts(0, True)
                for k in range(cfg.steps - 1):
                    copy_operand(0, 0, k)
                exps(0, 0)
                if cfg is Diff:
                    hi_parts(1, False)
                    hi_parts(1, True)
                if late is not None:
                    late()
                each_pair(act, pair)

            def transposed_out(base, scales):
                for k in range(KD):
                    act.wait_ge(oT_done, base + k + 1)
                    act.activation(oT_hi[:, k, :], oT_b[k % 2][:], ACT.Copy, scale=scales[k]).then_inc(oT_hi_done, 1)

            act.wait_ge(gains_loaded, 16 * 2)
            act.wait_ge(consts_made, 6)
            for m in range(KD):
                if m % 2 == 0:
                    act.wait_ge(x_loaded[m // 2], 16)
                    if m // 2 < LEAD:
                        split_hi(m // 2)
                act.activation(xg_hi[:, m, :], x[:, m, :], ACT.Copy,
                               scale=gain[:, 0, m:m + 1]).then_inc(xg_hi_done, 1)
                if m >= 2:
                    act.wait_ge(acc_done, m - 1)
                act.activation(tmp[:, m % 2, :], x[:, m, :], ACT.Square).then_inc(sq_done, 1)
            act.wait_ge(lam_step, 2)
            act.activation(lam[:, 2:4], lam[:, 0:2], ACT.Exp).then_inc(lam_exp, 1)

            ffn(0)
            out_chunks(0, FFN_AT[0] + 2 * FT, DOWN_U)

            u0 = AB_AT
            for m in range(LATENT):
                split_hi(u0 + AB_LAT + m + LEAD)
                if m == 1:
                    token_stat(AB_NORM)
                act.wait_ge(unit_used, used(u0 + AB_LAT + m))
                act.activation(lat_hi[:, m, :], bank[m][:], ACT.Copy, scale=lat_g[:, m:m + 1])
                act.activation(lat_sq[:, m, :], bank[m][:], ACT.Square).then_inc(lat_hi_done, 1)
            for k in range(4):
                split_hi(u0 + AB_G0 + k + LEAD)
            act.wait_ge(lat_step, 2)
            act.activation(r_lat, r_lat, ACT.Sqrt, bias=eps[:]).then_inc(lat_std, 1)
            act.wait_ge(rstd_ready, AB_NORM + 1)
            copy_groups(u0 + AB_G0 + 3, 0, bank[4:8], ab_tok, AB_W, 0)
            act.wait_ge(lat_step, 4)
            for o in range(16):
                if o in (0, 4, 8):
                    split_hi(u0 + AB_UP + min(o // 4, 2) + LEAD)
                if o % 2:
                    continue
                half, t = o // 4 % 2, o % 4
                act.wait_ge(tok_done, 3 + (3 * (o // 4) + t if o < 8 else 6 + o - 8) + 1)
                dst = (q_tok[:, t, half * 384:half * 384 + 384] if o < 8 else
                       kv_tok[:, t, half * 512:half * 512 + 512])
                n_el = 384 if o < 8 else 512
                r = r_lat[:, t:t + 1] if o < 8 else r_lat[:, TT + t:TT + t + 1]
                act.activation(dst, bank[o % 8][:, 0:n_el], ACT.Copy, scale=r).then_inc(tok_act, 1)
            for g in range(1, AB_GROUPS):
                for k in range(4):
                    split_hi(u0 + AB_G1 + 4 * (g - 1) + k + LEAD)
                    if g == 3 and k == 0:
                        act.wait_ge(tok_dve, 14)
                        act.wait_ge(tok_act, 14)
                        head_squares(MLA_SUMS, diff_sums)
                    if g == 3 and k == 1:
                        head_roots(DIFF_SUMS, [ss[:, 68:196]], DIFF_D)
                if g == 1:
                    act.wait_ge(tok_dve, 10)
                    act.wait_ge(tok_act, 10)
                    head_squares(0, mla_sums)
                    act.wait_ge(hs_keys, 1)
                    head_roots(MLA_SUMS, [ss[:, 0:64]], QK_D)
                copy_groups(u0 + AB_G1 + 4 * g - 1, 16 + 3 * (g - 1), bank[0:4] if g % 2 else bank[4:8],
                            ab_tok, AB_W, g)
            attention(Diff)
            attention(Mla)
            act.wait_ge(sub_sum, 1)
            act.activation(ss[:, 196:228], ss[:, 196:228], ACT.Sqrt, scale=1.0 / V_D,
                           bias=eps[:]).then_inc(sub_std, 1)
            transposed_out(0, [1.0] * 4 + [subln[:, 0:1]] * 4)
            out_chunks(1, AB_AT + AB_OUT, 1)

            ffn(1)
            out_chunks(2, FFN_AT[1] + 2 * FT, DOWN_U)
            ffn(2)
            out_chunks(3, FFN_AT[2] + 2 * FT, DOWN_U)

            def group_squares(g):
                act.wait_ge(tok_dve, AB_COPIES + 2 * g + 2)
                act.wait_ge(tok_act, AB_COPIES + 2 * g + 2)
                head_squares(C_SUMS[g], c_sums[g])

            def last_heads():
                group_squares(2)
                head_roots(C_SUMS[3], [ss_c[:, :, 8:GQA_H]], GQA_D)

            act.dma_start(rot_c[:], rot_c_in).then_inc(rot_c_loaded, 16)
            act.dma_start(hg[:, 0:1536], head_gains_c).then_inc(rot_c_loaded, 16)
            for g in range(C_GROUPS):
                for k in range(4):
                    split_hi(C_AT + 4 * g + k + LEAD)
                    if g == 2 and k == 0:
                        head_roots(C_SUMS[2], [ss_c[:, :, 0:8], ss_c[:, :, GQA_H:]], GQA_D)
                if g == 0:
                    token_stat(C_NORM)
                    act.wait_ge(rstd_ready, C_NORM + 1)
                copy_groups(C_AT + 4 * g + 3, AB_TOKS + 3 * g, c_b[g % 2], c_tok, C_W, C_ORDER[g])
                if g < 2:
                    group_squares(g)
            attention(Gqa, late=last_heads)
            transposed_out(KD, [1.0] * KD)
            out_chunks(4, C_AT + C_OUT, 1)

            ffn(3)
            u0 = FFN_AT[3] + 2 * FT + LEAD
            loops = (N_UNITS - u0) // RING
            with act.Fori(0, loops) as i:
                for k in range(RING):
                    split_hi(u0 + k, i, RING)
            for u in range(u0 + loops * RING, N_UNITS):
                split_hi(u)

        @block.vector
        def _(dve):
            def at_chunk(buf, m):
                return buf[:, m, :] if isinstance(m, int) else buf[:, bass.ds(m, 1), :].rearrange("p a n -> p (a n)")

            def norm_chunk(n, m, mm):
                dve.wait_ge(xg_hi_done, m + (KD * n + 1))
                g = gain[:, n, bass.ds(m, 1)] if not isinstance(m, int) else gain[:, n, m:m + 1]
                dve.scalar_tensor_tensor(out=at_chunk(xg_lo, m), in0=at_chunk(x, m), scalar=g,
                                         in1=at_chunk(xg_hi, m).bitcast(F32), op0=ALU.mult,
                                         op1=ALU.subtract).then_inc(xg_ready, 1)
                dve.wait_ge(sq_done, m + (KD * n + 1))
                if not (isinstance(m, int) and m + KD * n == 0):
                    dve.wait_ge(acc_done, m + KD * n)
                dve.tensor_tensor(acc[:], acc[:], tmp[:, mm % 2, :], ALU.add).then_inc(acc_done, 1)

            def zero_acc(n):
                dve.memset(acc[:], 0.0).then_inc(acc_zero, 1)
                dve.wait_ge(acc_zero, n + 1)

            def ffn_tile(c, u0, n, j, jj):
                p = jj % 2
                first = jj < 2
                u = j * 2 + u0
                dve.wait_ge(unit_used, used(u))
                if not first:
                    dve.wait_ge(h_raw, j + (FT * c - 1))
                dve.tensor_tensor(tmp[:, p, :], gate_b[p][:], rstd[:], ALU.mult).then_inc(gate_read, 1)
                dve.wait_ge(unit_used, used(u + 1))
                if not first:
                    dve.wait_ge(h_ready, j + (FT * c - 1))
                dve.tensor_tensor(tmp[:, 2 + p, :], up_b[p][:], rstd[:], ALU.mult).then_inc(up_read, 1)
                if jj > 0:
                    hidden_lo(c, j - 1, 1 - p)
                dve.wait_ge(silu_done, j + (FT * c + 1))
                dve.wait_ge(up_read, done(j + FT * c))
                dve.tensor_tensor(tmp[:, 2 + p, :], tmp[:, p, :], tmp[:, 2 + p, :], ALU.mult).then_inc(h_raw, 1)

            def hidden_lo(c, j, p):
                dve.wait_ge(h_hi_done, j + (FT * c + 1))
                dve.tensor_tensor(at_chunk(h_lo, j), tmp[:, 2 + p, :], at_chunk(h_hi, j).bitcast(F32),
                                  ALU.subtract).then_inc(h_ready, 1)

            def ffn(c):
                u0, n = FFN_AT[c], FFN_NORM[c]
                dve.wait_ge(std_done, n + 1)
                dve.reciprocal(rstd[:], rstd[:]).then_inc(rstd_ready, 1)
                dve.wait_ge(rstd_ready, n + 1)
                ffn_tile(c, u0, n, 0, 0)
                ffn_tile(c, u0, n, 1, 1)
                with dve.Fori(0, FT // 2 - 1) as i:
                    for jj in (2, 3):
                        ffn_tile(c, u0, n, i * 2 + jj, jj)
                hidden_lo(c, FT - 1, (FT - 1) % 2)

            def out_chunks(q, u0, per, coef, last=False):
                n = q + 1
                if not last:
                    zero_acc(n)
                with dve.Fori(0, KD // 4) as i:
                    for mm in range(4):
                        m = i * 4 + mm
                        dve.wait_ge(unit_used, used(i * (4 * per) + (u0 + per * mm + per - 1)))
                        dve.scalar_tensor_tensor(out=at_chunk(x, m), in0=y_b[mm % 2][:], scalar=coef,
                                                 in1=at_chunk(x, m), op0=ALU.mult, op1=ALU.add).then_inc(x_new, 1)
                        if not last:
                            dve.wait_ge(x_new, done(m + KD * q))
                            norm_chunk(n, m, mm)

            def token_stat(n):
                dve.wait_ge(std_done, n + 1)
                dve.reciprocal(rstd_tok, rstd_tok).then_inc(rstd_ready, 1)
                dve.wait_ge(rstd_ready, n + 1)

            def copy_groups(u, toks, banks, dst, width, g):
                for t in (1, 3):
                    if t == 3:
                        dve.wait_ge(unit_used, used(u))
                    else:
                        dve.wait_ge(tok_done, toks + t + 1)
                    dve.tensor_scalar(dst[:, t, g * width:(g + 1) * width], banks[t][:, 0:width],
                                      rstd_tok[:, t:t + 1], None, ALU.mult).then_inc(tok_dve, 1)

            def head_sums(at, sums):
                for k, (src, dst) in enumerate(sums):
                    dve.wait_ge(hs_sq, at + k + 1)
                    dve.tensor_reduce(dst, squares(at + k, src), AX.X, ALU.add).then_inc(hs_red, 1)

            def head_inverse(k, views):
                dve.wait_ge(hs_std, k)
                for v in views:
                    last = dve.reciprocal(v, v)
                last.then_inc(hs_ready, 1)

            def first_queries(cfg):
                if cfg is not Diff:
                    prepare(dve, cfg, False, 0, 0, 0, EVERY)

            def attention(cfg, late=None):
                nb = TT * cfg.heads

                def queries(i, sub, n, stages):
                    if cfg is not Diff:
                        prepare(dve, cfg, False, i, sub, n, stages)

                spread_stages = {1: (0, 1), 2: (2,), 3: (3,)} if cfg is Mla else {b + 2: (b,) for b in EVERY}

                def copy_operand(n, sub):
                    dve.wait_ge(tr_done, tr_step(cfg, n, cfg.steps - 1))
                    dst = kT_mla[:, 2 * sub, :] if cfg is Mla else kT[:, 2 * sub + 1, :]
                    dve.tensor_copy(dst, tr_b[:]).then_inc(tr_dve, 1)

                def maxima(n, bl):
                    for part in range(cfg.parts):
                        sat = score_at(cfg, n, bl, part)
                        slot = bl % 4 if cfg.parts == 1 else 2 * (bl % 2) + part
                        dve.wait_ge(s_done, sat + 1)
                        dve.tensor_reduce(negmax[:, bass.ds(sat, 1)], s_b[slot][:], AX.X, ALU.max,
                                          negate=True).then_inc(max_done, 1)

                def combine(n, bl):
                    sat = score_at(cfg, n, bl, 0)
                    b = n * nb + bl
                    p1, p2 = p_buf[:, 2 * (bl % 2), :], p_buf[:, 2 * (bl % 2) + 1, :]
                    dve.wait_ge(p_done, adone(score_at(cfg, n, bl, 1)))
                    dve.reciprocal(rinv[:, bass.ds(sat, 2)], rowsum[:, bass.ds(sat, 2)]).then_inc(r_diff, 1)
                    dve.wait_ge(r_diff, b + 1)
                    dve.scalar_tensor_tensor(out=ratio[:, bass.ds(b, 1)], in0=rinv[:, bass.ds(sat + 1, 1)],
                                             scalar=lam[:, 0:1], in1=rowsum[:, bass.ds(sat, 1)], op0=ALU.mult,
                                             op1=ALU.mult).then_inc(ratio_done, 1)
                    dve.wait_ge(ratio_done, b + 1)
                    dve.scalar_tensor_tensor(out=p1, in0=p2, scalar=ratio[:, bass.ds(b, 1)], in1=p1,
                                             op0=ALU.mult, op1=ALU.add).then_inc(w_done, 1)

                def out_block(i, sub, n, bl):
                    b = block_at(cfg, n, bl)
                    sat = score_at(cfg, n, bl, 0)
                    if cfg.parts == 1:
                        dve.wait_ge(p_done, adone(sat))
                        dve.reciprocal(rinv[:, bass.ds(sat, 1)], rowsum[:, bass.ds(sat, 1)]).then_inc(r_done, 1)
                        dve.wait_ge(r_done, sat + (1 - Mla.S0))
                    dve.wait_ge(o_done, adone(b))
                    dve.tensor_scalar(cfg.o_at(i, sub, bl // TT, bl % TT), o_b[:, 0:V_D],
                                      rinv[:, bass.ds(sat, 1)], None, ALU.mult).then_inc(o_out, 1)

                def pair(i, sub, n, ahead):
                    for bl in range(nb):
                        if cfg.parts == 2:
                            combine(n, bl)
                            if bl > 1:
                                out_block(i, sub, n, bl - 2)
                            elif not (isinstance(n, int) and n == 0):
                                out_block(*pair_at(i, sub, -1), n - 1, nb + bl - 2)
                        if bl > 0:
                            if bl + 2 < nb:
                                maxima(n, bl + 2)
                            elif ahead:
                                maxima(n + 1, bl + 2 - nb)
                        if bl == 1 and ahead:
                            copy_operand(n + 1, 1 - sub)
                        if cfg.parts == 1 and bl > 0:
                            out_block(i, sub, n, bl - 1)
                        if ahead == 2 and bl in spread_stages:
                            queries(*pair_at(i, sub, 2), n + 2, spread_stages[bl])
                        if bl == 0 and cfg is Mla and not ahead:
                            dve.wait_ge(sub_sq, TT)
                            dve.tensor_reduce(ss_o, heads(ab_tok[:, :, DQ0:DK0], V_D), AX.X,
                                              ALU.add).then_inc(sub_sum, 1)
                    if ahead:
                        maxima(n + 1, 2)
                    if cfg.parts == 1:
                        out_block(i, sub, n, nb - 1)
                    elif not ahead:
                        out_block(i, sub, n, nb - 2)
                        out_block(i, sub, n, nb - 1)

                copy_operand(0, 0)
                maxima(0, 0)
                maxima(0, 1)
                queries(0, 1, 1, EVERY)
                maxima(0, 2)
                if late is not None:
                    late()
                each_pair(dve, pair, peel=cfg.parts == 2)

            def transposed_out(base, scales):
                for k in range(KD):
                    dve.wait_ge(oT_hi_done, base + k + 1)
                    dve.scalar_tensor_tensor(out=oT_lo[:, k, :], in0=oT_b[k % 2][:], scalar=scales[k],
                                             in1=oT_hi[:, k, :].bitcast(F32), op0=ALU.mult,
                                             op1=ALU.subtract).then_inc(oT_ready, 1)

            dve.wait_ge(gains_loaded, 16 * 2)
            dve.wait_ge(consts_made, 6)
            zero_acc(0)
            for m in range(KD):
                if m % 2 == 0:
                    dve.wait_ge(x_loaded[m // 2], 16)
                norm_chunk(0, m, m)
            dve.wait_ge(consts_loaded, 16 * 4)
            for k, scale in enumerate((QK_D ** -0.5, 1.0, DIFF_D ** -0.5, 1.0)):
                seg = rot[:, 512 * k:512 * k + 512]
                dve.scalar_tensor_tensor(out=seg, in0=seg, scalar=scale, in1=hg[:, 512 * k:512 * k + 512],
                                         op0=ALU.mult, op1=ALU.mult).then_inc(tables_made, 1)
            dve.tensor_scalar(subln[:], subln[:], 1.0 - LAM_INIT, None, ALU.mult).then_inc(tables_made, 1)
            dve.tensor_tensor(lam_p[:], lam_v[:, 0:4:2, :], lam_v[:, 1:4:2, :], ALU.mult).then_inc(lam_step, 1)
            dve.wait_ge(lam_step, 1)
            dve.tensor_reduce(lam[:, 0:2], lam_p[:], AX.X, ALU.add).then_inc(lam_step, 1)

            dve.wait_ge(lam_exp, 1)
            dve.scalar_tensor_tensor(out=lam[:, 0:1], in0=lam[:, 3:4], scalar=-LAM_INIT, in1=lam[:, 2:3],
                                     op0=ALU.add, op1=ALU.subtract).then_inc(tables_made, 1)

            ffn(0)
            out_chunks(0, FFN_AT[0] + 2 * FT, DOWN_U, 0.5)

            u0 = AB_AT
            token_stat(AB_NORM)
            dve.tensor_tensor(rstd_sq, rstd_tok, rstd_tok, ALU.mult).then_inc(lat_step, 1)
            for m in range(LATENT):
                dve.wait_ge(lat_hi_done, m + 1)
                dve.scalar_tensor_tensor(out=lat_lo[:, m, :], in0=bank[m][:], scalar=lat_g[:, m:m + 1],
                                         in1=lat_hi[:, m, :].bitcast(F32), op0=ALU.mult,
                                         op1=ALU.subtract).then_inc(lat_ready, 1)
            dve.wait_ge(lat_stat, 1)
            dve.wait_ge(lat_step, 1)
            dve.tensor_tensor(r_lat.rearrange("p (a t) -> p a t", a=2),
                              tok_stat_b[:, TT:3 * TT].rearrange("p (a t) -> p a t", a=2),
                              rstd_sq[:, None, :].to_broadcast([P, 2, TT]), ALU.mult).then_inc(lat_step, 1)
            dve.wait_ge(lat_std, 1)
            dve.reciprocal(r_lat, r_lat).then_inc(lat_step, 1)
            dve.wait_ge(lat_step, 3)
            dve.tensor_tensor(r_lat.rearrange("p (a t) -> p a t", a=2), r_lat.rearrange("p (a t) -> p a t", a=2),
                              rstd_tok[:, None, :].to_broadcast([P, 2, TT]), ALU.mult).then_inc(lat_step, 1)
            dve.wait_ge(lat_step, 4)
            copy_groups(u0 + AB_G0 + 3, 0, bank[4:8], ab_tok, AB_W, 0)
            for o in range(1, 16, 2):
                half, t = o // 4 % 2, o % 4
                if o in (3, 7, 15):
                    dve.wait_ge(unit_used, used(u0 + AB_UP + min(o // 4, 2)))
                else:
                    dve.wait_ge(tok_done, 3 + (3 * (o // 4) + t if o < 8 else 6 + o - 8) + 1)
                dst = (q_tok[:, t, half * 384:half * 384 + 384] if o < 8 else
                       kv_tok[:, t, half * 512:half * 512 + 512])
                n_el = 384 if o < 8 else 512
                r = r_lat[:, t:t + 1] if o < 8 else r_lat[:, TT + t:TT + t + 1]
                dve.tensor_scalar(dst, bank[o % 8][:, 0:n_el], r, None, ALU.mult).then_inc(tok_dve, 1)
            for g in range(1, AB_GROUPS):
                if g == 1:
                    head_sums(0, mla_sums)
                    dve.wait_ge(hs_red, MLA_SUMS)
                    dve.tensor_tensor(ss_k, ss_k, ss_kr[:, :, None].to_broadcast([P, TT, MLA_H]),
                                      ALU.add).then_inc(hs_keys, 1)
                    head_inverse(1, [ss[:, 0:64]])
                if g == 3:
                    head_sums(MLA_SUMS, diff_sums)
                    head_inverse(2, [ss[:, 68:196]])
                copy_groups(u0 + AB_G1 + 4 * g - 1, 16 + 3 * (g - 1), bank[0:4] if g % 2 else bank[4:8],
                            ab_tok, AB_W, g)
            dve.wait_ge(tables_made, TABLES_AB)
            dve.wait_ge(hs_ready, 2)
            attention(Diff)
            dve.wait_ge(tr_done, tr_step(Diff, 2 * ITERS - 1, 3))
            dve.memset(qb[:, 0:SEQ].rearrange("p (t d) -> p t d", t=TT)[:, :, QK_D:P], 0.0).then_inc(pads_zero, 1)
            first_queries(Mla)
            attention(Mla)
            dve.wait_ge(sub_std, 1)
            dve.reciprocal(ss[:, 196:228], ss[:, 196:228]).then_inc(sub_inv, 1)
            dve.wait_ge(sub_inv, 1)
            for t in range(TT):
                od = ab_o[:, t, MLA_H * V_D:].rearrange("p (h d) -> p h d", d=V_D)
                dve.tensor_tensor(od, od, ss_o[:, t, :, None].to_broadcast([P, DIFF_H, V_D]),
                                  ALU.mult).then_inc(sub_done, 1)
            transposed_out(0, [1.0] * 4 + [subln[:, 0:1]] * 4)
            out_chunks(1, AB_AT + AB_OUT, 1, 1.0)

            ffn(1)
            out_chunks(2, FFN_AT[1] + 2 * FT, DOWN_U, 0.5)
            ffn(2)
            out_chunks(3, FFN_AT[2] + 2 * FT, DOWN_U, 0.5)

            token_stat(C_NORM)
            dve.wait_ge(rot_c_loaded, 32)
            for k, scale in enumerate((GQA_D ** -0.5, 1.0)):
                cut = slice(1024 * k, 1024 + 512 * k)
                seg = rot_c[:, cut]
                dve.scalar_tensor_tensor(out=seg, in0=seg, scalar=scale, in1=hg[:, cut],
                                         op0=ALU.mult, op1=ALU.mult).then_inc(tables_made, 1)
            dve.wait_ge(tables_made, TABLES_AB + TABLES_C)
            for g in range(C_GROUPS):
                copy_groups(C_AT + 4 * g + 3, AB_TOKS + 3 * g, c_b[g % 2], c_tok, C_W, C_ORDER[g])
                if g < 2:
                    head_sums(C_SUMS[g], c_sums[g])
                if g == 1:
                    head_inverse(3, [ss_c[:, :, 0:8], ss_c[:, :, GQA_H:]])
                    dve.wait_ge(hs_ready, 3)
                    first_queries(Gqa)

            def last_heads():
                head_sums(C_SUMS[2], c_sums[2])
                head_inverse(4, [ss_c[:, :, 8:GQA_H]])
                dve.wait_ge(hs_ready, 4)

            attention(Gqa, late=last_heads)
            transposed_out(KD, [1.0] * KD)
            out_chunks(4, C_AT + C_OUT, 1, 1.0)

            ffn(3)
            out_chunks(5, FFN_AT[3] + 2 * FT, DOWN_U, 0.5, last=True)

        @block.tensor
        def _(pe):
            def product(dst, a_hi, a_lo, b_hi, b_lo, start, stop):
                pe.matmul(dst, a_lo, b_hi, start=start, stop=False)
                pe.matmul(dst, a_hi, b_lo, start=False, stop=False)
                return pe.matmul(dst, a_hi, b_hi, start=False, stop=stop)

            def feature_unit(dst, u, s, in_hi, in_lo, k0, nk, start, stop, before=None):
                pe.wait_ge(lo_ready, u + 1)
                for r in range(nk):
                    if before is not None:
                        before(k0 + r)
                    c = slice(r * P, (r + 1) * P)
                    last = product(dst, w_hi[s][:, c], w_lo[s][:, c], in_hi[:, k0 + r, :], in_lo[:, k0 + r, :],
                                   start and r == 0, stop and r == nk - 1)
                last.then_inc(unit_used, 1)

            def xg_wait(n):
                def before(k):
                    pe.wait_ge(xg_ready, KD * n + k + 1)
                return before

            def ffn_tile(c, u0, n, j, jj):
                p = jj % 2
                for half, (banks, read) in enumerate(((gate_b, gate_read), (up_b, up_read))):
                    pe.wait_ge(read, free(j + FT * c))
                    feature_unit(banks[p][:], j * 2 + (u0 + half), (u0 + 2 * jj + half) % RING, xg_hi, xg_lo, 0, KD,
                                 True, True, xg_wait(n) if jj == 0 and half == 0 else None)

            def ffn(c):
                u0, n = FFN_AT[c], FFN_NORM[c]
                ffn_tile(c, u0, n, 0, 0)
                pe.wait_ge(acc_done, KD * (n + 1))
                pe.matmul(stat_b[:], ones_d[:], acc[:], start=True, stop=True).then_inc(stat_done, 1)
                ffn_tile(c, u0, n, 1, 1)
                with pe.Fori(0, FT // 2 - 1) as i:
                    for jj in (2, 3):
                        ffn_tile(c, u0, n, i * 2 + jj, jj)

            def out_chunks(q, u0, per, in_hi, in_lo, n_in, before):
                with pe.Fori(0, KD // 4) as i:
                    for mm in range(4):
                        pe.wait_ge(x_new, free(i * 4 + (KD * q + mm)))
                        for r in range(per):
                            a = u0 + per * mm + r
                            feature_unit(y_b[mm % 2][:], i * (4 * per) + a, a % RING, in_hi, in_lo, r * KD,
                                         min(KD, n_in - r * KD), r == 0, r == per - 1, before if mm == 0 else None)

            def down(c, q):
                def before(k):
                    if k == 0:
                        pe.wait_ge(h_ready, FT * c + FT - 2)
                    if k >= FT - 2:
                        pe.wait_ge(h_ready, FT * c + k + 1)
                out_chunks(q, FFN_AT[c] + 2 * FT, DOWN_U, h_hi, h_lo, FT, before)

            def token_stat(n):
                pe.wait_ge(acc_done, KD * (n + 1))
                for t in range(TT):
                    last = pe.matmul(tok_stat_b[:, t:t + 1], acc[:, tok[t]], ones_d[:, 0:1], start=True, stop=True)
                last.then_inc(stat_done, 1)

            def token_group(u0, banks, width, n_unit=4, before=None):
                for kk in range(n_unit):
                    u = u0 + kk
                    s = u % RING
                    pe.wait_ge(lo_ready, u + 1)
                    if kk < n_unit - 1:
                        for r in range(2):
                            if before is not None:
                                before(2 * kk + r)
                            for t in range(TT):
                                w = slice(r * width, (r + 1) * width)
                                last = product(banks[t][:, 0:width], xg_hi[:, 2 * kk + r, tok[t]],
                                               xg_lo[:, 2 * kk + r, tok[t]], w_hi[s][:, w], w_lo[s][:, w],
                                               kk == 0 and r == 0, False)
                        last.then_inc(unit_used, 1)
                    else:
                        for t in range(TT):
                            for r in range(2):
                                if before is not None:
                                    before(2 * kk + r)
                                w = slice(r * width, (r + 1) * width)
                                last = product(banks[t][:, 0:width], xg_hi[:, 2 * kk + r, tok[t]],
                                               xg_lo[:, 2 * kk + r, tok[t]], w_hi[s][:, w], w_lo[s][:, w],
                                               False, r == 1)
                            last.then_inc(tok_done if t < TT - 1 else unit_used, 1)

            def attention(cfg, before_scores=None):
                nb = TT * cfg.heads

                def source(k, t):
                    buf, k = (qb, k) if k < cfg.q_steps else (kb, k - cfg.q_steps)
                    if cfg is Mla:
                        at = t
                    elif cfg is Gqa and buf is kb:
                        at = TT * k + t
                    else:
                        at = 2 * t + k
                    return buf[:, at * P:(at + 1) * P]

                def transposes(n, k):
                    if k in (0, cfg.q_steps):
                        pe.wait_ge(k_prep if k else q_prep, n + (cfg.H0 + 1))
                    if k > 0:
                        pe.wait_ge(tr_act, act_copied(cfg, n, k))
                    elif not (cfg is Diff and isinstance(n, int) and n == 0):
                        pe.wait_ge(tr_dve, n + cfg.H0)
                    for t in range(TT):
                        last = pe.transpose(tr_b[:, tok[t]], source(k, t), ident[:])
                    last.then_inc(tr_done, 1)

                def scores(n, sub, bl):
                    if bl == 0:
                        pe.wait_ge(tr_act, act_copied(cfg, n, cfg.steps - 1))
                        pe.wait_ge(tr_dve, n + (cfg.H0 + 1))
                    for part in range(cfg.parts):
                        sat = score_at(cfg, n, bl, part)
                        slot = bl % 4 if cfg.parts == 1 else 2 * (bl % 2) + part
                        a = 2 * sub + bl // TT + part
                        q, t = qT[:, a, tok[bl % TT]], 2 * sub + part
                        pe.wait_ge(p_done, afree(sat, 4))
                        if cfg is Gqa:
                            pe.matmul(s_b[slot][:], q, kT[:, t + 1, :], start=True, stop=False)
                            last = pe.matmul(s_b[slot][:], q, kT[:, t, :], start=False, stop=True)
                        elif cfg is Diff:
                            last = pe.matmul(s_b[slot][:], q, kT[:, t, :], start=True, stop=True)
                        else:
                            last = pe.matmul(s_b[slot][:], qT_mla[:, a, tok[bl % TT]], kT_mla[:, t, :],
                                             start=True, stop=True)
                        last.then_inc(s_done, 1)

                def transpose_p(n, bl):
                    b = block_at(cfg, n, bl)
                    if cfg.parts == 2:
                        pe.wait_ge(w_done, n * nb + (bl + 1))
                    else:
                        pe.wait_ge(p_done, adone(score_at(cfg, n, bl, 0)))
                    pe.wait_ge(pT_ready, afree(b, 2))
                    src = p_buf[:, bl % 4 if cfg.parts == 1 else 2 * (bl % 2), :]
                    for c in range(TT):
                        last = pe.transpose(pT_b[bl % 2][:, tok[c]], src[:, tok[c]], ident[:])
                    last.then_inc(pT_done, 1)

                def values(i, sub, n, bl):
                    b = block_at(cfg, n, bl)
                    pe.wait_ge(pT_ready, adone(b))
                    pe.wait_ge(o_out, afree(b, 1))
                    for c in range(TT):
                        last = pe.matmul(o_b[:, 0:V_D], pT[:, bl % 2, tok[c]], cfg.v(i, sub, c),
                                         start=(c == 0), stop=(c == TT - 1))
                    last.then_inc(o_done, 1)

                def pair(i, sub, n, ahead):
                    for bl in range(nb):
                        if bl < 2 and ahead:
                            transposes(n + 1, bl if cfg.steps == 2 else 2 * bl)
                        if bl > 0:
                            if bl + 2 < nb:
                                scores(n, sub, bl + 2)
                            elif ahead:
                                scores(n + 1, 1 - sub, bl + 2 - nb)
                        transpose_p(n, bl)
                        if bl < 2 and ahead and cfg.steps == 4:
                            transposes(n + 1, 2 * bl + 1)
                        if bl > 0:
                            values(i, sub, n, bl - 1)
                    if ahead:
                        scores(n + 1, 1 - sub, 2)
                    values(i, sub, n, nb - 1)

                for k in range(cfg.steps):
                    transposes(0, k)
                if before_scores is not None:
                    before_scores()
                for bl in range(3):
                    scores(0, 0, bl)
                each_pair(pe, pair)

            def transposed_out(base, o, blocks):
                pe.wait_ge(o_out, adone(blocks - 1))
                for k in range(KD):
                    if o is ab_o and k == 4:
                        pe.wait_ge(sub_done, TT)
                    if k >= 2:
                        pe.wait_ge(oT_ready, base + k - 1)
                    for t in range(TT):
                        last = pe.transpose(oT_b[k % 2][:, tok[t]], o[:, t, k * P:(k + 1) * P], ident[:])
                    last.then_inc(oT_done, 1)

            def out_proj(q, u0, base):
                def before(k):
                    pe.wait_ge(oT_ready, base + k + 1)
                out_chunks(q, u0, 1, oT_hi, oT_lo, KD, before)

            pe.sem_inc(unit_used, RING)
            for s in (gate_read, up_read, x_new):
                pe.sem_inc(s, 2)
            for s in (tr_done, p_done, pT_done, pT_ready, o_done, o_out):
                pe.sem_inc(s, 4)
            pe.wait_ge(consts_made, 6)

            ffn(0)
            down(0, 0)

            def copies_done(n):
                def wait():
                    pe.wait_ge(tok_act, n)
                    pe.wait_ge(tok_dve, n)
                return wait

            u0 = AB_AT
            for m in range(LATENT):
                feature_unit(bank[m][:], u0 + AB_LAT + m, (u0 + AB_LAT + m) % RING, xg_hi, xg_lo, 0, KD, True, True,
                             xg_wait(AB_NORM) if m == 0 else None)
                if m == 0:
                    token_stat(AB_NORM)
            token_group(u0 + AB_G0, bank[4:8], AB_W)
            pe.wait_ge(lat_hi_done, LATENT)
            pe.wait_ge(std_done, AB_NORM + 1)
            for t in range(TT):
                for m in range(2):
                    pe.matmul(tok_stat_b[:, TT + t:TT + t + 1], lat_sq[:, m, tok[t]], ones_lat[:, 0:1],
                              start=(m == 0), stop=(m == 1))
            for t in range(TT):
                last = pe.matmul(tok_stat_b[:, 2 * TT + t:2 * TT + t + 1], lat_sq[:, 2, tok[t]], ones_lat[:, 1:2],
                                 start=True, stop=True)
            last.then_inc(lat_stat, 1)
            pe.wait_ge(lat_ready, LATENT)
            pe.wait_ge(lat_step, 2)
            for o in range(16):
                half, t = o // 4 % 2, o % 4
                u = u0 + AB_UP + min(o // 4, 2)
                s = u % RING
                if o in (0, 4, 8):
                    pe.wait_ge(lo_ready, u + 1)
                if o == 4:
                    pe.wait_ge(tok_act, 2)
                    pe.wait_ge(tok_dve, 2)
                if o >= 8:
                    pe.wait_ge(tok_dve if o % 2 else tok_act, 2 + (o - 8) // 2 + 1)
                if o < 8:
                    for r in range(2):
                        w = slice(r * 384, (r + 1) * 384)
                        last = product(bank[o % 8][:, 0:384], lat_hi[:, r, tok[t]], lat_lo[:, r, tok[t]],
                                       w_hi[s][:, w], w_lo[s][:, w], r == 0, r == 1)
                else:
                    w = slice(half * 512, (half + 1) * 512)
                    last = product(bank[o % 8][:], lat_hi[:, 2, tok[t]], lat_lo[:, 2, tok[t]], w_hi[s][:, w],
                                   w_lo[s][:, w], True, True)
                last.then_inc(unit_used if o in (3, 7, 15) else tok_done, 1)
            for g in range(1, AB_GROUPS):
                pe.wait_ge(tok_act, 4 + 2 * g if g > 1 else 8)
                pe.wait_ge(tok_dve, 4 + 2 * g if g > 1 else 8)
                if g == 2:
                    pe.wait_ge(tok_act, 10)
                    pe.wait_ge(tok_dve, 10)
                if g == 3:
                    pe.wait_ge(tok_act, 12)
                    pe.wait_ge(tok_dve, 12)
                token_group(u0 + AB_G1 + 4 * (g - 1), bank[0:4] if g % 2 else bank[4:8], AB_W)
            pe.wait_ge(tok_act, AB_COPIES - 2)
            pe.wait_ge(tok_dve, AB_COPIES - 2)
            attention(Diff, before_scores=copies_done(AB_COPIES))
            pe.wait_ge(pads_zero, 2)
            attention(Mla)
            transposed_out(0, ab_o, TT * (DIFF_H + MLA_H))
            out_proj(1, AB_AT + AB_OUT, 0)

            ffn(1)
            down(1, 2)
            ffn(2)
            down(2, 3)

            for g in range(C_GROUPS):
                if g == 1:
                    pe.wait_ge(std_done, C_NORM + 1)
                if g == 2:
                    pe.wait_ge(tok_act, AB_COPIES + 2)
                    pe.wait_ge(tok_dve, AB_COPIES + 2)
                token_group(C_AT + 4 * g, c_b[g % 2], C_W,
                            before=xg_wait(C_NORM) if g == 0 else None)
                if g == 0:
                    token_stat(C_NORM)
            copies_done(AB_COPIES + 2 * C_GROUPS - 2)()
            attention(Gqa, before_scores=copies_done(AB_COPIES + 2 * C_GROUPS))
            transposed_out(KD, c_o, TT * (DIFF_H + MLA_H + GQA_H))
            out_proj(4, C_AT + C_OUT, KD)

            ffn(3)
            down(3, 5)


def units_of(w):
    k, n = w.shape[0] // P, w.shape[1] // P
    u = w.reshape(k, P, n, P).transpose(2, 1, 0, 3)
    pad = -k % KD
    u = np.pad(u, ((0, 0), (0, 0), (0, pad), (0, 0)))
    u = u.reshape(n, P, (k + pad) // KD, UNIT).transpose(0, 2, 1, 3)
    return u.reshape(-1, P, UNIT)


def wide_units(w, width, rows):
    k, n = w.shape[0] // P, w.shape[1] // width
    u = w.reshape(k // rows, rows, P, n, width).transpose(3, 0, 2, 1, 4).reshape(-1, P, rows * width)
    return np.pad(u, ((0, 0), (0, 0), (0, UNIT - rows * width)))


def rotary(pos, dim):
    inv = np.float32(THETA) ** (-np.arange(0, dim, 2, dtype=np.float32) / np.float32(dim))
    ang = pos.astype(np.float32)[:, None] * inv[None, :]
    return np.cos(ang).astype(np.float32), np.sin(ang).astype(np.float32)


def token_major(a):
    return a.reshape(TT, P, -1).transpose(1, 0, 2).reshape(P, -1)


def rotary_tables():
    cos, sin = rotary(np.arange(SEQ), ROPE)
    c32, s32 = np.concatenate([cos, cos], 1), np.concatenate([-sin, sin], 1)
    mla_c = np.concatenate([np.ones((SEQ, NOPE), np.float32), c32], 1)
    two_c, two_s = np.tile(c32, (1, 2)), np.tile(s32, (1, 2))
    parts = [mla_c, s32, mla_c, s32, two_c, two_s, two_c, two_s]
    even = np.concatenate([token_major(p) for p in parts], 1)
    row, col = np.arange(SEQ) // GRID_W, np.arange(SEQ) % GRID_W
    (rc, rs), (cc, cs) = rotary(row, GQA_D // 2), rotary(col, GQA_D // 2)
    ax_c, ax_s = np.concatenate([rc, rc, cc, cc], 1), np.concatenate([-rs, rs, -cs, cs], 1)
    odd = [token_major(p) for p in (np.tile(ax_c, (1, 2)), np.tile(ax_s, (1, 2)), ax_c, ax_s)]
    odd = np.concatenate(odd, 1)
    return even, odd


def swapped(g):
    return g.reshape(-1, 2, 16)[:, ::-1].reshape(-1)


def spread(g):
    return token_major(np.broadcast_to(g, (SEQ, g.size)))


def kernel(**inputs):
    import concourse.bacc as _bacc
    from concourse.bass_utils import run_bass_kernel_spmd as _run

    a = {k: np.asarray(v) for k, v in inputs.items()}
    f = np.ascontiguousarray

    def ffn_units(which, i):
        gate, up = (units_of(a[f"{which}_w_{n}"][i]) for n in ("gate", "up"))
        both = np.stack([gate, up], 1).reshape(-1, P, UNIT)
        return [both, units_of(a[f"{which}_w_down"][i])]

    ab, latent = a["ab_w_in"][0], Q_RANK + KV_RANK
    groups = wide_units(ab[:, latent:], AB_W, 2)
    stream = ffn_units("ffn1", 0)
    stream += [units_of(ab[:, :latent]), groups[:4], wide_units(a["mla_w_uq"][0], 384, 2),
               wide_units(a["mla_w_ukv"][0], 1024, 1), groups[4:], units_of(a["ab_w_out"][0])]
    stream += ffn_units("ffn2", 0) + ffn_units("ffn1", 1)
    c_groups = wide_units(a["c_w_in"][0], C_W, 2).reshape(C_GROUPS, 4, P, UNIT)
    stream += [c_groups[g] for g in C_ORDER] + [units_of(a["c_w_out"][0])]
    stream += ffn_units("ffn2", 1)
    weights = np.concatenate(stream, 0)
    assert weights.shape[0] == N_UNITS

    def by_chunk(g):
        return g.reshape(-1, P).T

    norms = [a[n][i] for i in range(2) for n in ("ffn1_norm", "mix_norm", "ffn2_norm")]
    even, odd = rotary_tables()
    mq, mk, dq, dk = (a[n][0] for n in ("mla_q_norm", "mla_k_norm", "diff_q_norm", "diff_k_norm"))
    cq, ck = a["c_q_norm"][0], a["c_k_norm"][0]
    gains_even = [x for g in (mq, mk) for x in (spread(g), spread(swapped(g[NOPE:])))]
    gains_even += [x for g in (dq, dk) for x in (spread(np.tile(g, 2)), spread(np.tile(swapped(g), 2)))]
    gains_odd = [spread(np.tile(cq, 2)), spread(np.tile(swapped(cq), 2)), spread(ck), spread(swapped(ck))]
    lams = np.stack([a[f"diff_lambda_{n}"][0] for n in ("q1", "k1", "q2", "k2")])
    arrays = {
        "in_x": f(a["x"][0].T.reshape(KD, P, SEQ).transpose(1, 0, 2)),
        "in_weights": weights,
        "in_gains": f(np.stack([by_chunk(g) for g in norms], 1)),
        "in_lat_gain": f(np.concatenate([by_chunk(a["mla_q_lora_norm"][0]), by_chunk(a["mla_kv_lora_norm"][0])], 1)),
        "in_rot": f(even),
        "in_head_gains": f(np.concatenate(gains_even, 1)),
        "in_rot_c": f(odd),
        "in_head_gains_c": f(np.concatenate(gains_odd, 1)),
        "in_lambdas": f(np.broadcast_to(lams, (P, 4, DIFF_D))),
        "in_subln": f(np.tile(a["diff_subln"][0], 2)[:, None]),
    }
    nc = _bacc.Bacc("TRN2", target_bir_lowering=False, num_devices=1)
    args = [nc.dram_tensor(n, v.shape, F32, kind="ExternalInput").ap() for n, v in arrays.items()]
    args.append(nc.dram_tensor("out_x", (P, KD, SEQ), F32, kind="ExternalOutput").ap())
    build_kernel(nc, *args)
    r = _run(nc, [arrays], core_ids=[0])
    y = r.results[0]["out_x"]
    return np.ascontiguousarray(y.transpose(1, 0, 2).reshape(D_MODEL, SEQ).T)[None]
```

```python
import math
from contextlib import ExitStack

import numpy as np

import concourse.bass as bass
from concourse import mybir

P = 128
D_MODEL, SEQ, D_FF, GRID_W = 1024, 512, 2816, 64
THETA, EPS = 10000.0, 1e-6
KD = D_MODEL // P
FT = D_FF // P
TT = SEQ // P
MLA_H, NOPE, ROPE, V_D = 8, 64, 32, 64
QK_D = NOPE + ROPE
Q_RANK, KV_RANK = 256, 128
DIFF_H, DIFF_D = 8, 32
GQA_H, GQA_KV, GQA_D = 16, 4, 64
LAM_INIT = 0.8 - 0.6 * math.exp(-0.3 * 0)

UNIT = 1024
RING = 4
LEAD = 2
LATENT = (Q_RANK + KV_RANK) // P
AB_TOK = ROPE + 3 * DIFF_H * 2 * DIFF_D
AB_GROUPS, AB_W = 4, AB_TOK // 4
C_TOK = (GQA_H + 2 * GQA_KV) * GQA_D
C_GROUPS, C_W = 3, C_TOK // 3
C_ORDER = (2, 0, 1)
DQ0, DK0, DV0 = ROPE, ROPE + DIFF_H * 2 * DIFF_D, ROPE + 2 * DIFF_H * 2 * DIFF_D
CK0, CV0 = GQA_H * GQA_D, (GQA_H + GQA_KV) * GQA_D

DOWN_U = 3
FFN_UNITS = 2 * FT + DOWN_U * KD
AB_LAT, AB_G0 = 0, LATENT
AB_UP = AB_G0 + 4
AB_G1 = AB_UP + 3
AB_OUT = AB_G1 + 4 * (AB_GROUPS - 1)
AB_UNITS = AB_OUT + KD
C_OUT = 4 * C_GROUPS
C_UNITS = C_OUT + KD
FFN_AT = [0, FFN_UNITS + AB_UNITS, 2 * FFN_UNITS + AB_UNITS, 3 * FFN_UNITS + AB_UNITS + C_UNITS]
AB_AT = FFN_UNITS
C_AT = 3 * FFN_UNITS + AB_UNITS
N_UNITS = 4 * FFN_UNITS + AB_UNITS + C_UNITS
FFN_NORM = [0, 2, 3, 5]
AB_NORM, C_NORM = 1, 4

F32, F32R = mybir.dt.float32, mybir.dt.float32r
ALU = mybir.AluOpType
ACT = mybir.ActivationFunctionType
AX = mybir.AxisListType


def used(u):
    return RING + u + 1


def slot_free(u):
    return u + 1


def done(n):
    return n + 3


def free(n):
    return n + 1


def adone(n):
    return n + 5


def afree(n, ring):
    return n + (5 - ring)


def build_kernel(nc, x_in, weights, gains, lat_gain, rot_in, head_gains, rot_c_in, head_gains_c,
                 lam_in, subln_in, out):
    with ExitStack() as ctx:
        def sb(name, shape, dt=F32):
            return ctx.enter_context(nc.sbuf_tensor(name, shape, dt))

        def sem(name):
            return ctx.enter_context(nc.semaphore(name))

        def shared(*names_shapes):
            with ExitStack() as s:
                return [s.enter_context(nc.sbuf_tensor(n, sh, dt)) for n, sh, dt in names_shapes]

        x = sb("x", [P, KD, SEQ])
        stage = sb("stage", [P, RING, UNIT])
        w_hi = [sb(f"w_hi{s}", [P, UNIT], F32R) for s in range(RING)]
        w_lo = [sb(f"w_lo{s}", [P, UNIT], F32R) for s in range(RING)]
        tmp = sb("tmp", [P, 4, SEQ])
        acc = sb("acc", [P, SEQ])
        rstd = sb("rstd", [P, SEQ])
        ident = sb("ident", [P, P])
        ones_d = sb("ones_d", [P, P])
        ones_lat = sb("ones_lat", [P, 2])
        eps = sb("eps", [P, 1])
        gain = sb("gain", [P, 6, KD])
        lat_g = sb("lat_g", [P, LATENT])
        rot = sb("rot", [P, 2048])
        subln = sb("subln", [P, 1])
        lam = sb("lam", [P, 4])
        rtok = sb("rtok", [P, 4 * TT])
        ss = sb("ss", [P, 256])

        p_buf, pT, qT, kT, negmax, rowsum, rinv, ratio = shared(
            ("p_buf", [P, 4, SEQ], F32), ("pT", [P, 2, SEQ], F32), ("qT", [P, 4, SEQ], F32R),
            ("kT", [P, 4, SEQ], F32R), ("negmax", [P, 160], F32),
            ("rowsum", [P, 160], F32), ("rinv", [P, 160], F32), ("ratio", [P, 32], F32))
        xg_hi = sb("xg_hi", [P, KD, SEQ], F32R)
        xg_lo = sb("xg_lo", [P, KD, SEQ], F32R)

        q_tok, kv_tok, ab_tok, ab_o, lat_hi, lat_lo, lat_sq = shared(
            ("q_tok", [P, TT, MLA_H * QK_D], F32), ("kv_tok", [P, TT, MLA_H * 128], F32),
            ("ab_tok", [P, TT, AB_TOK], F32), ("ab_o", [P, TT, D_MODEL], F32),
            ("lat_hi", [P, LATENT, SEQ], F32R), ("lat_lo", [P, LATENT, SEQ], F32R),
            ("lat_sq", [P, LATENT, SEQ], F32))
        oT_hi, oT_lo, c_tok, c_o, rot_c = shared(
            ("oT_hi", [P, KD, SEQ], F32R), ("oT_lo", [P, KD, SEQ], F32R),
            ("c_tok", [P, TT, C_TOK], F32), ("c_o", [P, TT, D_MODEL], F32), ("rot_c", [P, 1536], F32))
        hg, lam_v, lam_p = shared(("hg", [P, 2048], F32), ("lam_v", [P, 4, DIFF_D], F32),
                                  ("lam_p", [P, 2, DIFF_D], F32))
        _, sq_room = shared(("below_oT_lo", [P, KD * SEQ], F32), ("sq_room", [P, 4, 1024], F32))
        _, qa, qd, ka, kd = shared(("below", [P, 2 * KD * SEQ + TT * (C_TOK + D_MODEL) + 2048], F32),
                                   ("qa", [P, SEQ], F32), ("qd", [P, SEQ], F32), ("ka", [P, SEQ], F32),
                                   ("kd", [P, SEQ], F32))
        h_hi = sb("h_hi", [P, FT, SEQ], F32R)
        h_lo = sb("h_lo", [P, FT, SEQ], F32R)

        bank = [ctx.enter_context(nc.psum_tensor(f"bank{b}", [P, 512], F32)) for b in range(8)]
        gate_b, up_b, y_b, stat_b = bank[0:2], bank[2:4], bank[4:6], bank[6]
        tok_stat_b = bank[3]
        c_b = [[bank[0], bank[1], bank[2], bank[6]], [bank[4], bank[5], bank[7], bank[3]]]
        s_b, pT_b, o_b, tr_b = bank[0:4], bank[4:6], bank[6], bank[7]
        first_b_even, first_b_odd = [bank[7], bank[4], bank[5], bank[6]], [bank[7], bank[4], bank[5], bank[3]]
        oT_b = bank[0:4]

        landed = [sem(f"landed{s}") for s in range(RING)]
        hi_ready = sem("hi_ready")
        lo_ready = sem("lo_ready")
        unit_used = sem("unit_used")
        x_loaded = [sem(f"x_loaded{k}") for k in range(4)]
        gains_loaded = sem("gains_loaded")
        consts_loaded = sem("consts_loaded")
        rot_c_loaded = sem("rot_c_loaded")
        consts_made = sem("consts_made")
        tables_made = sem("tables_made")
        lam_step = sem("lam_step")
        lam_exp = sem("lam_exp")
        xg_hi_done = sem("xg_hi_done")
        xg_ready = sem("xg_ready")
        sq_done = sem("sq_done")
        acc_zero = sem("acc_zero")
        acc_done = sem("acc_done")
        stat_done = sem("stat_done")
        std_done = sem("std_done")
        rstd_ready = sem("rstd_ready")
        gate_read = sem("gate_read")
        up_read = sem("up_read")
        silu_done = sem("silu_done")
        h_raw = sem("h_raw")
        h_hi_done = sem("h_hi_done")
        h_ready = sem("h_ready")
        x_new = sem("x_new")
        stored = sem("stored")
        waits_taken = sem("waits_taken")
        lat_hi_done = sem("lat_hi_done")
        lat_ready = sem("lat_ready")
        lat_stat = sem("lat_stat")
        lat_step = sem("lat_step")
        lat_std = sem("lat_std")
        tok_done = sem("tok_done")
        tok_act = sem("tok_act")
        tok_dve = sem("tok_dve")
        hs_sq = sem("hs_sq")
        hs_red = sem("hs_red")
        hs_keys = sem("hs_keys")
        hs_std = sem("hs_std")
        hs_ready = sem("hs_ready")
        q_step = sem("q_step")
        q_prep = sem("q_prep")
        k_step = sem("k_step")
        k_prep = sem("k_prep")
        pads_zero = sem("pads_zero")
        tr_done = sem("tr_done")
        tr_act = sem("tr_act")
        tr_dve = sem("tr_dve")
        s_done = sem("s_done")
        max_done = sem("max_done")
        p_done = sem("p_done")
        ratio_done = sem("ratio_done")
        w_done = sem("w_done")
        pT_done = sem("pT_done")
        pT_ready = sem("pT_ready")
        o_done = sem("o_done")
        r_done = sem("r_done")
        o_out = sem("o_out")
        sub_sq = sem("sub_sq")
        sub_sum = sem("sub_sum")
        sub_inv = sem("sub_inv")
        sub_done = sem("sub_done")
        sub_std = sem("sub_std")
        oT_done = sem("oT_done")
        oT_hi_done = sem("oT_hi_done")
        oT_ready = sem("oT_ready")

        block = ctx.enter_context(nc.Block())

        tok = [slice(t * P, (t + 1) * P) for t in range(TT)]
        rstd_tok, rstd_sq = rtok[:, 0:4], rtok[:, 4:8]
        r_lat = rtok[:, 8:16]
        ss_q = ss[:, 0:32].rearrange("p (t h) -> p t h", t=TT)
        ss_k = ss[:, 32:64].rearrange("p (t h) -> p t h", t=TT)
        ss_kr = ss[:, 64:68]
        ss_d = ss[:, 68:196].rearrange("p (t h) -> p t h", t=TT)
        ss_c = ss[:, 0:80].rearrange("p (t h) -> p t h", t=TT)
        ss_o = ss[:, 196:228].rearrange("p (t h) -> p t h", t=TT)
        qb, kb = (tmp[:, k:k + 2, :].rearrange("p a n -> p (a n)") for k in (0, 2))
        qb_r, kb_r = qb.bitcast(F32R), kb.bitcast(F32R)
        qc, kc = acc, rstd
        sq_ab = [ab_o[:, k, :] for k in range(4)]
        sq_c = [sq_room[:, k, :] for k in range(4)]

        def tables(src, specs):
            got, at = [], 0
            for n in specs:
                got.append(src[:, at:at + n])
                at += n
            return got

        m_cq, m_sq, m_ck, m_sk, d_cq, d_sq, d_ck, d_sk = tables(rot, [384, 128, 384, 128, 256, 256, 256, 256])
        c_cq, c_sq, c_ck, c_sk = tables(rot_c, [512, 512, 256, 256])

        class Diff:
            parts, heads, steps, q_steps = 2, 1, 4, 2
            S0, B0, H0, T0 = 0, 0, 0, 0
            act_copies, dve_copies, A0, D0 = 3, 1, 0, 0

            @staticmethod
            def v(i, sub, c):
                return ab_tok[:, c, bass.ds(i * (2 * V_D) + (DV0 + sub * V_D), V_D)]

            @staticmethod
            def o_at(i, sub, a, t):
                return ab_o[:, t, bass.ds(i * (2 * V_D) + ((MLA_H + sub) * V_D), V_D)]

        class Mla:
            parts, heads, steps, q_steps = 1, 1, 2, 1
            S0, B0, H0, T0 = 2 * TT * DIFF_H, TT * DIFF_H, DIFF_H, 4 * DIFF_H
            act_copies, dve_copies, A0, D0 = 2, 2, 3 * DIFF_H, DIFF_H

            @staticmethod
            def v(i, sub, c):
                return kv_tok[:, c, bass.ds(i * 256 + (sub * 128 + NOPE), V_D)]

            @staticmethod
            def o_at(i, sub, a, t):
                return ab_o[:, t, bass.ds(i * (2 * V_D) + sub * V_D, V_D)]

        class Gqa:
            parts, heads, steps, q_steps = 1, 2, 4, 2
            S0 = 2 * TT * DIFF_H + TT * MLA_H
            B0, H0, T0 = TT * (DIFF_H + MLA_H), DIFF_H + MLA_H, 4 * DIFF_H + 2 * MLA_H
            act_copies, dve_copies, A0, D0 = 3, 1, 3 * DIFF_H + 2 * MLA_H, DIFF_H + 2 * MLA_H

            @staticmethod
            def v(i, sub, c):
                return c_tok[:, c, bass.ds(i * V_D + CV0, V_D)]

            @staticmethod
            def o_at(i, sub, a, t):
                return c_o[:, t, bass.ds(i * (4 * GQA_D) + (2 * sub + a) * GQA_D, V_D)]

        ITERS = 4

        def apart(eng):
            eng.sem_inc(waits_taken, 1)

        def block_at(pair, bl):
            cfg, _, _, n = pair
            return n * (TT * cfg.heads) + (cfg.B0 + bl)

        def score_at(pair, bl, part):
            cfg, _, _, n = pair
            return n * (TT * cfg.heads * cfg.parts) + (cfg.S0 + bl * cfg.parts + part)

        def blocks(pair):
            return TT * pair[0].heads

        def slot_of(pair, bl, part=0):
            return bl % 4 if pair[0].parts == 1 else 2 * (bl % 2) + part

        def operands_at(pair, nxt, bl):
            if nxt is None or bl >= (4 if blocks(pair) == 2 * TT else 2):
                return None, None
            if blocks(pair) == 2 * TT or nxt[0].steps == 2:
                return bl, None
            return 2 * bl, 2 * bl + 1

        def neighbour(cfgs, pair, k):
            cfg, i, sub, n = pair
            if not isinstance(n, int):
                return cfg, i + (sub + k) // 2, (sub + k) % 2, n + k
            at = cfgs.index(cfg) * 2 * ITERS + n + k
            if not 0 <= at < 2 * ITERS * len(cfgs):
                return None
            m = at % (2 * ITERS)
            return cfgs[at // (2 * ITERS)], m // 2, m % 2, m

        def tr_bank(pair, k):
            cfg, _, _, n = pair
            if isinstance(n, int) and n == 0 and cfg is not Mla:
                return (first_b_even if cfg is Diff else first_b_odd)[k]
            return tr_b

        def each_pair(eng, cfgs, body):
            def one(cfg, i, sub, n):
                here = (cfg, i, sub, n)
                body(here, lambda k: neighbour(cfgs, here, k))

            for cfg in cfgs:
                for sub in range(2):
                    one(cfg, 0, sub, sub)
                with eng.Fori(1, ITERS - 1) as i:
                    for sub in range(2):
                        one(cfg, i, sub, i * 2 + sub)
                for sub in range(2):
                    one(cfg, ITERS - 1, sub, (ITERS - 1) * 2 + sub)

        def tr_step(cfg, n, k):
            return n * cfg.steps + (4 + cfg.T0 + k + 1)

        def act_copied(cfg, n, k):
            return n * cfg.act_copies + (cfg.A0 + k)

        def dve_copied(cfg, n, k):
            return n * cfg.dve_copies + (cfg.D0 + k)

        def parts_of(cfg, keys):
            d = kd if keys else qd
            w = DIFF_D if cfg is Diff else GQA_D
            n_el = TT * GQA_D * (2 if cfg is Gqa and not keys else 1)
            full = d[:, 0:n_el].rearrange("p (g d) -> p g d", d=w)
            b_r = kb_r if keys else qb_r
            if cfg is Diff and not keys:
                parts = b_r.rearrange("p (g c h d) -> p g c h d", c=2, h=2, d=w)
                hi, lo = parts[:, :, :, 0, :], parts[:, :, :, 1, :]
            elif cfg is Diff:
                parts = b_r.rearrange("p (g h c d) -> p g h c d", c=2, h=2, d=w)
                hi, lo = parts[:, :, 0, :, :], parts[:, :, 1, :, :]
            elif keys:
                parts = b_r.rearrange("p (h g c d) -> p h g c d", c=2, h=2, d=w)
                hi, lo = parts[:, 0, :, :, :], parts[:, 1, :, :, :]
            else:
                parts = b_r.rearrange("p (g h d) -> p g h d", h=2, d=w)
                hi, lo = parts[:, :, 0, :], parts[:, :, 1, :]
            if len(hi.shape) == 4:
                full = full[:, :, None, :].to_broadcast(list(hi.shape))
            return full, hi, lo

        def parts_free(eng, cfg, keys, n):
            eng.wait_ge(tr_done, tr_step(cfg, n - 1, cfg.steps - 1 if keys else cfg.q_steps - 1))
            apart(eng)

        def prepare(eng, cfg, keys, i, sub, n, stages):
            a, b, c = (ka, kb, kc) if keys else (qa, qb, qc)
            d = kd if keys else qd
            step_sem, out_sem = (k_step, k_prep) if keys else (q_step, q_prep)
            steps = 2 if cfg is Mla else 4
            step0 = 4 * cfg.H0 if cfg is not Gqa else 4 * DIFF_H + 2 * MLA_H

            def stepped(k):
                eng.wait_ge(step_sem, n * steps + (step0 + k))

            if cfg is Mla:
                n_el, cos, sin = TT * QK_D, m_ck if keys else m_cq, m_sk if keys else m_sq
                a3 = a[:, 0:n_el].rearrange("p (t d) -> p t d", t=TT)
                b3 = b[:, 0:SEQ].rearrange("p (t d) -> p t d", t=TT)[:, :, 0:QK_D]
                a_rot, b_rot = a3[:, :, NOPE:QK_D], b3[:, :, NOPE:QK_D]
            else:
                if cfg is Diff:
                    n_el, cos, sin = TT * 2 * DIFF_D, d_ck if keys else d_cq, d_sk if keys else d_sq
                elif keys:
                    n_el, cos, sin = TT * GQA_D, c_ck, c_sk
                else:
                    n_el, cos, sin = TT * 2 * GQA_D, c_cq, c_sq
                a_rot = a[:, 0:n_el].rearrange("p (g d) -> p g d", d=32)
                b_rot = d[:, 0:n_el].rearrange("p (g d) -> p g d", d=32)
            s3 = sin.rearrange("p (g d) -> p g d", d=32)
            c3 = c[:, 0:s3.shape[1] * 32].rearrange("p (g d) -> p g d", d=32)

            if 0 in stages:
                if cfg is Mla:
                    eng.wait_ge(tr_done, tr_step(cfg, n - 1, 1 if keys else 0))
                    apart(eng)
                if cfg is Mla and keys:
                    r = ss_k[:, :, bass.ds(i * 2 + sub, 1)]
                    eng.tensor_tensor(a3[:, :, 0:NOPE], kv_tok[:, :, bass.ds(i * 256 + sub * 128, NOPE)],
                                      r.to_broadcast([P, TT, NOPE]), ALU.mult)
                    eng.tensor_tensor(a3[:, :, NOPE:QK_D], ab_tok[:, :, 0:ROPE], r.to_broadcast([P, TT, ROPE]),
                                      ALU.mult).then_inc(step_sem, 1)
                elif cfg is Mla:
                    eng.tensor_tensor(a3, q_tok[:, :, bass.ds(i * (2 * QK_D) + sub * QK_D, QK_D)],
                                      ss_q[:, :, bass.ds(i * 2 + sub, 1)].to_broadcast([P, TT, QK_D]),
                                      ALU.mult).then_inc(step_sem, 1)
                else:
                    if cfg is Diff:
                        src = ab_tok[:, :, bass.ds(i * 128 + (sub * 64 + (DK0 if keys else DQ0)), 64)].rearrange(
                            "p t (e d) -> p t e d", e=2)
                        r = ss_d[:, :, bass.ds(i * 4 + (sub * 2 + (16 if keys else 0)), 2), None]
                    elif keys:
                        src = c_tok[:, :, None, bass.ds(i * GQA_D + CK0, GQA_D)]
                        r = ss_c[:, :, bass.ds(i + GQA_H, 1), None]
                    else:
                        src = c_tok[:, :, bass.ds(i * 256 + sub * 128, 128)].rearrange("p t (e d) -> p t e d", e=2)
                        r = ss_c[:, :, bass.ds(i * 4 + sub * 2, 2), None]
                    eng.tensor_tensor(a[:, 0:n_el].rearrange("p (t e d) -> p t e d", t=TT, e=src.shape[2]), src,
                                      r.to_broadcast(list(src.shape)), ALU.mult).then_inc(step_sem, 1)
            if 1 in stages:
                stepped(1)
                if cfg is Mla:
                    eng.tensor_tensor(b3, a3, cos.rearrange("p (t d) -> p t d", t=TT), ALU.mult)
                else:
                    eng.tensor_tensor(d[:, 0:n_el], a[:, 0:n_el], cos, ALU.mult)
            if 2 in stages:
                eng.tensor_tensor(c3[:, :, 0:16], a_rot[:, :, 16:32], s3[:, :, 0:16], ALU.mult)
                eng.tensor_tensor(c3[:, :, 16:32], a_rot[:, :, 0:16], s3[:, :, 16:32],
                                  ALU.mult).then_inc(step_sem, 1)
            if 3 in stages:
                stepped(2)
                eng.tensor_tensor(b_rot, b_rot, c3, ALU.add).then_inc(out_sem if cfg is Mla else step_sem, 1)
            if cfg is not Mla:
                full, hi, lo = parts_of(cfg, keys)
                if 4 in stages:
                    stepped(3)
                    parts_free(eng, cfg, keys, n)
                    eng.tensor_copy(hi, full).then_inc(step_sem, 1)
                if 5 in stages:
                    stepped(4)
                    eng.tensor_tensor(lo, full, hi.bitcast(F32), ALU.subtract).then_inc(out_sem, 1)

        EVERY = range(6)
        LAST_GQA = 2 * ITERS - 1

        def heads(v, d):
            return v.rearrange("p t (h d) -> p t h d", d=d)

        mla_sums = [(ab_tok[:, :, None, 0:ROPE], ss_kr[:, :, None])]
        mla_sums += [(heads(q_tok[:, t:t + 1, :], QK_D), ss_q[:, t:t + 1, :]) for t in range(TT)]
        mla_sums += [(heads(kv_tok[:, t:t + 2, :], 128)[:, :, :, 0:NOPE], ss_k[:, t:t + 2, :]) for t in (0, 2)]
        diff_sums = [(heads(ab_tok[:, t:t + 1, DQ0:DV0], DIFF_D), ss_d[:, t:t + 1, :]) for t in range(TT)]
        c_sums = [[(heads(c_tok[:, :, CK0:CV0], GQA_D), ss_c[:, :, GQA_H:])]]
        c_sums += [[(heads(c_tok[:, t:t + 2, g * C_W:(g + 1) * C_W], GQA_D), ss_c[:, t:t + 2, g * 8:g * 8 + 8])
                    for t in (0, 2)] for g in range(2)]
        MLA_SUMS, DIFF_SUMS = len(mla_sums), len(mla_sums) + len(diff_sums)
        C_SUMS = [DIFF_SUMS, DIFF_SUMS + 1, DIFF_SUMS + 3, DIFF_SUMS + 5]

        def squares(at, src):
            t, h, d = src.shape[1:]
            room = (sq_ab if at < DIFF_SUMS else sq_c)[at % 4]
            return room[:, 0:t * h * d].rearrange("p (t h d) -> p t h d", h=h, d=d)

        TABLES_AB, TABLES_C = 6, 2
        AB_COPIES, AB_TOKS = 2 * AB_GROUPS + 8, 3 * AB_GROUPS + 6 + 7

        @block.sync
        def _(sp):
            def load_unit(k):
                sp.dma_start(stage[:, k, :], weights[k]).then_inc(landed[k], 16)

            load_unit(0)
            for dst, src in ((gain, gains), (lat_g, lat_gain)):
                sp.dma_start(dst[:], src).then_inc(gains_loaded, 16)
            for k in range(4):
                sp.dma_start(x[:, 2 * k:2 * k + 2, :], x_in[:, 2 * k:2 * k + 2, :]).then_inc(x_loaded[k], 16)
                if k == 2:
                    load_unit(1)
            for k in range(2, RING):
                load_unit(k)
            for dst, src in ((rot, rot_in), (hg, head_gains), (lam_v, lam_in), (subln, subln_in)):
                sp.dma_start(dst[:], src).then_inc(consts_loaded, 16)
            with sp.Fori(1, N_UNITS // RING) as i:
                for s in range(RING):
                    sp.wait_ge(lo_ready, i * RING + (s - RING + 1))
                    sp.dma_start(stage[:, s, :], weights[i * RING + s]).then_inc(landed[s], 16)
            for u in range(N_UNITS // RING * RING, N_UNITS):
                sp.wait_ge(lo_ready, u - RING + 1)
                sp.dma_start(stage[:, u % RING, :], weights[u]).then_inc(landed[u % RING], 16)
            for m in range(KD):
                sp.wait_ge(x_new, done(5 * KD + m))
                sp.dma_start(out[:, m, :], x[:, m, :]).then_inc(stored, 16)
            sp.wait_ge(stored, 16 * KD)

        @block.gpsimd
        def _(pool):
            def split_lo(u, s):
                pool.wait_ge(hi_ready, u + 1)
                pool.tensor_tensor(w_lo[s][:], stage[:, s, :], w_hi[s][:].bitcast(F32),
                                   ALU.subtract).then_inc(lo_ready, 1)

            def split_range(a, b):
                n = (b - a) // RING
                if n > 1:
                    with pool.Fori(0, n) as i:
                        for s in range(RING):
                            split_lo(i * RING + (a + s), (a + s) % RING)
                    a += n * RING
                for u in range(a, b):
                    split_lo(u, u % RING)

            pool.memset(ident[:], 0.0).then_inc(consts_made, 1)
            pool.wait_ge(consts_made, 1)
            pool.affine_select(out=ident[:], in_=ident[:], compare_op=ALU.not_equal, fill=1.0, base=0,
                               pattern=[[-1, P]], channel_multiplier=1).then_inc(consts_made, 1)
            pool.memset(ones_d[:], 1.0 / D_MODEL).then_inc(consts_made, 1)
            pool.memset(ones_lat[:, 0:1], 1.0 / Q_RANK).then_inc(consts_made, 1)
            pool.memset(ones_lat[:, 1:2], 1.0 / KV_RANK).then_inc(consts_made, 1)
            pool.memset(eps[:], EPS).then_inc(consts_made, 1)

            def pair_prep(cfg, i, sub, n):
                if cfg is Diff:
                    for stages in (range(4), (5,)):
                        prepare(pool, cfg, False, i, sub, n, stages)
                        prepare(pool, cfg, True, i, sub, n, stages)
                else:
                    prepare(pool, cfg, True, i, sub, n, EVERY)

            def all_preps(cfg, first=0, end=ITERS):
                with pool.Fori(first, end) as i:
                    for sub in range(2):
                        pair_prep(cfg, i, sub, i * 2 + sub)

            pool.wait_ge(lo_ready, 1)
            for u in range(1, RING):
                split_lo(u, u)
            split_range(RING, AB_AT + AB_OUT + LEAD)
            pool.wait_ge(tables_made, TABLES_AB)
            pool.wait_ge(hs_ready, 2)
            pool.wait_ge(k_prep, 1)
            for stages in (range(4), (5,)):
                prepare(pool, Diff, True, 0, 1, 1, stages)
            pool.wait_ge(q_prep, 2)
            all_preps(Diff, 1)
            pool.wait_ge(tr_done, tr_step(Diff, 2 * ITERS - 1, 3))
            pool.memset(kb[:, 0:SEQ].rearrange("p (t d) -> p t d", t=TT)[:, :, QK_D:P], 0.0).then_inc(pads_zero, 1)
            all_preps(Mla, 0, ITERS // 2)
            pool.wait_ge(o_out, adone(TT * DIFF_H - 1))
            for t in range(TT):
                od = ab_o[:, t, MLA_H * V_D:]
                pool.tensor_tensor(ab_tok[:, t, DQ0:DK0], od, od, ALU.mult).then_inc(sub_sq, 1)
            all_preps(Mla, ITERS // 2)
            pool.wait_ge(sub_inv, 1)
            for t in range(TT):
                od = ab_o[:, t, MLA_H * V_D:].rearrange("p (h d) -> p h d", d=V_D)
                pool.tensor_tensor(od, od, ss_o[:, t, :, None].to_broadcast([P, DIFF_H, V_D]),
                                   ALU.mult).then_inc(sub_done, 1)
            split_range(AB_AT + AB_OUT + LEAD, C_AT + C_OUT + LEAD)
            pool.wait_ge(tables_made, TABLES_AB + TABLES_C)
            pool.wait_ge(hs_ready, 3)
            all_preps(Gqa)
            split_range(C_AT + C_OUT + LEAD, N_UNITS)

        @block.scalar
        def _(act):
            def split_hi(a, i=0, step=0):
                s = a % RING
                act.wait_ge(landed[s], i * (16 * step // RING) + 16 * (a // RING + 1))
                act.wait_ge(unit_used, slot_free(i * step + a))
                act.activation(w_hi[s][:], stage[:, s, :], ACT.Copy).then_inc(hi_ready, 1)

            def ffn_tile(c, u0, n, j, jj, i=0):
                p = jj % 2
                if c > 0 or jj > 0:
                    split_hi(u0 + 2 * jj + LEAD, i, 4)
                    split_hi(u0 + 2 * jj + LEAD + 1, i, 4)
                if jj == 0:
                    act.wait_ge(stat_done, n + 1)
                    act.activation(rstd[:], stat_b[:], ACT.Sqrt, bias=eps[:]).then_inc(std_done, 1)
                act.wait_ge(gate_read, done(j + FT * c))
                act.activation(tmp[:, p, :], tmp[:, p, :], ACT.Silu).then_inc(silu_done, 1)
                act.wait_ge(h_raw, j + (FT * c + 1))
                apart(act)
                h = (h_hi[:, j, :] if isinstance(j, int) else
                     h_hi[:, bass.ds(j, 1), :].rearrange("p a n -> p (a n)"))
                act.activation(h, tmp[:, 2 + p, :], ACT.Copy).then_inc(h_hi_done, 1)

            def ffn(c):
                u0, n = FFN_AT[c], FFN_NORM[c]
                ffn_tile(c, u0, n, 0, 0)
                ffn_tile(c, u0, n, 1, 1)
                with act.Fori(0, FT // 2 - 1) as i:
                    for jj in (2, 3):
                        ffn_tile(c, u0, n, i * 2 + jj, jj, i)

            def out_chunks(q, u0, per):
                n = q + 1
                with act.Fori(0, KD // 4) as i:
                    for mm in range(4):
                        m = i * 4 + mm
                        for r in range(per):
                            split_hi(u0 + per * mm + r + LEAD, i, 4 * per)
                        act.wait_ge(x_new, done(m + KD * q))
                        apart(act)
                        act.activation(xg_hi[:, bass.ds(m, 1), :].rearrange("p a n -> p (a n)"),
                                       x[:, bass.ds(m, 1), :].rearrange("p a n -> p (a n)"), ACT.Copy,
                                       scale=gain[:, n, bass.ds(m, 1)]).then_inc(xg_hi_done, 1)
                        act.wait_ge(acc_done, m + (KD * n - 1))
                        apart(act)
                        act.activation(tmp[:, mm % 2, :], x[:, bass.ds(m, 1), :].rearrange("p a n -> p (a n)"),
                                       ACT.Square).then_inc(sq_done, 1)

            def token_stat(n):
                act.wait_ge(stat_done, n + 1)
                act.activation(rstd_tok, tok_stat_b[:, 0:TT], ACT.Sqrt, bias=eps[:]).then_inc(std_done, 1)

            def copy_groups(u, toks, banks, dst, width, g):
                for t in (0, 2):
                    act.wait_ge(tok_done, toks + t + 1)
                    act.activation(dst[:, t, g * width:(g + 1) * width], banks[t][:, 0:width], ACT.Copy,
                                   scale=rstd_tok[:, t:t + 1]).then_inc(tok_act, 1)

            def head_squares(at, sums):
                for k, (src, _) in enumerate(sums):
                    if at + k >= 4:
                        act.wait_ge(hs_red, at + k - 3)
                    act.activation(squares(at + k, src), src, ACT.Square).then_inc(hs_sq, 1)

            def head_roots(at, views, d):
                act.wait_ge(hs_red, at)
                for v in views:
                    last = act.activation(v, v, ACT.Sqrt, scale=1.0 / d, bias=eps[:])
                last.then_inc(hs_std, 1)

            def attention(cfgs, late):
                def copy_operand(pair, k):
                    cfg, _, sub, n = pair
                    act.wait_ge(tr_done, tr_step(cfg, n, k))
                    dst = (qT[:, 2 * sub + k, :] if k < cfg.q_steps else
                           kT[:, 2 * sub + k - cfg.q_steps, :])
                    act.activation(dst, tr_bank(pair, k)[:], ACT.Copy).then_inc(tr_act, 1)

                def hi_parts(n, keys):
                    full, hi, _ = parts_of(Diff, keys)
                    step_sem = k_step if keys else q_step
                    act.wait_ge(step_sem, n * 4 + 3)
                    parts_free(act, Diff, keys, n)
                    act.activation(hi, full, ACT.Copy).then_inc(step_sem, 1)

                def exps(pair, bl):
                    cfg, _, _, n = pair
                    for part in range(cfg.parts):
                        sat, slot = score_at(pair, bl, part), slot_of(pair, bl, part)
                        act.wait_ge(max_done, sat + 1)
                        ring = 2 if cfg is Mla and isinstance(n, int) and n == 0 else 4 // cfg.parts
                        act.wait_ge(pT_done, afree(block_at(pair, bl), ring))
                        apart(act)
                        act.activation(p_buf[:, slot, :], s_b[slot][:], ACT.Exp, bias=negmax[:, bass.ds(sat, 1)],
                                       accum_out=rowsum[:, bass.ds(sat, 1)]).then_inc(p_done, 1)

                def copy_pT(pair, bl):
                    b = block_at(pair, bl)
                    act.wait_ge(pT_done, adone(b))
                    act.wait_ge(o_done, afree(b, 2))
                    act.activation(pT[:, bl % 2, :], pT_b[bl % 2][:], ACT.Copy).then_inc(pT_ready, 1)

                def work(pair, at):
                    nb, nxt, after = blocks(pair), at(1), at(2)
                    for bl in range(nb):
                        early, late_one = operands_at(pair, nxt, bl)
                        keys_first = bl == 1 and nxt and nxt[0] is Mla
                        if keys_first:
                            copy_operand(nxt, early)
                        if bl + 1 < nb:
                            exps(pair, bl + 1)
                        elif nxt:
                            exps(nxt, 0)
                        if not keys_first and early is not None and early < nxt[0].act_copies:
                            copy_operand(nxt, early)
                        copy_pT(pair, bl)
                        if late_one is not None and late_one < nxt[0].act_copies:
                            copy_operand(nxt, late_one)
                        if after and after[0] is Diff and bl in (1, 2):
                            hi_parts(after[3], keys=(bl == 2))
                        late(pair, bl)

                first = (cfgs[0], 0, 0, 0)
                act.activation(lam[:, 3:4], eps[:], ACT.Exp)
                for k in range(cfgs[0].steps - 1):
                    copy_operand(first, k)
                exps(first, 0)
                if cfgs[0] is Diff:
                    hi_parts(1, True)
                each_pair(act, cfgs, work)

            def out_part(base, k, src, scale=1.0):
                act.wait_ge(oT_done, base + k + 1)
                act.activation(oT_hi[:, k, :], src[:], ACT.Copy, scale=scale).then_inc(oT_hi_done, 1)

            act.wait_ge(consts_made, 6)
            act.activation(lam[:, 2:3], eps[:], ACT.Copy)
            split_hi(0)
            act.wait_ge(gains_loaded, 16 * 2)
            for m in range(KD):
                if m % 2 == 0:
                    act.wait_ge(x_loaded[m // 2], 16)
                if m == 6:
                    split_hi(1)
                act.activation(xg_hi[:, m, :], x[:, m, :], ACT.Copy,
                               scale=gain[:, 0, m:m + 1]).then_inc(xg_hi_done, 1)
                if m >= 2:
                    act.wait_ge(acc_done, m - 1)
                act.activation(tmp[:, m % 2, :], x[:, m, :], ACT.Square).then_inc(sq_done, 1)
            for u in range(LEAD, RING):
                split_hi(u)
            act.wait_ge(lam_step, 2)
            act.activation(lam[:, 2:4], lam[:, 0:2], ACT.Exp).then_inc(lam_exp, 1)

            ffn(0)
            out_chunks(0, FFN_AT[0] + 2 * FT, DOWN_U)

            u0 = AB_AT
            for m in range(LATENT):
                split_hi(u0 + AB_LAT + m + LEAD)
                if m == 1:
                    token_stat(AB_NORM)
                act.wait_ge(unit_used, used(u0 + AB_LAT + m))
                act.activation(lat_hi[:, m, :], bank[m][:], ACT.Copy, scale=lat_g[:, m:m + 1])
                act.activation(lat_sq[:, m, :], bank[m][:], ACT.Square).then_inc(lat_hi_done, 1)
            for k in range(4):
                split_hi(u0 + AB_G0 + k + LEAD)
            act.wait_ge(lat_step, 2)
            act.activation(r_lat, r_lat, ACT.Sqrt, bias=eps[:]).then_inc(lat_std, 1)
            act.wait_ge(rstd_ready, AB_NORM + 1)
            copy_groups(u0 + AB_G0 + 3, 0, bank[4:8], ab_tok, AB_W, 0)
            act.wait_ge(lat_step, 4)
            for o in range(16):
                if o in (0, 4, 8):
                    split_hi(u0 + AB_UP + min(o // 4, 2) + LEAD)
                if o % 2:
                    continue
                half, t = o // 4 % 2, o % 4
                act.wait_ge(tok_done, 3 + (3 * (o // 4) + t if o < 8 else 6 + o - 8) + 1)
                dst = (q_tok[:, t, half * 384:half * 384 + 384] if o < 8 else
                       kv_tok[:, t, half * 512:half * 512 + 512])
                n_el = 384 if o < 8 else 512
                r = r_lat[:, t:t + 1] if o < 8 else r_lat[:, TT + t:TT + t + 1]
                act.activation(dst, bank[o % 8][:, 0:n_el], ACT.Copy, scale=r).then_inc(tok_act, 1)
            for g in range(1, AB_GROUPS):
                for k in range(4):
                    split_hi(u0 + AB_G1 + 4 * (g - 1) + k + LEAD)
                    if g == 3 and k == 0:
                        act.wait_ge(tok_dve, 14)
                        act.wait_ge(tok_act, 14)
                        head_squares(MLA_SUMS, diff_sums)
                    if g == 3 and k == 1:
                        head_roots(DIFF_SUMS, [ss[:, 68:196]], DIFF_D)
                if g == 1:
                    act.wait_ge(tok_dve, 10)
                    act.wait_ge(tok_act, 10)
                    head_squares(0, mla_sums)
                    act.wait_ge(hs_keys, 1)
                    head_roots(MLA_SUMS, [ss[:, 0:64]], QK_D)
                copy_groups(u0 + AB_G1 + 4 * g - 1, 16 + 3 * (g - 1), bank[0:4] if g % 2 else bank[4:8],
                            ab_tok, AB_W, g)
            def differential_roots(pair, bl):
                if pair[0] is Mla and isinstance(pair[3], int) and pair[3] == MLA_H - 2 and bl == TT - 1:
                    act.wait_ge(sub_sum, TT)
                    act.activation(ss[:, 196:228], ss[:, 196:228], ACT.Sqrt, scale=1.0 / V_D,
                                   bias=eps[:]).then_inc(sub_std, 1)

            attention([Diff, Mla], differential_roots)
            for k in range(KD):
                out_part(0, k, oT_b[k % 4], 1.0 if k < 4 else subln[:, 0:1])
            out_chunks(1, AB_AT + AB_OUT, 1)

            ffn(1)
            out_chunks(2, FFN_AT[1] + 2 * FT, DOWN_U)
            ffn(2)
            out_chunks(3, FFN_AT[2] + 2 * FT, DOWN_U)

            def group_squares(g):
                act.wait_ge(tok_dve, AB_COPIES + 2 * g + 2)
                act.wait_ge(tok_act, AB_COPIES + 2 * g + 2)
                head_squares(C_SUMS[g], c_sums[g])

            def last_heads(pair, bl):
                if isinstance(pair[3], int) and pair[3] == 0:
                    if bl == 2:
                        act.wait_ge(tok_dve, AB_COPIES + 6)
                        act.wait_ge(tok_act, AB_COPIES + 6)
                    if bl in (2, 4):
                        head_squares(C_SUMS[2] + bl // 2 - 1, c_sums[2][bl // 2 - 1:bl // 2])
                    if bl == 7:
                        head_roots(C_SUMS[3], [ss_c[:, :, 8:GQA_H]], GQA_D)
                if isinstance(pair[3], int) and pair[3] == LAST_GQA and bl < KD - 1:
                    out_part(KD, bl, tr_b)

            act.dma_start(rot_c[:], rot_c_in).then_inc(rot_c_loaded, 16)
            act.dma_start(hg[:, 0:1536], head_gains_c).then_inc(rot_c_loaded, 16)
            for g in range(C_GROUPS):
                for k in range(4):
                    split_hi(C_AT + 4 * g + k + LEAD)
                    if g == 2 and k == 0:
                        head_roots(C_SUMS[2], [ss_c[:, :, 0:8], ss_c[:, :, GQA_H:]], GQA_D)
                if g == 0:
                    token_stat(C_NORM)
                    act.wait_ge(rstd_ready, C_NORM + 1)
                copy_groups(C_AT + 4 * g + 3, AB_TOKS + 3 * g, c_b[g % 2], c_tok, C_W, C_ORDER[g])
                if g < 2:
                    group_squares(g)
            attention([Gqa], last_heads)
            out_part(KD, KD - 1, oT_b[0])
            out_chunks(4, C_AT + C_OUT, 1)

            ffn(3)
            u0 = FFN_AT[3] + 2 * FT + LEAD
            loops = (N_UNITS - u0) // RING
            with act.Fori(0, loops) as i:
                for k in range(RING):
                    split_hi(u0 + k, i, RING)
            for u in range(u0 + loops * RING, N_UNITS):
                split_hi(u)

        @block.vector
        def _(dve):
            def at_chunk(buf, m):
                return buf[:, m, :] if isinstance(m, int) else buf[:, bass.ds(m, 1), :].rearrange("p a n -> p (a n)")

            def norm_chunk(n, m, mm):
                dve.wait_ge(xg_hi_done, m + (KD * n + 1))
                g = gain[:, n, bass.ds(m, 1)] if not isinstance(m, int) else gain[:, n, m:m + 1]
                dve.scalar_tensor_tensor(out=at_chunk(xg_lo, m), in0=at_chunk(x, m), scalar=g,
                                         in1=at_chunk(xg_hi, m).bitcast(F32), op0=ALU.mult,
                                         op1=ALU.subtract).then_inc(xg_ready, 1)
                dve.wait_ge(sq_done, m + (KD * n + 1))
                if not (isinstance(m, int) and m + KD * n == 0):
                    dve.wait_ge(acc_done, m + KD * n)
                dve.tensor_tensor(acc[:], acc[:], tmp[:, mm % 2, :], ALU.add).then_inc(acc_done, 1)

            def zero_acc(n):
                dve.memset(acc[:], 0.0).then_inc(acc_zero, 1)
                dve.wait_ge(acc_zero, n + 1)

            def ffn_tile(c, u0, n, j, jj):
                p = jj % 2
                first = jj < 2
                u = j * 2 + u0
                dve.wait_ge(unit_used, used(u))
                if not first:
                    dve.wait_ge(h_raw, j + (FT * c - 1))
                dve.tensor_tensor(tmp[:, p, :], gate_b[p][:], rstd[:], ALU.mult).then_inc(gate_read, 1)
                dve.wait_ge(unit_used, used(u + 1))
                if not first:
                    dve.wait_ge(h_ready, j + (FT * c - 1))
                dve.tensor_tensor(tmp[:, 2 + p, :], up_b[p][:], rstd[:], ALU.mult).then_inc(up_read, 1)
                if jj > 0:
                    hidden_lo(c, j - 1, 1 - p)
                dve.wait_ge(silu_done, j + (FT * c + 1))
                dve.wait_ge(up_read, done(j + FT * c))
                dve.tensor_tensor(tmp[:, 2 + p, :], tmp[:, p, :], tmp[:, 2 + p, :], ALU.mult).then_inc(h_raw, 1)

            def hidden_lo(c, j, p):
                dve.wait_ge(h_hi_done, j + (FT * c + 1))
                dve.tensor_tensor(at_chunk(h_lo, j), tmp[:, 2 + p, :], at_chunk(h_hi, j).bitcast(F32),
                                  ALU.subtract).then_inc(h_ready, 1)

            def ffn(c):
                u0, n = FFN_AT[c], FFN_NORM[c]
                dve.wait_ge(std_done, n + 1)
                dve.reciprocal(rstd[:], rstd[:]).then_inc(rstd_ready, 1)
                dve.wait_ge(rstd_ready, n + 1)
                ffn_tile(c, u0, n, 0, 0)
                ffn_tile(c, u0, n, 1, 1)
                with dve.Fori(0, FT // 2 - 1) as i:
                    for jj in (2, 3):
                        ffn_tile(c, u0, n, i * 2 + jj, jj)
                hidden_lo(c, FT - 1, (FT - 1) % 2)

            def out_chunks(q, u0, per, coef, last=False):
                n = q + 1
                if not last:
                    zero_acc(n)
                with dve.Fori(0, KD // 4) as i:
                    for mm in range(4):
                        m = i * 4 + mm
                        dve.wait_ge(unit_used, used(i * (4 * per) + (u0 + per * mm + per - 1)))
                        dve.scalar_tensor_tensor(out=at_chunk(x, m), in0=y_b[mm % 2][:], scalar=coef,
                                                 in1=at_chunk(x, m), op0=ALU.mult, op1=ALU.add).then_inc(x_new, 1)
                        if not last:
                            dve.wait_ge(x_new, done(m + KD * q))
                            norm_chunk(n, m, mm)

            def token_stat(n):
                dve.wait_ge(std_done, n + 1)
                dve.reciprocal(rstd_tok, rstd_tok).then_inc(rstd_ready, 1)
                dve.wait_ge(rstd_ready, n + 1)

            def copy_groups(u, toks, banks, dst, width, g):
                for t in (1, 3):
                    if t == 3:
                        dve.wait_ge(unit_used, used(u))
                    else:
                        dve.wait_ge(tok_done, toks + t + 1)
                    dve.tensor_scalar(dst[:, t, g * width:(g + 1) * width], banks[t][:, 0:width],
                                      rstd_tok[:, t:t + 1], None, ALU.mult).then_inc(tok_dve, 1)

            def head_sums(at, sums):
                for k, (src, dst) in enumerate(sums):
                    dve.wait_ge(hs_sq, at + k + 1)
                    dve.tensor_reduce(dst, squares(at + k, src), AX.X, ALU.add).then_inc(hs_red, 1)

            def head_inverse(k, views):
                dve.wait_ge(hs_std, k)
                for v in views:
                    last = dve.reciprocal(v, v)
                last.then_inc(hs_ready, 1)

            def attention(cfgs, late):
                spread = {Mla: {0: (0,), 1: (1, 2), 2: (3,)}, Gqa: {b + 1: (b,) for b in EVERY}}

                def copy_operand(pair, k):
                    cfg, _, sub, n = pair
                    if cfg is Mla:
                        both = (qT, kT)[k]
                        dve.wait_ge(tr_act, act_copied(cfg, n, k + 1))
                        dve.tensor_tensor(both[:, 2 * sub + 1, :], tr_b[:], both[:, 2 * sub, :].bitcast(F32),
                                          ALU.subtract).then_inc(tr_dve, 1)
                    else:
                        dve.wait_ge(tr_done, tr_step(cfg, n, k))
                        dve.tensor_copy(kT[:, 2 * sub + 1, :], tr_bank(pair, k)[:]).then_inc(tr_dve, 1)

                def maxima(pair, bl, between=None):
                    for part in range(pair[0].parts):
                        if between is not None and part == pair[0].parts - 1:
                            inverse_sums(*between)
                        sat = score_at(pair, bl, part)
                        dve.wait_ge(s_done, sat + 1)
                        dve.tensor_reduce(negmax[:, bass.ds(sat, 1)], s_b[slot_of(pair, bl, part)][:], AX.X, ALU.max,
                                          negate=True).then_inc(max_done, 1)

                def inverse_sums(pair, bl):
                    cfg, sat = pair[0], score_at(pair, bl, 0)
                    dve.wait_ge(p_done, adone(score_at(pair, bl, cfg.parts - 1)))
                    dve.reciprocal(rinv[:, bass.ds(sat, cfg.parts)],
                                   rowsum[:, bass.ds(sat, cfg.parts)]).then_inc(r_done, 1)

                def combine(pair, bl):
                    sat, b = score_at(pair, bl, 0), block_at(pair, bl)
                    p1, p2 = (p_buf[:, slot_of(pair, bl, part), :] for part in range(2))
                    dve.wait_ge(r_done, b + 1)
                    dve.scalar_tensor_tensor(out=ratio[:, bass.ds(b, 1)], in0=rinv[:, bass.ds(sat + 1, 1)],
                                             scalar=lam[:, 0:1], in1=rowsum[:, bass.ds(sat, 1)], op0=ALU.mult,
                                             op1=ALU.mult).then_inc(ratio_done, 1)
                    dve.wait_ge(ratio_done, b + 1)
                    dve.scalar_tensor_tensor(out=p1, in0=p2, scalar=ratio[:, bass.ds(b, 1)], in1=p1,
                                             op0=ALU.mult, op1=ALU.add).then_inc(w_done, 1)

                def out_block(pair, bl):
                    cfg, i, sub, n = pair
                    b, sat = block_at(pair, bl), score_at(pair, bl, 0)
                    dve.wait_ge(r_done, b + 1)
                    dve.wait_ge(o_done, adone(b))
                    dve.tensor_scalar(cfg.o_at(i, sub, bl // TT, bl % TT), o_b[:, 0:V_D],
                                      rinv[:, bass.ds(sat, 1)], None, ALU.mult).then_inc(o_out, 1)

                def queries(pair, stages):
                    cfg, i, sub, n = pair
                    if cfg is Mla and isinstance(n, int) and n == 0 and 0 in stages:
                        dve.wait_ge(tr_done, tr_step(Diff, 2 * ITERS - 1, 1))
                        dve.memset(qb[:, 0:SEQ].rearrange("p (t d) -> p t d", t=TT)[:, :, QK_D:P],
                                   0.0).then_inc(pads_zero, 1)
                    prepare(dve, cfg, False, i, sub, n, stages)

                def work(pair, at):
                    cfg, nb, prev, nxt, after = pair[0], blocks(pair), at(-1), at(1), at(2)
                    for bl in range(nb):
                        if cfg is Diff:
                            combine(pair, bl)
                            if bl > 1:
                                out_block(pair, bl - 2)
                            elif prev:
                                out_block(prev, nb + bl - 2)
                        elif bl == 0 and prev and prev[0] is Diff:
                            out_block(prev, blocks(prev) - 2)
                        if cfg is not Diff and bl > 0:
                            inverse_sums(pair, bl - 1)
                        elif cfg is not Diff and prev and prev[0] is not Diff:
                            inverse_sums(prev, blocks(prev) - 1)
                        if nxt and nxt[0] is Mla and bl < 2:
                            copy_operand(nxt, bl)
                        follows = None
                        if cfg is Diff and bl + 1 < nb:
                            follows = (pair, bl + 1)
                        elif cfg is Diff and nxt[0] is Diff:
                            follows = (nxt, 0)
                        if bl + 2 < nb:
                            maxima(pair, bl + 2, follows)
                        elif nxt:
                            maxima(nxt, bl + 2 - nb, follows)
                        if nxt and nxt[0] is not Mla and nxt[0].steps - 1 in operands_at(pair, nxt, bl):
                            copy_operand(nxt, nxt[0].steps - 1)
                        if cfg is not Diff:
                            if bl > 0:
                                out_block(pair, bl - 1)
                            elif prev:
                                out_block(prev, blocks(prev) - 1)
                        if after and after[0] in spread and bl in spread[after[0]]:
                            queries(after, spread[after[0]][bl])
                        late(pair, bl)
                    if not nxt:
                        inverse_sums(pair, nb - 1)
                        out_block(pair, nb - 1)

                first = (cfgs[0], 0, 0, 0)
                copy_operand(first, cfgs[0].steps - 1)
                maxima(first, 0)
                prepare(dve, cfgs[0], False, 0, 1, 1, (4,))
                maxima(first, 1)
                prepare(dve, cfgs[0], False, 0, 1, 1, (5,))
                if cfgs[0] is Diff:
                    inverse_sums(first, 0)
                each_pair(dve, cfgs, work)

            def out_part(base, k, src, scale=1.0):
                dve.wait_ge(oT_hi_done, base + k + 1)
                dve.scalar_tensor_tensor(out=oT_lo[:, k, :], in0=src[:], scalar=scale,
                                         in1=oT_hi[:, k, :].bitcast(F32), op0=ALU.mult,
                                         op1=ALU.subtract).then_inc(oT_ready, 1)

            zero_acc(0)
            dve.wait_ge(hi_ready, 1)
            dve.tensor_tensor(w_lo[0][:], stage[:, 0, :], w_hi[0][:].bitcast(F32), ALU.subtract).then_inc(lo_ready, 1)
            dve.wait_ge(gains_loaded, 16 * 2)
            dve.wait_ge(consts_made, 6)
            for m in range(KD):
                if m % 2 == 0:
                    dve.wait_ge(x_loaded[m // 2], 16)
                norm_chunk(0, m, m)
            dve.wait_ge(consts_loaded, 16 * 4)
            for k, scale in enumerate((QK_D ** -0.5, 1.0, DIFF_D ** -0.5, 1.0)):
                seg = rot[:, 512 * k:512 * k + 512]
                dve.scalar_tensor_tensor(out=seg, in0=seg, scalar=scale, in1=hg[:, 512 * k:512 * k + 512],
                                         op0=ALU.mult, op1=ALU.mult).then_inc(tables_made, 1)
            dve.tensor_scalar(subln[:], subln[:], 1.0 - LAM_INIT, None, ALU.mult).then_inc(tables_made, 1)
            dve.tensor_tensor(lam_p[:], lam_v[:, 0:4:2, :], lam_v[:, 1:4:2, :], ALU.mult).then_inc(lam_step, 1)
            dve.wait_ge(lam_step, 1)
            dve.tensor_reduce(lam[:, 0:2], lam_p[:], AX.X, ALU.add).then_inc(lam_step, 1)

            dve.wait_ge(lam_exp, 1)
            dve.scalar_tensor_tensor(out=lam[:, 0:1], in0=lam[:, 3:4], scalar=-LAM_INIT, in1=lam[:, 2:3],
                                     op0=ALU.add, op1=ALU.subtract).then_inc(tables_made, 1)

            ffn(0)
            out_chunks(0, FFN_AT[0] + 2 * FT, DOWN_U, 0.5)

            u0 = AB_AT
            token_stat(AB_NORM)
            dve.tensor_tensor(rstd_sq, rstd_tok, rstd_tok, ALU.mult).then_inc(lat_step, 1)
            for m in range(LATENT):
                dve.wait_ge(lat_hi_done, m + 1)
                dve.scalar_tensor_tensor(out=lat_lo[:, m, :], in0=bank[m][:], scalar=lat_g[:, m:m + 1],
                                         in1=lat_hi[:, m, :].bitcast(F32), op0=ALU.mult,
                                         op1=ALU.subtract).then_inc(lat_ready, 1)
            dve.wait_ge(lat_stat, 1)
            dve.wait_ge(lat_step, 1)
            dve.tensor_tensor(r_lat.rearrange("p (a t) -> p a t", a=2),
                              tok_stat_b[:, TT:3 * TT].rearrange("p (a t) -> p a t", a=2),
                              rstd_sq[:, None, :].to_broadcast([P, 2, TT]), ALU.mult).then_inc(lat_step, 1)
            dve.wait_ge(lat_std, 1)
            dve.reciprocal(r_lat, r_lat).then_inc(lat_step, 1)
            dve.wait_ge(lat_step, 3)
            dve.tensor_tensor(r_lat.rearrange("p (a t) -> p a t", a=2), r_lat.rearrange("p (a t) -> p a t", a=2),
                              rstd_tok[:, None, :].to_broadcast([P, 2, TT]), ALU.mult).then_inc(lat_step, 1)
            dve.wait_ge(lat_step, 4)
            copy_groups(u0 + AB_G0 + 3, 0, bank[4:8], ab_tok, AB_W, 0)
            for o in range(1, 16, 2):
                half, t = o // 4 % 2, o % 4
                if o in (3, 7, 15):
                    dve.wait_ge(unit_used, used(u0 + AB_UP + min(o // 4, 2)))
                else:
                    dve.wait_ge(tok_done, 3 + (3 * (o // 4) + t if o < 8 else 6 + o - 8) + 1)
                dst = (q_tok[:, t, half * 384:half * 384 + 384] if o < 8 else
                       kv_tok[:, t, half * 512:half * 512 + 512])
                n_el = 384 if o < 8 else 512
                r = r_lat[:, t:t + 1] if o < 8 else r_lat[:, TT + t:TT + t + 1]
                dve.tensor_scalar(dst, bank[o % 8][:, 0:n_el], r, None, ALU.mult).then_inc(tok_dve, 1)
            for g in range(1, AB_GROUPS):
                if g == 1:
                    head_sums(0, mla_sums)
                    dve.wait_ge(hs_red, MLA_SUMS)
                    dve.tensor_tensor(ss_k, ss_k, ss_kr[:, :, None].to_broadcast([P, TT, MLA_H]),
                                      ALU.add).then_inc(hs_keys, 1)
                    head_inverse(1, [ss[:, 0:64]])
                if g == 3:
                    head_sums(MLA_SUMS, diff_sums)
                    head_inverse(2, [ss[:, 68:196]])
                    dve.wait_ge(tables_made, TABLES_AB)
                    dve.wait_ge(hs_ready, 2)
                    prepare(dve, Diff, False, 0, 0, 0, EVERY)
                    prepare(dve, Diff, True, 0, 0, 0, EVERY)
                    prepare(dve, Diff, False, 0, 1, 1, range(4))
                copy_groups(u0 + AB_G1 + 4 * g - 1, 16 + 3 * (g - 1), bank[0:4] if g % 2 else bank[4:8],
                            ab_tok, AB_W, g)
            def differential_sums(pair, bl):
                cfg, _, _, n = pair
                if cfg is Mla and isinstance(n, int) and n == MLA_H - 2:
                    dve.wait_ge(sub_sq, bl + 1)
                    dve.tensor_reduce(ss_o[:, bl:bl + 1, :], heads(ab_tok[:, bl:bl + 1, DQ0:DK0], V_D), AX.X,
                                      ALU.add).then_inc(sub_sum, 1)
                if cfg is Mla and isinstance(n, int) and n == MLA_H - 1 and bl == 0:
                    dve.wait_ge(sub_std, 1)
                    dve.reciprocal(ss[:, 196:228], ss[:, 196:228]).then_inc(sub_inv, 1)

            attention([Diff, Mla], differential_sums)
            for k in range(KD):
                out_part(0, k, oT_b[k % 4], 1.0 if k < 4 else subln[:, 0:1])
            out_chunks(1, AB_AT + AB_OUT, 1, 1.0)

            ffn(1)
            out_chunks(2, FFN_AT[1] + 2 * FT, DOWN_U, 0.5)
            ffn(2)
            out_chunks(3, FFN_AT[2] + 2 * FT, DOWN_U, 0.5)

            token_stat(C_NORM)
            dve.wait_ge(rot_c_loaded, 32)
            for k, scale in enumerate((GQA_D ** -0.5, 1.0)):
                cut = slice(1024 * k, 1024 + 512 * k)
                seg = rot_c[:, cut]
                dve.scalar_tensor_tensor(out=seg, in0=seg, scalar=scale, in1=hg[:, cut],
                                         op0=ALU.mult, op1=ALU.mult).then_inc(tables_made, 1)
            dve.wait_ge(tables_made, TABLES_AB + TABLES_C)
            for g in range(C_GROUPS):
                copy_groups(C_AT + 4 * g + 3, AB_TOKS + 3 * g, c_b[g % 2], c_tok, C_W, C_ORDER[g])
                if g < 2:
                    head_sums(C_SUMS[g], c_sums[g])
                if g == 1:
                    head_inverse(3, [ss_c[:, :, 0:8], ss_c[:, :, GQA_H:]])
                    dve.wait_ge(hs_ready, 3)
                    prepare(dve, Gqa, False, 0, 0, 0, EVERY)
                    prepare(dve, Gqa, False, 0, 1, 1, range(4))

            def last_heads(pair, bl):
                n = pair[3]
                if isinstance(n, int) and n == 0 and bl in (3, 5):
                    head_sums(C_SUMS[2] + bl // 2 - 1, c_sums[2][bl // 2 - 1:bl // 2])
                if isinstance(n, int) and n == 1 and bl == 0:
                    head_inverse(4, [ss_c[:, :, 8:GQA_H]])
                    dve.wait_ge(hs_ready, 4)
                if isinstance(n, int) and n == LAST_GQA and bl < KD - 1:
                    out_part(KD, bl, tr_b)

            attention([Gqa], last_heads)
            out_part(KD, KD - 1, oT_b[0])
            out_chunks(4, C_AT + C_OUT, 1, 1.0)

            ffn(3)
            out_chunks(5, FFN_AT[3] + 2 * FT, DOWN_U, 0.5, last=True)

        @block.tensor
        def _(pe):
            def product(dst, a_hi, a_lo, b_hi, b_lo, start, stop):
                pe.matmul(dst, a_lo, b_hi, start=start, stop=False)
                pe.matmul(dst, a_hi, b_lo, start=False, stop=False)
                return pe.matmul(dst, a_hi, b_hi, start=False, stop=stop)

            def feature_unit(dst, u, s, in_hi, in_lo, k0, nk, start, stop, before=None):
                pe.wait_ge(lo_ready, u + 1)
                for r in range(nk):
                    if before is not None:
                        before(k0 + r)
                    c = slice(r * P, (r + 1) * P)
                    last = product(dst, w_hi[s][:, c], w_lo[s][:, c], in_hi[:, k0 + r, :], in_lo[:, k0 + r, :],
                                   start and r == 0, stop and r == nk - 1)
                last.then_inc(unit_used, 1)

            def xg_wait(n):
                def before(k):
                    pe.wait_ge(xg_ready, KD * n + k + 1)
                return before

            def ffn_tile(c, u0, n, j, jj):
                p = jj % 2
                for half, (banks, read) in enumerate(((gate_b, gate_read), (up_b, up_read))):
                    pe.wait_ge(read, free(j + FT * c))
                    feature_unit(banks[p][:], j * 2 + (u0 + half), (u0 + 2 * jj + half) % RING, xg_hi, xg_lo, 0, KD,
                                 True, True, xg_wait(n) if jj == 0 and half == 0 else None)

            def ffn(c):
                u0, n = FFN_AT[c], FFN_NORM[c]
                ffn_tile(c, u0, n, 0, 0)
                pe.wait_ge(acc_done, KD * (n + 1))
                pe.matmul(stat_b[:], ones_d[:], acc[:], start=True, stop=True).then_inc(stat_done, 1)
                ffn_tile(c, u0, n, 1, 1)
                with pe.Fori(0, FT // 2 - 1) as i:
                    for jj in (2, 3):
                        ffn_tile(c, u0, n, i * 2 + jj, jj)

            def out_chunks(q, u0, per, in_hi, in_lo, n_in, before):
                with pe.Fori(0, KD // 4) as i:
                    for mm in range(4):
                        pe.wait_ge(x_new, free(i * 4 + (KD * q + mm)))
                        for r in range(per):
                            a = u0 + per * mm + r
                            feature_unit(y_b[mm % 2][:], i * (4 * per) + a, a % RING, in_hi, in_lo, r * KD,
                                         min(KD, n_in - r * KD), r == 0, r == per - 1, before if mm == 0 else None)

            def down(c, q):
                def before(k):
                    if k == 0:
                        pe.wait_ge(h_ready, FT * c + FT - 2)
                    if k >= FT - 2:
                        pe.wait_ge(h_ready, FT * c + k + 1)
                out_chunks(q, FFN_AT[c] + 2 * FT, DOWN_U, h_hi, h_lo, FT, before)

            def token_stat(n):
                pe.wait_ge(acc_done, KD * (n + 1))
                for t in range(TT):
                    last = pe.matmul(tok_stat_b[:, t:t + 1], acc[:, tok[t]], ones_d[:, 0:1], start=True, stop=True)
                last.then_inc(stat_done, 1)

            def token_group(u0, banks, width, n_unit=4, before=None):
                for kk in range(n_unit):
                    u = u0 + kk
                    s = u % RING
                    pe.wait_ge(lo_ready, u + 1)
                    if kk < n_unit - 1:
                        for r in range(2):
                            if before is not None:
                                before(2 * kk + r)
                            for t in range(TT):
                                w = slice(r * width, (r + 1) * width)
                                last = product(banks[t][:, 0:width], xg_hi[:, 2 * kk + r, tok[t]],
                                               xg_lo[:, 2 * kk + r, tok[t]], w_hi[s][:, w], w_lo[s][:, w],
                                               kk == 0 and r == 0, False)
                        last.then_inc(unit_used, 1)
                    else:
                        for t in range(TT):
                            for r in range(2):
                                if before is not None:
                                    before(2 * kk + r)
                                w = slice(r * width, (r + 1) * width)
                                last = product(banks[t][:, 0:width], xg_hi[:, 2 * kk + r, tok[t]],
                                               xg_lo[:, 2 * kk + r, tok[t]], w_hi[s][:, w], w_lo[s][:, w],
                                               False, r == 1)
                            last.then_inc(tok_done if t < TT - 1 else unit_used, 1)

            def attention(cfgs, before_scores, late):
                def source(cfg, k, t):
                    buf, k = (qb, k) if k < cfg.q_steps else (kb, k - cfg.q_steps)
                    if cfg is Mla:
                        at = t
                    elif cfg is Gqa and buf is kb:
                        at = TT * k + t
                    else:
                        at = 2 * t + k
                    return buf[:, at * P:(at + 1) * P]

                def transposes(pair, k):
                    cfg, _, _, n = pair
                    if k in (0, cfg.q_steps):
                        pe.wait_ge(k_prep if k else q_prep, n + (cfg.H0 + 1))
                    if cfg is Mla and isinstance(n, int) and n == 0 and k == 0:
                        pe.wait_ge(pads_zero, 2)
                    dst = tr_bank(pair, k)
                    if not isinstance(n, int) or n > 0 or cfg is Mla:
                        if k > 0 and cfg is not Mla:
                            pe.wait_ge(tr_act, act_copied(cfg, n, k))
                        else:
                            pe.wait_ge(tr_dve, dve_copied(cfg, n, k))
                    for t in range(TT):
                        last = pe.transpose(dst[:, tok[t]], source(cfg, k, t), ident[:])
                    last.then_inc(tr_done, 1)

                def scores(pair, bl):
                    cfg, _, sub, n = pair
                    if bl == 0:
                        pe.wait_ge(tr_act, act_copied(cfg, n, cfg.act_copies))
                        pe.wait_ge(tr_dve, dve_copied(cfg, n, cfg.dve_copies))
                    for part in range(cfg.parts):
                        sat = score_at(pair, bl, part)
                        dst = s_b[slot_of(pair, bl, part)][:]
                        a, t = 2 * sub + bl // TT + part, 2 * sub + part
                        q = qT[:, a, tok[bl % TT]]
                        pe.wait_ge(p_done, afree(sat, 4))
                        if cfg is Gqa:
                            pe.matmul(dst, q, kT[:, t + 1, :], start=True, stop=False)
                            last = pe.matmul(dst, q, kT[:, t, :], start=False, stop=True)
                        elif cfg is Diff:
                            last = pe.matmul(dst, q, kT[:, t, :], start=True, stop=True)
                        else:
                            last = product(dst, qT[:, 2 * sub, tok[bl]], qT[:, 2 * sub + 1, tok[bl]],
                                           kT[:, 2 * sub, :], kT[:, 2 * sub + 1, :], True, True)
                        last.then_inc(s_done, 1)

                def transpose_p(pair, bl):
                    b = block_at(pair, bl)
                    if pair[0] is Diff:
                        pe.wait_ge(w_done, b + 1)
                    else:
                        pe.wait_ge(p_done, adone(score_at(pair, bl, 0)))
                    pe.wait_ge(pT_ready, afree(b, 2))
                    src = p_buf[:, slot_of(pair, bl), :]
                    for c in range(TT):
                        last = pe.transpose(pT_b[bl % 2][:, tok[c]], src[:, tok[c]], ident[:])
                    last.then_inc(pT_done, 1)

                def values(pair, bl):
                    cfg, i, sub, n = pair
                    b = block_at(pair, bl)
                    pe.wait_ge(pT_ready, adone(b))
                    pe.wait_ge(o_out, afree(b, 1))
                    for c in range(TT):
                        last = pe.matmul(o_b[:, 0:V_D], pT[:, bl % 2, tok[c]], cfg.v(i, sub, c),
                                         start=(c == 0), stop=(c == TT - 1))
                    last.then_inc(o_done, 1)

                def work(pair, at):
                    nb, prev, nxt = blocks(pair), at(-1), at(1)
                    for bl in range(nb):
                        if bl + 2 < nb:
                            scores(pair, bl + 2)
                        elif nxt:
                            scores(nxt, bl + 2 - nb)
                        early, late_one = operands_at(pair, nxt, bl)
                        if early is not None:
                            transposes(nxt, early)
                        transpose_p(pair, bl)
                        if late_one is not None:
                            transposes(nxt, late_one)
                        if bl > 0:
                            values(pair, bl - 1)
                        elif prev:
                            values(prev, blocks(prev) - 1)
                        late(pair, bl)
                    if not nxt:
                        values(pair, nb - 1)

                first = (cfgs[0], 0, 0, 0)
                for k in range(cfgs[0].steps):
                    transposes(first, k)
                before_scores()
                scores(first, 0)
                scores(first, 1)
                each_pair(pe, cfgs, work)

            def out_part(k, o, dst):
                for t in range(TT):
                    last = pe.transpose(dst[:, tok[t]], o[:, t, k * P:(k + 1) * P], ident[:])
                last.then_inc(oT_done, 1)

            def out_proj(q, u0, base):
                def before(k):
                    pe.wait_ge(oT_ready, base + k + 1)
                out_chunks(q, u0, 1, oT_hi, oT_lo, KD, before)

            pe.sem_inc(unit_used, RING)
            for s in (gate_read, up_read, x_new):
                pe.sem_inc(s, 2)
            for s in (tr_done, p_done, pT_done, pT_ready, o_done, o_out):
                pe.sem_inc(s, 4)
            pe.wait_ge(consts_made, 6)

            ffn(0)
            down(0, 0)

            def copies_done(n):
                def wait():
                    pe.wait_ge(tok_act, n)
                    pe.wait_ge(tok_dve, n)
                return wait

            u0 = AB_AT
            for m in range(LATENT):
                feature_unit(bank[m][:], u0 + AB_LAT + m, (u0 + AB_LAT + m) % RING, xg_hi, xg_lo, 0, KD, True, True,
                             xg_wait(AB_NORM) if m == 0 else None)
                if m == 0:
                    token_stat(AB_NORM)
            token_group(u0 + AB_G0, bank[4:8], AB_W)
            pe.wait_ge(lat_hi_done, LATENT)
            pe.wait_ge(std_done, AB_NORM + 1)
            for t in range(TT):
                for m in range(2):
                    pe.matmul(tok_stat_b[:, TT + t:TT + t + 1], lat_sq[:, m, tok[t]], ones_lat[:, 0:1],
                              start=(m == 0), stop=(m == 1))
            for t in range(TT):
                last = pe.matmul(tok_stat_b[:, 2 * TT + t:2 * TT + t + 1], lat_sq[:, 2, tok[t]], ones_lat[:, 1:2],
                                 start=True, stop=True)
            last.then_inc(lat_stat, 1)
            pe.wait_ge(lat_ready, LATENT)
            pe.wait_ge(lat_step, 2)
            for o in range(16):
                half, t = o // 4 % 2, o % 4
                u = u0 + AB_UP + min(o // 4, 2)
                s = u % RING
                if o in (0, 4, 8):
                    pe.wait_ge(lo_ready, u + 1)
                if o == 4:
                    pe.wait_ge(tok_act, 2)
                    pe.wait_ge(tok_dve, 2)
                if o >= 8:
                    pe.wait_ge(tok_dve if o % 2 else tok_act, 2 + (o - 8) // 2 + 1)
                if o < 8:
                    for r in range(2):
                        w = slice(r * 384, (r + 1) * 384)
                        last = product(bank[o % 8][:, 0:384], lat_hi[:, r, tok[t]], lat_lo[:, r, tok[t]],
                                       w_hi[s][:, w], w_lo[s][:, w], r == 0, r == 1)
                else:
                    w = slice(half * 512, (half + 1) * 512)
                    last = product(bank[o % 8][:], lat_hi[:, 2, tok[t]], lat_lo[:, 2, tok[t]], w_hi[s][:, w],
                                   w_lo[s][:, w], True, True)
                last.then_inc(unit_used if o in (3, 7, 15) else tok_done, 1)
            for g in range(1, AB_GROUPS):
                pe.wait_ge(tok_act, 4 + 2 * g if g > 1 else 8)
                pe.wait_ge(tok_dve, 4 + 2 * g if g > 1 else 8)
                if g == 2:
                    pe.wait_ge(tok_act, 10)
                    pe.wait_ge(tok_dve, 10)
                if g == 3:
                    pe.wait_ge(tok_act, 12)
                    pe.wait_ge(tok_dve, 12)
                token_group(u0 + AB_G1 + 4 * (g - 1), bank[0:4] if g % 2 else bank[4:8], AB_W)
            pe.wait_ge(tok_act, AB_COPIES - 2)
            pe.wait_ge(tok_dve, AB_COPIES - 2)
            attention([Diff, Mla], copies_done(AB_COPIES), lambda pair, bl: None)
            pe.wait_ge(o_out, adone(TT * (DIFF_H + MLA_H) - 1))
            for k in range(KD):
                if k == KD // 2:
                    pe.wait_ge(sub_done, TT)
                if k >= 4:
                    pe.wait_ge(oT_ready, k - 3)
                out_part(k, ab_o, oT_b[k % 4])
            out_proj(1, AB_AT + AB_OUT, 0)

            ffn(1)
            down(1, 2)
            ffn(2)
            down(2, 3)

            for g in range(C_GROUPS):
                if g == 1:
                    pe.wait_ge(std_done, C_NORM + 1)
                if g == 2:
                    pe.wait_ge(tok_act, AB_COPIES + 2)
                    pe.wait_ge(tok_dve, AB_COPIES + 2)
                token_group(C_AT + 4 * g, c_b[g % 2], C_W,
                            before=xg_wait(C_NORM) if g == 0 else None)
                if g == 0:
                    token_stat(C_NORM)
            copies_done(AB_COPIES + 2 * C_GROUPS - 2)()
            def early_chunk(pair, bl):
                if isinstance(pair[3], int) and pair[3] == LAST_GQA and bl < KD - 1:
                    pe.wait_ge(o_out, adone(Gqa.B0 + 2 * TT * (bl + 1) - 1))
                    if bl > 0:
                        pe.wait_ge(oT_ready, KD + bl)
                    out_part(bl, c_o, tr_b)

            attention([Gqa], copies_done(AB_COPIES + 2 * C_GROUPS), early_chunk)
            pe.wait_ge(o_out, adone(Gqa.B0 + 2 * TT * KD - 1))
            out_part(KD - 1, c_o, oT_b[0])
            out_proj(4, C_AT + C_OUT, KD)

            ffn(3)
            down(3, 5)


def units_of(w):
    k, n = w.shape[0] // P, w.shape[1] // P
    u = w.reshape(k, P, n, P).transpose(2, 1, 0, 3)
    pad = -k % KD
    u = np.pad(u, ((0, 0), (0, 0), (0, pad), (0, 0)))
    u = u.reshape(n, P, (k + pad) // KD, UNIT).transpose(0, 2, 1, 3)
    return u.reshape(-1, P, UNIT)


def wide_units(w, width, rows):
    k, n = w.shape[0] // P, w.shape[1] // width
    u = w.reshape(k // rows, rows, P, n, width).transpose(3, 0, 2, 1, 4).reshape(-1, P, rows * width)
    return np.pad(u, ((0, 0), (0, 0), (0, UNIT - rows * width)))


def rotary(pos, dim):
    inv = np.float32(THETA) ** (-np.arange(0, dim, 2, dtype=np.float32) / np.float32(dim))
    ang = pos.astype(np.float32)[:, None] * inv[None, :]
    return np.cos(ang).astype(np.float32), np.sin(ang).astype(np.float32)


def token_major(a):
    return a.reshape(TT, P, -1).transpose(1, 0, 2).reshape(P, -1)


def rotary_tables():
    cos, sin = rotary(np.arange(SEQ), ROPE)
    c32, s32 = np.concatenate([cos, cos], 1), np.concatenate([-sin, sin], 1)
    mla_c = np.concatenate([np.ones((SEQ, NOPE), np.float32), c32], 1)
    two_c, two_s = np.tile(c32, (1, 2)), np.tile(s32, (1, 2))
    parts = [mla_c, s32, mla_c, s32, two_c, two_s, two_c, two_s]
    even = np.concatenate([token_major(p) for p in parts], 1)
    row, col = np.arange(SEQ) // GRID_W, np.arange(SEQ) % GRID_W
    (rc, rs), (cc, cs) = rotary(row, GQA_D // 2), rotary(col, GQA_D // 2)
    ax_c, ax_s = np.concatenate([rc, rc, cc, cc], 1), np.concatenate([-rs, rs, -cs, cs], 1)
    odd = [token_major(p) for p in (np.tile(ax_c, (1, 2)), np.tile(ax_s, (1, 2)), ax_c, ax_s)]
    odd = np.concatenate(odd, 1)
    return even, odd


def swapped(g):
    return g.reshape(-1, 2, 16)[:, ::-1].reshape(-1)


def spread(g):
    return token_major(np.broadcast_to(g, (SEQ, g.size)))


def kernel(**inputs):
    import concourse.bacc as _bacc
    from concourse.bass_utils import run_bass_kernel_spmd as _run

    a = {k: np.asarray(v) for k, v in inputs.items()}
    f = np.ascontiguousarray

    def ffn_units(which, i):
        gate, up = (units_of(a[f"{which}_w_{n}"][i]) for n in ("gate", "up"))
        both = np.stack([gate, up], 1).reshape(-1, P, UNIT)
        return [both, units_of(a[f"{which}_w_down"][i])]

    ab, latent = a["ab_w_in"][0], Q_RANK + KV_RANK
    groups = wide_units(ab[:, latent:], AB_W, 2)
    stream = ffn_units("ffn1", 0)
    stream += [units_of(ab[:, :latent]), groups[:4], wide_units(a["mla_w_uq"][0], 384, 2),
               wide_units(a["mla_w_ukv"][0], 1024, 1), groups[4:], units_of(a["ab_w_out"][0])]
    stream += ffn_units("ffn2", 0) + ffn_units("ffn1", 1)
    c_groups = wide_units(a["c_w_in"][0], C_W, 2).reshape(C_GROUPS, 4, P, UNIT)
    stream += [c_groups[g] for g in C_ORDER] + [units_of(a["c_w_out"][0])]
    stream += ffn_units("ffn2", 1)
    weights = np.concatenate(stream, 0)
    assert weights.shape[0] == N_UNITS

    def by_chunk(g):
        return g.reshape(-1, P).T

    norms = [a[n][i] for i in range(2) for n in ("ffn1_norm", "mix_norm", "ffn2_norm")]
    even, odd = rotary_tables()
    mq, mk, dq, dk = (a[n][0] for n in ("mla_q_norm", "mla_k_norm", "diff_q_norm", "diff_k_norm"))
    cq, ck = a["c_q_norm"][0], a["c_k_norm"][0]
    gains_even = [x for g in (mq, mk) for x in (spread(g), spread(swapped(g[NOPE:])))]
    gains_even += [x for g in (dq, dk) for x in (spread(np.tile(g, 2)), spread(np.tile(swapped(g), 2)))]
    gains_odd = [spread(np.tile(cq, 2)), spread(np.tile(swapped(cq), 2)), spread(ck), spread(swapped(ck))]
    lams = np.stack([a[f"diff_lambda_{n}"][0] for n in ("q1", "k1", "q2", "k2")])
    arrays = {
        "in_x": f(a["x"][0].T.reshape(KD, P, SEQ).transpose(1, 0, 2)),
        "in_weights": weights,
        "in_gains": f(np.stack([by_chunk(g) for g in norms], 1)),
        "in_lat_gain": f(np.concatenate([by_chunk(a["mla_q_lora_norm"][0]), by_chunk(a["mla_kv_lora_norm"][0])], 1)),
        "in_rot": f(even),
        "in_head_gains": f(np.concatenate(gains_even, 1)),
        "in_rot_c": f(odd),
        "in_head_gains_c": f(np.concatenate(gains_odd, 1)),
        "in_lambdas": f(np.broadcast_to(lams, (P, 4, DIFF_D))),
        "in_subln": f(np.tile(a["diff_subln"][0], 2)[:, None]),
    }
    nc = _bacc.Bacc("TRN2", target_bir_lowering=False, num_devices=1)
    args = [nc.dram_tensor(n, v.shape, F32, kind="ExternalInput").ap() for n, v in arrays.items()]
    args.append(nc.dram_tensor("out_x", (P, KD, SEQ), F32, kind="ExternalOutput").ap())
    build_kernel(nc, *args)
    r = _run(nc, [arrays], core_ids=[0])
    y = r.results[0]["out_x"]
    return np.ascontiguousarray(y.transpose(1, 0, 2).reshape(D_MODEL, SEQ).T)[None]
```
